# Optimizing a Trainium2 kernel written in Bass

```python
import jax, jax.numpy as jnp
from jax import lax
import numpy as np

D_MODEL = 1024
BATCH = 1
SEQ = 512
DEPTH = 1
DEC_BATCH = 1
DEC_SEQ = 256
PAST_LEN = 128

A_GROUPS = 8
A_WIDTH = 512
A_CHUNK = 128
A_GROUP_DIM = A_WIDTH // A_GROUPS
HG_HEADS = 8
HG_DK = 128
HG_DV = 128
HG_WIDTH = HG_HEADS * HG_DK
HG_CHUNK = 32
N_IN = 2 * A_WIDTH + 5 * HG_WIDTH + 2 * D_MODEL
N_EXPERTS = 64
TOP_K = 6
N_GROUPS = 8
TOPK_GROUPS = 4
EXPERT_DIM = 256
SHARED_DIM = 256
ROUTED_SCALE = 2.5
MOE_BLOCK = 128
ALPHA = (2.0 * DEPTH) ** 0.25
BETA = (8.0 * DEPTH) ** -0.25
LN_EPS = 1e-5
RMS_EPS = 1e-6

kernel_name = "hybrid_gmlp_hgrn2_moe_encoder"

def layer_norm(x, g, b):
    xf = x.astype(jnp.float32)
    mu = xf.mean(-1, keepdims=True)
    var = jnp.square(xf - mu).mean(-1, keepdims=True)
    return ((xf - mu) * lax.rsqrt(var + LN_EPS) * g + b).astype(x.dtype)

def split_in(h):
    sizes = (A_WIDTH, A_WIDTH, HG_WIDTH, HG_WIDTH, HG_WIDTH, HG_WIDTH, HG_WIDTH, D_MODEL, D_MODEL)
    cuts = [int(c) for c in np.cumsum(sizes)[:-1]]
    return jnp.split(h, cuts, axis=-1)

def gmlp_branch(u, v, ln_g, ln_b, ws, sb):
    u = jax.nn.gelu(u)
    v = layer_norm(jax.nn.gelu(v), ln_g, ln_b)
    B, S, _ = v.shape
    vc = v.reshape(B, S // A_CHUNK, A_CHUNK, A_GROUPS, A_GROUP_DIM)
    mixed = jnp.einsum('gts,bnsgc->bntgc', ws, vc) + sb[:, :, None]
    return u * mixed.reshape(B, S, A_WIDTH)

def hgrn2_scan(q, k, logf, v):
    B, S, H, DK = q.shape
    DV = v.shape[-1]
    n = S // HG_CHUNK

    def chunks(t):
        return t.reshape(B, n, HG_CHUNK, H, t.shape[-1]).transpose(1, 0, 3, 2, 4)

    tri = jnp.tril(jnp.ones((HG_CHUNK, HG_CHUNK), dtype=bool))

    def step(state, inp):
        qc, kc, gc, vc = inp
        b = jnp.cumsum(gc, axis=2)
        diff = b[:, :, :, None, :] - b[:, :, None, :, :]
        dec = jnp.where(tri[:, :, None], jnp.exp(jnp.minimum(diff, 0.0)), 0.0)
        scores = jnp.einsum('bhtk,bhsk,bhtsk->bhts', qc, kc, dec)
        o = (jnp.einsum('bhts,bhsv->bhtv', scores, vc)
             + jnp.einsum('bhtk,bhkv->bhtv', qc * jnp.exp(b), state))
        b_last = b[:, :, -1:, :]
        state = (jnp.exp(b_last[:, :, 0, :, None]) * state
                 + jnp.einsum('bhsk,bhsv->bhkv', kc * jnp.exp(b_last - b), vc))
        return state, o

    init = jnp.zeros((B, H, DK, DV), jnp.float32)
    _, o = lax.scan(step, init, (chunks(q), chunks(k), chunks(logf), chunks(v)))
    return o.transpose(1, 0, 3, 2, 4).reshape(B, S, H, DV)

def hgrn2_branch(q, f_fwd, f_bwd, i_in, g_out, lb, norm_g):
    B, S, _ = q.shape
    f32 = jnp.float32

    def heads(t):
        return t.astype(f32).reshape(B, S, HG_HEADS, HG_DK)

    qh = heads(jax.nn.silu(q))
    vh = heads(i_in)

    def gates(fpre, lb_dir):
        f = lb_dir + (1.0 - lb_dir) * jax.nn.sigmoid(fpre.astype(f32))
        return heads(1.0 - f), heads(jnp.log(f))

    kf, gf = gates(f_fwd, lb[0])
    kb, gb = gates(f_bwd, lb[1])
    o_f = hgrn2_scan(qh, kf, gf, vh)
    o_b = jnp.flip(hgrn2_scan(jnp.flip(qh, 1), jnp.flip(kb, 1), jnp.flip(gb, 1), jnp.flip(vh, 1)), 1)
    o = o_f + o_b
    o = o * lax.rsqrt(jnp.mean(jnp.square(o), -1, keepdims=True) + RMS_EPS)
    o = o.reshape(B, S, HG_WIDTH) * norm_g * jax.nn.silu(g_out.astype(f32))
    return o.astype(q.dtype)

def moe_ffn(x, w_router, router_bias, w_e_gate, w_e_up, w_e_down, w_sh_gate, w_sh_up, w_sh_down):
    B, S, D = x.shape
    f32 = jnp.float32
    xt = x.reshape(-1, D)
    T = xt.shape[0]
    scores = jax.nn.sigmoid((xt @ w_router).astype(f32))
    biased = scores + router_bias.astype(f32)
    grp_score = lax.top_k(biased.reshape(T, N_GROUPS, N_EXPERTS // N_GROUPS), 2)[0].sum(-1)
    _, grp_idx = lax.top_k(grp_score, TOPK_GROUPS)
    grp_mask = jnp.any(grp_idx[..., None] == jnp.arange(N_GROUPS), axis=1)
    allowed = jnp.where(jnp.repeat(grp_mask, N_EXPERTS // N_GROUPS, axis=1), biased, -jnp.inf)
    _, idx = lax.top_k(allowed, TOP_K)
    w = jnp.take_along_axis(scores, idx, axis=1)
    w = w / w.sum(-1, keepdims=True) * ROUTED_SCALE
    TK = T * TOP_K
    flat_e = idx.reshape(-1).astype(jnp.int32)
    order = jnp.argsort(flat_e)
    sorted_e = flat_e[order]
    tok = (order // TOP_K).astype(jnp.int32)
    gate = w.reshape(-1)[order]
    counts = jnp.bincount(flat_e, length=N_EXPERTS).astype(jnp.int32)
    padded = (counts + MOE_BLOCK - 1) // MOE_BLOCK * MOE_BLOCK
    pad_end = jnp.cumsum(padded)
    pad_start = pad_end - padded
    start = jnp.cumsum(counts) - counts
    dest = pad_start[sorted_e] + jnp.arange(TK, dtype=jnp.int32) - start[sorted_e]
    n_blocks = -(-TK // MOE_BLOCK) + N_EXPERTS
    P = n_blocks * MOE_BLOCK
    buf_tok = jnp.full((P,), T, jnp.int32).at[dest].set(tok)
    buf_gate = jnp.zeros((P,), f32).at[dest].set(gate)
    blk_exp = jnp.minimum(jnp.searchsorted(pad_end, jnp.arange(n_blocks, dtype=jnp.int32) * MOE_BLOCK, side='right'), N_EXPERTS - 1)
    x_pad = jnp.concatenate([xt, jnp.zeros((1, D), xt.dtype)], axis=0)

    def run_block(args):
        t_idx, g, e = args
        xb = x_pad[t_idx]
        hb = jax.nn.silu(xb @ w_e_gate[e]) * (xb @ w_e_up[e])
        return (hb @ w_e_down[e]).astype(f32) * g[:, None]

    yb = lax.map(run_block, (buf_tok.reshape(n_blocks, MOE_BLOCK), buf_gate.reshape(n_blocks, MOE_BLOCK), blk_exp))
    routed = jnp.zeros((T + 1, D), f32).at[buf_tok].add(yb.reshape(P, D))[:T]
    shared = (jax.nn.silu(xt @ w_sh_gate) * (xt @ w_sh_up)) @ w_sh_down
    return (routed + shared.astype(f32)).astype(x.dtype).reshape(B, S, D)

def encoder_layer(x, lb, w_in, a_ln_g, a_ln_b, a_ws, a_sb, hg_norm_g, w_pa, w_pb, w_o,
                  ln1_g, ln1_b, w_router, router_bias, w_e_gate, w_e_up, w_e_down,
                  w_sh_gate, w_sh_up, w_sh_down, ln2_g, ln2_b):
    h = x @ w_in
    u_a, v_a, q, f_fwd, f_bwd, i_in, g_out, gate_a, gate_b = split_in(h)
    a = gmlp_branch(u_a, v_a, a_ln_g, a_ln_b, a_ws, a_sb) @ w_pa
    r = hgrn2_branch(q, f_fwd, f_bwd, i_in, g_out, lb, hg_norm_g) @ w_pb
    mixed = jax.nn.sigmoid(gate_a) * a + jax.nn.sigmoid(gate_b) * r
    x = layer_norm(ALPHA * x + mixed @ w_o, ln1_g, ln1_b)
    y = moe_ffn(x, w_router, router_bias, w_e_gate, w_e_up, w_e_down, w_sh_gate, w_sh_up, w_sh_down)
    return layer_norm(ALPHA * x + y, ln2_g, ln2_b)

def encode(x, p):
    (ln_in_g, ln_in_b, w_in, a_ln_g, a_ln_b, a_ws, a_sb, hg_lb_logits, hg_norm_g, w_pa, w_pb, w_o,
     ln1_g, ln1_b, w_router, router_bias, w_e_gate, w_e_up, w_e_down, w_sh_gate, w_sh_up, w_sh_down,
     ln2_g, ln2_b) = p
    x = layer_norm(x, ln_in_g, ln_in_b)
    lb_all = jnp.cumsum(jax.nn.softmax(hg_lb_logits.astype(jnp.float32), axis=1), axis=1)
    for l in range(DEPTH):
        x = encoder_layer(x, lb_all[:, l], w_in[l], a_ln_g[l], a_ln_b[l], a_ws[l], a_sb[l], hg_norm_g[l],
                          w_pa[l], w_pb[l], w_o[l], ln1_g[l], ln1_b[l], w_router[l], router_bias[l],
                          w_e_gate[l], w_e_up[l], w_e_down[l], w_sh_gate[l], w_sh_up[l], w_sh_down[l],
                          ln2_g[l], ln2_b[l])
    return x

def setup_inputs(seed: int = 0) -> dict:
    key = jax.random.key(seed)
    ks = iter(jax.random.split(key, 40))
    nrm = lambda shape, s: jax.random.normal(next(ks), shape, jnp.float32) * s
    gain = lambda shape: 1.0 + nrm(shape, 0.02)
    L, D, E = DEPTH, D_MODEL, N_EXPERTS
    return {
        "x_prompt": nrm((BATCH, SEQ, D), 1.0),
        "x_sample": nrm((DEC_BATCH, DEC_SEQ, D), 1.0),
        "ln_in_g": gain((D,)),
        "ln_in_b": nrm((D,), 0.02),
        "w_in": nrm((L, D, N_IN), D ** -0.5),
        "a_ln_g": gain((L, A_WIDTH)),
        "a_ln_b": nrm((L, A_WIDTH), 0.02),
        "a_ws": nrm((L, A_GROUPS, A_CHUNK, A_CHUNK), A_CHUNK ** -0.5),
        "a_sb": gain((L, A_CHUNK, A_GROUPS)),
        "hg_lb_logits": nrm((2, L + 1, HG_WIDTH), 0.5),
        "hg_norm_g": gain((L, HG_WIDTH)),
        "w_pa": nrm((L, A_WIDTH, D), A_WIDTH ** -0.5 * BETA),
        "w_pb": nrm((L, HG_WIDTH, D), HG_WIDTH ** -0.5 * BETA),
        "w_o": nrm((L, D, D), D ** -0.5 * BETA),
        "ln1_g": gain((L, D)),
        "ln1_b": nrm((L, D), 0.02),
        "w_router": nrm((L, D, E), D ** -0.5),
        "router_bias": nrm((L, E), 0.01),
        "w_e_gate": nrm((L, E, D, EXPERT_DIM), D ** -0.5),
        "w_e_up": nrm((L, E, D, EXPERT_DIM), D ** -0.5),
        "w_e_down": nrm((L, E, EXPERT_DIM, D), EXPERT_DIM ** -0.5 * BETA),
        "w_sh_gate": nrm((L, D, SHARED_DIM), D ** -0.5),
        "w_sh_up": nrm((L, D, SHARED_DIM), D ** -0.5),
        "w_sh_down": nrm((L, SHARED_DIM, D), SHARED_DIM ** -0.5 * BETA),
        "ln2_g": gain((L, D)),
        "ln2_b": nrm((L, D), 0.02),
    }

def reference(x_prompt, x_sample, ln_in_g, ln_in_b, w_in, a_ln_g, a_ln_b, a_ws, a_sb, hg_lb_logits,
              hg_norm_g, w_pa, w_pb, w_o, ln1_g, ln1_b, w_router, router_bias, w_e_gate, w_e_up,
              w_e_down, w_sh_gate, w_sh_up, w_sh_down, ln2_g, ln2_b):
    params = (ln_in_g, ln_in_b, w_in, a_ln_g, a_ln_b, a_ws, a_sb, hg_lb_logits, hg_norm_g, w_pa, w_pb, w_o,
              ln1_g, ln1_b, w_router, router_bias, w_e_gate, w_e_up, w_e_down, w_sh_gate, w_sh_up,
              w_sh_down, ln2_g, ln2_b)
    y_prompt = encode(x_prompt, params)
    y_sample = encode(x_sample, params)
    return (y_prompt, y_sample)


_drawn_inputs = setup_inputs


def setup_inputs(seed=0):
    import zlib

    import numpy as np

    out = dict(_drawn_inputs(seed))
    spreads = {}
    factors = {'a_ln_g': 3.808,
     'a_ln_b': 4.451,
     'a_sb': 3.509,
     'hg_lb_logits': 2.811,
     'hg_norm_g': 4.383,
     'ln2_g': 2.851,
     'ln2_b': 2.806}
    for name, (base, spread) in spreads.items():
        noise = np.random.default_rng([zlib.crc32(name.encode()), seed]).standard_normal(out[name].shape)
        drawn = base * np.exp(spread * noise) if base else spread * noise
        out[name] = __import__('jax').numpy.asarray(drawn.astype(out[name].dtype))
    for name, factor in factors.items():
        out[name] = (out[name] * factor).astype(out[name].dtype)
    return out
```

```python
from contextlib import ExitStack

import numpy as np

import concourse.bass as bass
import concourse.mybir as mybir

F32 = mybir.dt.float32
I32 = mybir.dt.int32
U32 = mybir.dt.uint32
ALU = mybir.AluOpType
ACT = mybir.ActivationFunctionType
AX = mybir.AxisListType

P = 128
D = 1024
SEQ, DEC_SEQ = 512, 256
T = SEQ + DEC_SEQ
NT = T // P
NTP = SEQ // P
KC = D // P
HALF = T // 2
AW = 512
AG = 8
AGD = AW // AG
H = 8
DK = 128
LEVELS = 7
E = 64
EG = 8
TOPK = 6
TOPG = 4
F = 256
KSTRIDE = 8
MIN_BLOCKS = T * TOPK // P
NBMAX = MIN_BLOCKS + E
NCOL = NBMAX + 2
SCALE = 2.5
ALPHA = 2.0 ** 0.25
LN_EPS = 1e-5
RMS_EPS = 1e-6
BIG = 1e30
NOWHERE = 1 << 20
C_U, C_V, C_Q, C_FF, C_FB, C_I, C_G, C_GA, C_GB = 0, 512, 1024, 2048, 3072, 4096, 5120, 6144, 7168

K_IDENT = 0
K_ONES = K_IDENT + P
K_TRI = K_ONES + P
K_IOTA = K_TRI + P
K_MASK = K_IOTA + P
K_IOTAP = K_MASK + LEVELS * P
K_DST = K_IOTAP + 1
NCONST = K_DST + NT * TOPK

FILLS = 11
FWD_TILES = (0, 1, 2, 4)
BWD_TILES = (3, 2, 1, 5)


def constants():
    c = np.zeros((P, NCONST), np.float32)
    p = np.arange(P)
    c[:, K_IDENT:K_IDENT + P] = np.eye(P)
    c[:, K_ONES:K_ONES + P] = 1.0
    c[:, K_TRI:K_TRI + P] = p[:, None] < p[None, :]
    c[:, K_IOTA:K_IOTA + P] = p[None, :]
    for j in range(LEVELS):
        same = (p[:, None] >> (j + 1)) == (p[None, :] >> (j + 1))
        c[:, K_MASK + j * P:K_MASK + (j + 1) * P] = same & ((p[:, None] >> j) != (p[None, :] >> j))
    c[:, K_IOTAP] = p
    for i in range(NT):
        for k in range(TOPK):
            c[:, K_DST + i * TOPK + k] = (i * P + p) * KSTRIDE + k + 1
    return c


class Chain:

    def __init__(self, eng, sem):
        self.eng, self.sem, self.n = eng, sem, 0

    def link(self, ins):
        self.n += 1
        ins.then_inc(self.sem, 1)
        self.eng.wait_ge(self.sem, self.n)

    def restart(self):
        self.eng.wait_ge(self.sem, self.n)
        self.eng.sem_clear(self.sem)
        self.n = 0


def build(nc, d):
    with ExitStack() as ctx:
        def sb(name, words, dt=F32):
            return ctx.enter_context(nc.sbuf_tensor(name, [P, words], dt))

        def ps(name, words):
            return ctx.enter_context(nc.psum_tensor(name, [P, words], F32))

        def sem(name):
            return ctx.enter_context(nc.semaphore(name))

        con = sb("con", NCONST)
        rA = sb("rA", KC * T)
        rB = sb("rB", KC * T)
        rCD = sb("rCD", 2 * KC * T)
        rEF = sb("rEF", 2 * KC * T)
        aTr = sb("aTr", 4 * T)
        hw = sb("hw", 3 * KC * P)
        ew = sb("ew", 6 * D)
        rows = sb("rows", 2 * D)
        lbs = sb("lbs", 2 * H)
        lbc = sb("lbc", 2 * H)
        sbt = sb("sbt", AG)
        lbraw = sb("lbraw", P)
        blki = lbraw[:, :].bitcast(I32)
        lbw = sb("lbw", 4 * 4 * H)
        bias = sb("bias", E)
        bst = sb("bst", 12 * NT)
        mv = sb("mv", 2 * NT)
        std = sb("std", NT * H)
        rstd = sb("rstd", NT * H)
        bexp = sb("bexp", 1)
        nbi = sb("nbi", 8, I32)

        ident = con[:, K_IDENT:K_IDENT + P]
        ones = con[:, K_ONES:K_ONES + P]
        tri = con[:, K_TRI:K_TRI + P]
        iota = con[:, K_IOTA:K_IOTA + P]

        def slabs(ap, c):
            return ap.rearrange("p (c n) -> p c n", c=c)

        def at(region, offset, dims):
            ap = region[:, :]
            return bass.AP(ap.tensor, ap.offset + offset, [list(ap.ap[0])] + [list(x) for x in dims])

        x1T = slabs(rA[:, :], KC)
        mT = x1T
        v_tok = slabs(rB[:, :], NT)
        rT = slabs(rB[:, :], KC)
        x2 = slabs(rB[:, :], NT)
        x_in = slabs(rCD[:, 0:NT * D], NT)
        g_tok = slabs(rCD[:, 0:NT * D], NT)
        o_tok = slabs(rCD[:, NT * D:], NT)
        u_tok = slabs(rCD[:, NT * D:NT * D + NT * AW], NT)
        vn_tok = slabs(rCD[:, NT * D + NT * AW:], NT)
        wo_sb = slabs(rCD[:, 0:KC * D], KC)
        wsh = slabs(rCD[:, KC * D:KC * D + KC * 2 * F], KC)
        strip = [slabs(rEF[:, n * KC * 512:(n + 1) * KC * 512], KC) for n in range(2)]
        ws_sb = slabs(rEF[:, 2 * KC * 512:2 * KC * 512 + AG * P], AG)
        wsT = slabs(rEF[:, 2 * KC * 512 + AG * P:2 * KC * 512 + 2 * AG * P], AG)
        sga = slabs(rEF[:, 0:KC * T], KC)
        sgb = slabs(rEF[:, KC * T:], KC)
        x1_back = slabs(rEF[:, 0:NT * D], NT)
        acc = x1_back
        x2T = slabs(rEF[:, KC * T:], KC)
        aT = slabs(aTr[:, :], 4)
        wsh_d = slabs(aTr[:, 0:2 * D], 2)
        hw3 = [slabs(hw[:, m * KC * P:(m + 1) * KC * P], KC) for m in range(3)]
        nrow = ew[:, 3 * D:4 * D]

        q_next, sig_next = rEF[:, 0:T], rEF[:, T:3 * T]
        OFF = {"q": 3 * T, "P": 4 * T, "k": 6 * T, "S": 8 * T, "Q0": 10 * T, "Q1": 11 * T,
               "K0": 12 * T, "K1": 13 * T, "prod": 14 * T, "AT": 15 * T}
        keT = slabs(ew[:, 0:8 * P], 8)
        states = slabs(ew[:, 8 * P:16 * P], 8)

        def hv(name, n=1):
            return rEF[:, OFF[name]:OFF[name] + n * T]

        cut = [0]

        def scratch(n):
            cut[0] += n
            assert cut[0] <= KC * D
            return rCD[:, cut[0] - n:cut[0]]

        NK = NT * TOPK
        onehot, work = scratch(NK * E), scratch(NK * E)
        score, biased, allowed, select, posd = (scratch(NT * E) for _ in range(5))
        best, second, gsum, gcnt, gmask = (scratch(NT * EG) for _ in range(5))
        gtop, gidx, gidxf, etop, eidx, eidxf = (scratch(NT * 8) for _ in range(6))
        gate, gatew, slot, slotl, sloth, low, high = (scratch(NK) for _ in range(7))
        wsum, nblk, incl, base = scratch(NT), scratch(E), scratch(E), scratch(E)

        def oh_place(x):
            return ew[:, (x % 4) * (P + 2 * NCOL):][:, 0:P]

        def oh_block(x):
            return ew[:, (x % 4) * (P + 2 * NCOL) + P:][:, 0:2 * NCOL]

        weights = (rB[:, :], rEF[:, KC * T:])
        wg, wu, wd = [[slabs(w[:, n * 2 * D:(n + 1) * 2 * D], c) for w in weights]
                      for n, c in ((0, KC), (1, KC), (2, 2))]
        work2 = (rA[:, 0:3 * D + 4 * F], ew[:, 0:3 * D + 4 * F])
        xg = [w[:, 0:D] for w in work2]
        xT = [slabs(w[:, D:2 * D], KC) for w in work2]
        yrow = [w[:, 2 * D:3 * D] for w in work2]
        silu_g = [w[:, 3 * D:3 * D + F] for w in work2]
        hT = [slabs(w[:, 3 * D + F:3 * D + 2 * F], 2) for w in work2]
        hid = rA[:, 3 * D + 2 * F:3 * D + 3 * F]
        hidT = slabs(rA[:, 3 * D + 3 * F:3 * D + 4 * F], 2)
        tblg = rA[:, 4 * D:4 * D + P]
        tbld = rA[:, 4 * D + P:4 * D + 2 * P]
        tbldi = rA[:, 4 * D + 2 * P:4 * D + 3 * P].bitcast(I32)
        tblti = rA[:, 4 * D + 3 * P:4 * D + 4 * P].bitcast(I32)
        tokcol, dstcol = ([rA[:, 4 * D + 4 * P + 2 * m + n:][:, 0:1].bitcast(I32) for n in range(2)]
                          for m in range(2))
        gcol = [rA[:, 4 * D + 4 * P + 4 + n:][:, 0:1] for n in range(2)]
        lgT = rA[:, 4 * D + 5 * P:4 * D + 5 * P + T]
        wr_sb = slabs(rA[:, 5 * D + 4 * P:5 * D + 4 * P + KC * E], KC)

        pg = ps("pg", 1024)
        pA = ps("pA", 1024)
        pB = ps("pB", 1024)
        pX = ps("pX", 1024)
        pair = [pA, pB]
        pairY = [pB, pX]

        s_con = sem("constants_loaded")
        s_x = [sem(f"x_loaded{i}") for i in range(NT)]
        s_rows = sem("ln_rows_loaded")
        s_aln = sem("gmlp_ln_rows_loaded")
        s_ln1 = sem("ln1_rows_loaded")
        s_ln2 = sem("ln2_rows_loaded")
        s_misc = sem("small_params_loaded")
        dve = sem("dve_chain")
        pool = sem("pool_chain")
        var_ready = sem("variance_ready")
        std_ready = sem("std_ready")
        x1_ready = sem("x1_ready")
        x1_stored = sem("x1_stored")
        t_filled = sem("transposes_in_psum")
        t_evicted = sem("transposes_in_sbuf")
        s_strip = [sem(f"strip_loaded{n}") for n in range(2)]
        s_hw = [sem(f"column_weights_loaded{m}") for m in range(3)]
        g_filled = sem("product_in_psum")
        g_evicted = sem("product_in_sbuf")
        v_normed = sem("gmlp_v_normed")
        ws_filled = sem("ws_transposed")
        ws_evicted = sem("ws_in_sbuf")
        mix_filled = sem("mix_in_psum")
        a_ready = sem("gmlp_a_ready")
        lb_filled = sem("lb_logits_transposed")
        lb_sub = sem("lb_logits_centred")
        lb_exp = sem("lb_exp_ready")
        cur_taken = sem("gates_taken")
        diag_ready = sem("diag_ready")
        lvl_ready = sem("level_ready")
        ke_ready = sem("k_decayed_ready")
        st_ready = sem("states_ready")
        hg_filled = sem("recurrence_in_psum")
        hg_used = sem("recurrence_psum_used")
        r_done = sem("r_ready")
        rt_evicted = sem("rT_in_sbuf")
        rt_filled = sem("rT_in_psum")
        s_pa = sem("w_pa_loaded")
        s_pb = sem("w_pb_loaded")
        pa_filled = sem("a_projected")
        pb_filled = sem("r_projected")
        pa_taken = sem("a_projection_taken")
        pb_taken = sem("r_projection_taken")
        m_ready = sem("mixed_ready")
        s_wo = sem("w_o_loaded")
        s_x1b = sem("x1_reloaded")
        of_filled = sem("out_projection_in_psum")
        z_taken = sem("out_projection_taken")
        x2_ready = sem("x2_ready")
        x2_stored = sem("x2_stored")
        x2t_filled = sem("x2T_in_psum")
        x2t_evicted = sem("x2T_in_sbuf")
        s_wr = sem("router_loaded")
        s_wsh = sem("shared_expert_loaded")
        lg_filled = sem("logits_in_psum")
        lg_evicted = sem("logits_in_sbuf")
        lgt_filled = sem("logits_token_major")
        sc_ready = sem("scores_ready")
        sel_ready = sem("selection_ready")
        pos_filled = sem("positions_in_psum")
        oh_ready = sem("slot_onehots_ready")
        oh_used = sem("slot_onehots_used")
        tb_filled = sem("tables_in_psum")
        blk_ready = sem("block_expert_ready")
        blk_filled = sem("block_expert_row")
        tb_ready = sem("tables_ready")
        sh_gu = sem("shared_gate_up_in_psum")
        sh_silu = sem("shared_silu_ready")
        sh_h = sem("shared_hidden_ready")
        sh_ht = sem("shared_hiddenT_in_psum")
        sh_hte = sem("shared_hiddenT_ready")
        sh_y = sem("shared_down_in_psum")
        sh_acc = sem("shared_added")
        s_wgu = [sem(f"w_gate_up_loaded{n}") for n in range(2)]
        s_wd = [sem(f"w_down_loaded{n}") for n in range(2)]
        gu_filled = sem("gate_up_in_psum")
        silu_ready = sem("silu_ready")
        h_ready = sem("hidden_ready")
        y_filled = sem("down_in_psum")
        y_ready = sem("y_ready")
        gc_ready = sem("gate_column_ready")
        xg_clear = sem("gather_buffer_cleared")
        xg_loaded = [sem(f"rows_gathered{n}") for n in range(2)]
        xt_filled = sem("gathered_T_in_psum")
        xt_ready = sem("gathered_T_ready")
        y_stored = [sem(f"y_scattered{n}") for n in range(2)]
        s_yb = [sem(f"routed_rows_loaded{n}") for n in range(2)]
        yb_used = sem("routed_rows_used")
        out_ready = sem("out_ready")
        out_stored = sem("out_stored")

        block = ctx.enter_context(nc.Block())

        @block.sync
        def _(sp):
            w_in = d["w_in"].rearrange("(p c) n -> p c n", c=KC)

            sp.dma_start(x_in[:, 0, :], d["x_prompt"][0:P, :]).then_inc(s_x[0], 16)
            sp.dma_start(con[:, :], d["consts"]).then_inc(s_con, 16)
            for i in range(1, NT):
                src = d["x_prompt"][i * P:(i + 1) * P, :] if i < NTP else \
                    d["x_sample"][(i - NTP) * P:(i - NTP + 1) * P, :]
                sp.dma_start(x_in[:, i, :], src).then_inc(s_x[i], 16)
            sp.dma_start(rows[:, 0:D], d["ln_in_g"].to_broadcast([P, D])).then_inc(s_rows, 16)
            sp.dma_start(rows[:, D:], d["ln_in_b"].to_broadcast([P, D])).then_inc(s_rows, 16)
            for n, c0 in enumerate((C_U, C_V, C_I, C_I + 512, C_G, C_G + 512)):
                if n >= 2:
                    sp.wait_ge(g_filled, NT * (n - 1))
                sp.dma_start(strip[n % 2], w_in[:, :, c0:c0 + 512]).then_inc(s_strip[n % 2], 16)
                if n == 0:
                    sp.dma_start(ws_sb, d["a_ws"].rearrange("g t s -> t g s")).then_inc(s_misc, 16)
                    sp.dma_start(sbt[:, :], d["a_sb"]).then_inc(s_misc, 16)
                    sp.dma_start(nrow, d["hg_norm_g"].to_broadcast([P, D])).then_inc(s_misc, 16)
                    sp.dma_start(lbraw[0:4 * H, :], d["hg_lb_logits"].rearrange(
                        "a l (h k) -> (a l h) k", h=H)).then_inc(s_misc, 16)
            sp.wait_ge(x1_ready, NT)
            for i in range(NT):
                sp.dma_start(d["x1_dram"][i * P:(i + 1) * P, :], x_in[:, i, :]).then_inc(x1_stored, 16)
            sp.dma_start(rows[:, 0:AW], d["a_ln_g"].to_broadcast([P, AW])).then_inc(s_aln, 16)
            sp.dma_start(rows[:, AW:2 * AW], d["a_ln_b"].to_broadcast([P, AW])).then_inc(s_aln, 16)
            for m, c0 in enumerate((C_Q, C_FF, C_FB)):
                sp.dma_start(hw3[m], w_in[:, :, c0:c0 + DK]).then_inc(s_hw[m], 16)
            with sp.Fori(1, H) as h:
                for m, c0 in enumerate((C_Q, C_FF, C_FB)):
                    sp.wait_ge(g_filled, 36 + 2 * (m + 1) + (h - 1) * 6)
                    sp.dma_start(hw3[m], w_in[:, :, bass.ds(c0 + h * DK, DK)]).then_inc(s_hw[m], 16)
            base = 36 + 6 * H
            for m, c0 in enumerate((C_GA, C_GB)):
                sp.wait_ge(g_filled, base - 4 + 2 * m)
                sp.dma_start(hw3[m], w_in[:, :, c0:c0 + P]).then_inc(s_hw[m], 16)
            with sp.Fori(1, KC) as f:
                for m, c0 in enumerate((C_GA, C_GB)):
                    sp.wait_ge(g_filled, base + 2 * (m + 1) + (f - 1) * 4)
                    sp.dma_start(hw3[m], w_in[:, :, bass.ds(c0 + f * P, P)]).then_inc(s_hw[m], 16)
            w_pa = d["w_pa"].rearrange("(p c) n -> p c n", c=4)
            w_pb = d["w_pb"].rearrange("(p c) n -> p c n", c=KC)
            sp.wait_ge(g_filled, base + 4 * KC)
            sp.dma_start(hw3[0][:, 0:4, :], w_pa[:, :, 0:P]).then_inc(s_pa, 16)
            sp.dma_start(hw3[1], w_pb[:, :, 0:P]).then_inc(s_pb, 16)
            with sp.Fori(1, KC) as f:
                sp.wait_ge(pa_filled, f)
                sp.dma_start(hw3[0][:, 0:4, :], w_pa[:, :, bass.ds(f * P, P)]).then_inc(s_pa, 16)
                sp.wait_ge(pb_filled, f)
                sp.dma_start(hw3[1], w_pb[:, :, bass.ds(f * P, P)]).then_inc(s_pb, 16)
            sp.wait_ge(rt_filled, NT)
            sp.dma_start(wo_sb, d["w_o"].rearrange("(c p) n -> p c n", p=P)).then_inc(s_wo, 16)
            sp.dma_start(wsh[:, :, 0:F], d["w_sh_gate"].rearrange("(p c) n -> p c n", c=KC)).then_inc(s_wsh, 16)
            sp.dma_start(wsh[:, :, F:], d["w_sh_up"].rearrange("(p c) n -> p c n", c=KC)).then_inc(s_wsh, 16)
            sp.dma_start(rows[:, 0:D], d["ln1_g"].to_broadcast([P, D])).then_inc(s_ln1, 16)
            sp.dma_start(rows[:, D:], d["ln1_b"].to_broadcast([P, D])).then_inc(s_ln1, 16)
            sp.wait_ge(pa_filled, KC)
            sp.dma_start(wsh_d, d["w_sh_down"].rearrange("(j p) n -> p j n", p=P)).then_inc(s_wsh, 16)
            sp.wait_ge(m_ready, KC)
            sp.wait_ge(x1_stored, 16 * NT)
            for i in range(NT):
                sp.dma_start(x1_back[:, i, :], d["x1_dram"][i * P:(i + 1) * P, :]).then_inc(s_x[i], 16)
            sp.dma_start(hw[:, 0:D], d["ln2_g"].to_broadcast([P, D])).then_inc(s_ln2, 16)
            sp.dma_start(hw[:, D:2 * D], d["ln2_b"].to_broadcast([P, D])).then_inc(s_ln2, 16)
            sp.dma_start(bias[:, :], d["router_bias"].to_broadcast([P, E])).then_inc(s_ln2, 16)
            for i in range(NT):
                sp.wait_ge(x2_ready, i + 1)
                sp.dma_start(d["x2_dram"][i * P:(i + 1) * P, :], x2[:, i, :]).then_inc(x2_stored, 16)
            sp.wait_ge(of_filled, NT)
            sp.dma_start(wr_sb, d["w_router"].rearrange("(p c) n -> p c n", c=KC)).then_inc(s_wr, 16)

            sp.wait_ge(x2_stored, 16 * NT)
            sp.wait_ge(tb_ready, 1)
            pairs = sp.value_load(nbi[0:1, 0:1], min_val=MIN_BLOCKS // 2, max_val=NBMAX // 2)
            wg_d = d["w_e_gate"].rearrange("e (p c) n -> e p c n", c=KC)
            wu_d = d["w_e_up"].rearrange("e (p c) n -> e p c n", c=KC)
            wd_d = d["w_e_down"].rearrange("e (j p) n -> e p j n", p=P)

            def load_expert(b, n, first=False):
                e = sp.value_load(blki[0:1, bass.ds(b, 1)], min_val=0, max_val=E - 1)
                if not first:
                    sp.wait_ge(gu_filled, b - 1)
                for src, dst in ((wg_d, wg[n]), (wu_d, wu[n])):
                    sp.dma_start(dst, src[bass.ds(e, 1), :, :, :].rearrange("e p c n -> (e p) c n")).then_inc(s_wgu[n], 16)
                if not first:
                    sp.wait_ge(y_filled, b - 1)
                sp.dma_start(wd[n], wd_d[bass.ds(e, 1), :, :, :].rearrange("e p j n -> (e p) j n")).then_inc(s_wd[n], 16)

            load_expert(0, 0, True)
            load_expert(1, 1, True)
            with sp.Fori(1, pairs) as r:
                load_expert(r * 2, 0)
                load_expert(r * 2 + 1, 1)
            sp.wait_ge(y_stored[0], pairs * 16)
            sp.wait_ge(y_stored[1], pairs * 16)
            yb = d["y_dram"].rearrange("(t k) n -> t k n", k=KSTRIDE)
            land = [slabs(rCD[:, n * TOPK * D:(n + 1) * TOPK * D], TOPK) for n in range(2)]
            for i in range(NT):
                if i >= 2:
                    sp.wait_ge(yb_used, i - 1)
                sp.dma_start(land[i % 2], yb[i * P:(i + 1) * P, 0:TOPK, :]).then_inc(s_yb[i % 2], 16)
            for i in range(NT):
                sp.wait_ge(out_ready, i + 1)
                dst = d["y_prompt"][i * P:(i + 1) * P, :] if i < NTP else \
                    d["y_sample"][(i - NTP) * P:(i - NTP + 1) * P, :]
                sp.dma_start(dst, acc[:, i, :]).then_inc(out_stored, 16)
            sp.wait_ge(out_stored, 16 * NT)

        @block.tensor
        def _(pe):
            mm, tr = nc.tensor.matmul, nc.tensor.transpose

            pe.wait_ge(s_con, 16)
            pe.wait_ge(s_misc, 64)
            tr(pX[:, 0:4 * H], lbraw[0:4 * H, :], ident[0:4 * H, 0:4 * H]).then_inc(lb_filled, 1)
            for i in range(NT):
                pe.wait_ge(x1_ready, i + 1)
                if i >= 2:
                    pe.wait_ge(t_evicted, i - 1)
                for c in range(KC):
                    last = tr(pair[i % 2][:, c * P:(c + 1) * P], x_in[:, i, c:D:KC], ident)
                last.then_inc(t_filled, 1)
            for n in range(6):
                pe.wait_ge(s_strip[n % 2], 16 * (n // 2 + 1))
                for i in range(NT):
                    fill = n * NT + i
                    if n == 0:
                        pe.wait_ge(t_evicted, i + 1)
                    if fill >= 2:
                        pe.wait_ge(g_evicted, fill - 1)
                    for c in range(KC):
                        last = mm(pg[:, (fill % 2) * 512:(fill % 2) * 512 + 512], x1T[:, c, i * P:(i + 1) * P],
                                  strip[n % 2][:, c, :], start=(c == 0), stop=(c == KC - 1))
                    last.then_inc(g_filled, 1)
                if n == 1:
                    for g in range(AG):
                        last = tr(pA[:, g * P:(g + 1) * P], ws_sb[:, g, :], ident)
                    last.then_inc(ws_filled, 1)
            pe.wait_ge(ws_evicted, 1)
            pe.wait_ge(v_normed, 1)
            for g in range(AG):
                if g >= 2:
                    pe.wait_ge(a_ready, g - 1)
                mm(pB[:, (g % 2) * 512:(g % 2) * 512 + NT * AGD], wsT[:, g, :],
                   vn_tok[:, :, g * AGD:(g + 1) * AGD], start=True, stop=True).then_inc(mix_filled, 1)

            def head_product(m, n, evicted, weights):
                if n == 0:
                    pe.wait_ge(s_hw[m], weights)
                pe.wait_ge(g_evicted, evicted)
                for c in range(KC):
                    last = mm(pg[:, n * 512:n * 512 + HALF], hw3[m][:, c, :], x1T[:, c, n * HALF:(n + 1) * HALF],
                              start=(c == 0), stop=(c == KC - 1))
                last.then_inc(g_filled, 1)

            for m in range(3):
                for n in range(2):
                    head_product(m, n, 36 + 2 * m + n - 1, 16)
            pe.wait_ge(a_ready, AG)
            for i in range(NT):
                if i >= 2:
                    pe.wait_ge(t_evicted, NT + i - 1)
                for c in range(4):
                    last = tr(pair[i % 2][:, c * P:(c + 1) * P], u_tok[:, i, c:AW:4], ident)
                last.then_inc(t_filled, 1)
            pe.wait_ge(t_evicted, 2 * NT)

            def recurrence(h, nxt):
                def start(step):
                    pe.wait_ge(hg_used, h * FILLS + max(step - 1, 0))
                    return pair[step % 2]

                def diag():
                    buf = start(0)
                    pe.wait_ge(diag_ready, h + 1)
                    for n in range(2):
                        last = mm(buf[:, n * 512:n * 512 + HALF], ones,
                                  hv("prod")[:, n * HALF:(n + 1) * HALF], start=True, stop=True)
                    last.then_inc(hg_filled, 1)

                def level(j):
                    buf = start(j + 1)
                    pe.wait_ge(lvl_ready, h * LEVELS + (j + 1))
                    kt = hv(f"K{j % 2}")
                    qt = hv(f"Q{j % 2}")
                    for i in range(NT):
                        o = (i // 3) * 512 + (i % 3) * P
                        last = mm(buf[:, o:o + P], kt[:, i * P:(i + 1) * P], qt[:, i * P:(i + 1) * P],
                                  start=True, stop=True)
                    last.then_inc(hg_filled, 1)

                def k_transposed():
                    buf = start(8)
                    pe.wait_ge(ke_ready, 2 * h + 1)
                    for s in range(8):
                        i = FWD_TILES[s] if s < 4 else BWD_TILES[s - 4]
                        o = (s // 4) * T + i * P
                        last = tr(buf[:, s * P:(s + 1) * P], hv("S", 2)[:, o:o + P], ident)
                    last.then_inc(hg_filled, 1)

                def increments():
                    buf = start(9)
                    pe.wait_ge(hg_used, h * FILLS + 9)
                    for s in range(8):
                        i = FWD_TILES[s] if s < 4 else BWD_TILES[s - 4]
                        last = mm(buf[:, s * P:(s + 1) * P], keT[:, s, :], v_tok[:, i, bass.ds(h * DK, DK)],
                                  start=True, stop=True)
                    last.then_inc(hg_filled, 1)

                def outputs():
                    buf = start(10)
                    pe.wait_ge(ke_ready, 2 * h + 2)
                    pe.wait_ge(st_ready, h + 1)
                    qe = hv("k", 2)
                    for i in range(NT):
                        o = (i // 3) * 512 + (i % 3) * P
                        terms = [(hv("AT")[:, i * P:(i + 1) * P], v_tok[:, i, bass.ds(h * DK, DK)])]
                        if i not in (0, NTP):
                            s = FWD_TILES.index(i - 1)
                            terms.append((qe[:, i * P:(i + 1) * P], states[:, s, :]))
                        if i not in (NTP - 1, NT - 1):
                            s = 4 + BWD_TILES.index(i + 1)
                            terms.append((qe[:, T + i * P:T + (i + 1) * P], states[:, s, :]))
                        for n, (a, b) in enumerate(terms):
                            last = mm(buf[:, o:o + P], a, b, start=(n == 0), stop=(n == len(terms) - 1))
                    last.then_inc(hg_filled, 1)

                def product(x):
                    if nxt is not None:
                        m, n = x // 2, x % 2
                        head_product(m, n, nxt * 6 + (36 + x - 1), nxt * 16 + 16)

                diag()
                level(0)
                product(0)
                level(1)
                product(1)
                level(2)
                product(2)
                level(3)
                product(3)
                level(4)
                level(5)
                product(4)
                level(6)
                k_transposed()
                product(5)
                increments()
                outputs()

            with pe.Fori(0, H - 1) as h:
                recurrence(h, h + 1)
            recurrence(H - 1, None)

            def gate_products(f):
                for m in range(2):
                    pe.wait_ge(s_hw[m], 16 * H + 16 + f * 16)
                    for n in range(2):
                        x = 2 * m + n
                        pe.wait_ge(g_evicted, f * 4 + (36 + 6 * H + x - 1))
                        for c in range(KC):
                            last = mm(pg[:, n * 512:n * 512 + HALF], hw3[m][:, c, :],
                                      x1T[:, c, n * HALF:(n + 1) * HALF], start=(c == 0), stop=(c == KC - 1))
                        last.then_inc(g_filled, 1)

            with pe.Fori(0, KC) as f:
                gate_products(f)
            pe.wait_ge(hg_used, H * FILLS)
            for i in range(NT):
                pe.wait_ge(r_done, i + 1)
                if i >= 2:
                    pe.wait_ge(rt_evicted, i - 1)
                for c in range(KC):
                    last = tr(pair[i % 2][:, c * P:(c + 1) * P], o_tok[:, i, c:D:KC], ident)
                last.then_inc(rt_filled, 1)
            pe.wait_ge(rt_evicted, NT)
            with pe.Fori(0, KC) as f:
                pe.wait_ge(s_pa, f * 16 + 16)
                pe.wait_ge(pa_taken, f)
                for n in range(2):
                    for c in range(4):
                        last = mm(pA[:, n * 512:n * 512 + HALF], hw3[0][:, c, :], aT[:, c, n * HALF:(n + 1) * HALF],
                                  start=(c == 0), stop=(c == 3))
                last.then_inc(pa_filled, 1)
                pe.wait_ge(s_pb, f * 16 + 16)
                pe.wait_ge(pb_taken, f)
                for n in range(2):
                    for c in range(KC):
                        last = mm(pB[:, n * 512:n * 512 + HALF], hw3[1][:, c, :], rT[:, c, n * HALF:(n + 1) * HALF],
                                  start=(c == 0), stop=(c == KC - 1))
                last.then_inc(pb_filled, 1)
            pe.wait_ge(m_ready, KC)
            pe.wait_ge(s_wo, 16)

            def x2_transposed(i):
                pe.wait_ge(x2_ready, i + 1)
                if i >= 1:
                    pe.wait_ge(x2t_evicted, i)
                for c in range(KC):
                    last = tr(pg[:, c * P:(c + 1) * P], x2[:, i, c:D:KC], ident)
                last.then_inc(x2t_filled, 1)

            pe.wait_ge(g_evicted, 36 + 6 * H + 4 * KC)
            for i in range(NT):
                if i >= 2:
                    pe.wait_ge(z_taken, i - 1)
                for n in range(2):
                    for c in range(KC):
                        last = mm(pair[i % 2][:, n * 512:(n + 1) * 512], mT[:, c, i * P:(i + 1) * P],
                                  wo_sb[:, c, n * 512:(n + 1) * 512], start=(c == 0), stop=(c == KC - 1))
                last.then_inc(of_filled, 1)
                if i >= 1:
                    x2_transposed(i - 1)
            x2_transposed(NT - 1)
            pe.wait_ge(s_wr, 16)
            pe.wait_ge(x2t_evicted, NT)
            pe.wait_ge(z_taken, NT)
            for n in range(2):
                for c in range(KC):
                    last = mm(pA[0:E, n * 512:n * 512 + HALF], wr_sb[:, c, :], x2T[:, c, n * HALF:(n + 1) * HALF],
                              start=(c == 0), stop=(c == KC - 1))
            last.then_inc(lg_filled, 1)

            def shared_up(i):
                for c in range(KC):
                    last = mm(pX[:, 0:512], x2T[:, c, i * P:(i + 1) * P], wsh[:, c, :],
                              start=(c == 0), stop=(c == KC - 1))
                last.then_inc(sh_gu, 1)

            def shared_turn(i):
                pe.wait_ge(sh_h, i + 1)
                if i >= 1:
                    pe.wait_ge(sh_hte, i)
                for j in range(2):
                    last = tr(pX[:, 512 + j * P:512 + (j + 1) * P], hid[:, j * P:(j + 1) * P], ident)
                last.then_inc(sh_ht, 1)

            def shared_down(i):
                pe.wait_ge(sh_hte, i + 1)
                if i >= 1:
                    pe.wait_ge(sh_acc, i)
                for n in range(2):
                    for j in range(2):
                        last = mm(pB[:, n * 512:(n + 1) * 512], hidT[:, j, :], wsh_d[:, j, n * 512:(n + 1) * 512],
                                  start=(j == 0), stop=(j == 1))
                last.then_inc(sh_y, 1)

            def positions():
                pe.wait_ge(sel_ready, 1)
                sel = slabs(select, NT)
                for i in range(NT):
                    for j in range(i + 1):
                        mm(pA[:, i * E:(i + 1) * E], tri if j == i else ones, sel[:, j, :],
                           start=(j == 0), stop=(j == i))
                for j in range(NT):
                    last = mm(pA[:, NT * E:(NT + 1) * E], ones, sel[:, j, :],
                              start=(j == 0), stop=(j == NT - 1))
                last.then_inc(pos_filled, 1)

            pe.wait_ge(s_wsh, 48)
            shared_up(0)
            pe.wait_ge(lg_evicted, 1)
            for i in range(NT):
                last = tr(pA[:, i * E:(i + 1) * E], lgT[0:E, i * P:(i + 1) * P], ident[0:E, 0:E])
            last.then_inc(lgt_filled, 1)
            shared_turn(0)
            for i in range(1, NT):
                shared_up(i)
                shared_down(i - 1)
                shared_turn(i)
                if i == 3:
                    positions()
            shared_down(NT - 1)
            for x in range(NT * TOPK):
                pe.wait_ge(oh_ready, x + 1)
                mm(pX[:, 0:2 * NCOL], oh_place(x), oh_block(x), start=(x == 0),
                   stop=(x == NT * TOPK - 1)).then_inc(oh_used, 1)
            pe.wait_ge(blk_ready, 1)
            tr(pX[0:1, 512:512 + P], bexp[:, :], ident).then_inc(blk_filled, 1)

            pe.wait_ge(tb_ready, 1)
            pairs = pe.value_load(nbi[0:1, 0:1], min_val=MIN_BLOCKS // 2, max_val=NBMAX // 2)

            def gathered_turn(n, loads):
                pe.wait_ge(xg_loaded[n], loads * 16)
                for c in range(KC):
                    last = tr(pg[:, c * P:(c + 1) * P], xg[n][:, c:D:KC], ident)
                last.then_inc(xt_filled, 1)

            def up(b, n, r):
                pe.wait_ge(xt_ready, b + 1)
                pe.wait_ge(s_wgu[n], r * 32 + 32)
                for m, w in ((0, wg[n]), (1, wu[n])):
                    for j in range(2):
                        o = n * 512 + (2 * m + j) * P
                        for c in range(KC):
                            last = mm(pA[:, o:o + P], w[:, c, j * P:(j + 1) * P], xT[n][:, c, :],
                                      start=(c == 0), stop=(c == KC - 1))
                last.then_inc(gu_filled, 1)

            def down(b, n, r, first=False):
                pe.wait_ge(h_ready, b + 1)
                pe.wait_ge(s_wd[n], r * 16 + 16)
                if not first:
                    pe.wait_ge(y_ready, b - 1)
                for m in range(2):
                    for j in range(2):
                        last = mm(pairY[n][:, m * 512:(m + 1) * 512], hT[n][:, j, :],
                                  wd[n][:, j, m * 512:(m + 1) * 512], start=(j == 0), stop=(j == 1))
                last.then_inc(y_filled, 1)

            def expert_block(b, n, r, first=False):
                up(b, n, r)
                gathered_turn(1 - n, r + 1 + n)
                down(b, n, r, first)

            gathered_turn(0, 1)
            for n in range(2):
                expert_block(n, n, 0, True)
            with pe.Fori(1, pairs) as r:
                for n in range(2):
                    expert_block(r * 2 + n, n, r)

        @block.scalar
        def _(sc):
            fn = nc.scalar.activation

            def root(n, times):
                sc.wait_ge(var_ready, times)
                fn(std[:, 0:n], std[:, 0:n], ACT.Sqrt).then_inc(std_ready, 1)

            root(NT, 1)
            for i in range(NT):
                sc.wait_ge(t_filled, i + 1)
                fn(x1T[:, :, i * P:(i + 1) * P], slabs(pair[i % 2][:, :], KC), ACT.Copy).then_inc(t_evicted, 1)
            sc.wait_ge(lb_sub, 1)
            fn(lbw[:, 2 * 4 * H:3 * 4 * H], lbw[:, 4 * H:2 * 4 * H], ACT.Exp).then_inc(lb_exp, 1)
            outs = ((u_tok, 0, ACT.Gelu_apprx_tanh), (vn_tok, 0, ACT.Gelu_apprx_tanh), (v_tok, 0, ACT.Copy),
                    (v_tok, 512, ACT.Copy), (g_tok, 0, ACT.Silu), (g_tok, 512, ACT.Silu))
            for n, (dst, c0, func) in enumerate(outs):
                if n == 4:
                    sc.wait_ge(x1_stored, 16 * NT)
                for i in range(NT):
                    fill = n * NT + i
                    sc.wait_ge(g_filled, fill + 1)
                    fn(dst[:, i, c0:c0 + 512], pg[:, (fill % 2) * 512:(fill % 2) * 512 + 512],
                       func).then_inc(g_evicted, 1)
                if n == 1:
                    sc.wait_ge(ws_filled, 1)
                    fn(wsT, slabs(pA[:, :], AG), ACT.Copy).then_inc(ws_evicted, 1)
                if n == 2:
                    root(NT, 2)

            def head_gates(nxt, x):
                m, n = x // 2, x % 2
                sc.wait_ge(g_filled, nxt * 6 + (36 + x + 1))
                dst = q_next if m == 0 else sig_next[:, (m - 1) * T:m * T]
                fn(dst[:, n * HALF:(n + 1) * HALF], pg[:, n * 512:n * 512 + HALF],
                   ACT.Silu if m == 0 else ACT.Sigmoid).then_inc(g_evicted, 1)

            for x in range(6):
                head_gates(0, x)
            for i in range(NT):
                sc.wait_ge(t_filled, NT + i + 1)
                fn(aT[:, :, i * P:(i + 1) * P], slabs(pair[i % 2][:, 0:4 * P], 4), ACT.Copy).then_inc(t_evicted, 1)
            with sc.Fori(1, H) as h:
                sc.wait_ge(cur_taken, h)
                for x in range(6):
                    head_gates(h, x)

            def merge_gates(f):
                for x in range(4):
                    n = x % 2
                    sc.wait_ge(g_filled, f * 4 + (36 + 6 * H + x + 1))
                    dst = sga if x < 2 else sgb
                    out = dst[:, bass.ds(f, 1), n * HALF:(n + 1) * HALF].rearrange("p a n -> p (a n)")
                    fn(out, pg[:, n * 512:n * 512 + HALF], ACT.Sigmoid).then_inc(g_evicted, 1)

            merge_gates(0)
            merge_gates(1)
            root(NT * H, 3)
            with sc.Fori(2, KC) as f:
                merge_gates(f)
            for i in range(NT):
                sc.wait_ge(rt_filled, i + 1)
                fn(rT[:, :, i * P:(i + 1) * P], slabs(pair[i % 2][:, :], KC), ACT.Copy).then_inc(rt_evicted, 1)

            def x2_turned(i):
                sc.wait_ge(x2t_filled, i + 1)
                fn(x2T[:, :, i * P:(i + 1) * P], slabs(pg[:, :], KC), ACT.Copy).then_inc(x2t_evicted, 1)

            for i in range(NT):
                if i >= 1:
                    x2_turned(i - 1)
                root(1, 4 + i)
            x2_turned(NT - 1)
            sc.wait_ge(lg_filled, 1)
            fn(lgT[0:E, :].rearrange("p (n t) -> p n t", n=2),
               slabs(pA[0:E, :], 2)[:, :, 0:HALF], ACT.Copy).then_inc(lg_evicted, 1)
            for i in range(NT):
                sc.wait_ge(sh_gu, i + 1)
                if i >= 1:
                    sc.wait_ge(sh_h, i)
                fn(silu_g[0], pX[:, 0:F], ACT.Silu).then_inc(sh_silu, 1)
                if i == 0:
                    sc.wait_ge(lgt_filled, 1)
                    fn(score, pA[:, 0:NT * E], ACT.Sigmoid).then_inc(sc_ready, 1)
                sc.wait_ge(sh_ht, i + 1)
                if i >= 1:
                    sc.wait_ge(sh_y, i)
                fn(hidT, slabs(pX[:, 512:512 + F], 2), ACT.Copy).then_inc(sh_hte, 1)

            sc.wait_ge(tb_ready, 1)
            pairs = sc.value_load(nbi[0:1, 0:1], min_val=MIN_BLOCKS // 2, max_val=NBMAX // 2)

            def gathered(b, n):
                sc.wait_ge(xt_filled, b + 1)
                fn(xT[n], slabs(pg[:, :], KC), ACT.Copy).then_inc(xt_ready, 1)

            def silu(b, n, first=False):
                sc.wait_ge(gu_filled, b + 1)
                if not first:
                    sc.wait_ge(h_ready, b - 1)
                fn(silu_g[n], pA[:, n * 512:n * 512 + F], ACT.Silu).then_inc(silu_ready, 1)

            def weighted(b, n, stores):
                sc.wait_ge(y_filled, b + 1)
                sc.wait_ge(gc_ready, b + 1)
                if stores is not None:
                    sc.wait_ge(y_stored[n], stores * 16)
                fn(yrow[n], pairY[n][:, :], ACT.Copy, scale=gcol[n]).then_inc(y_ready, 1)

            gathered(0, 0)
            silu(0, 0, True)
            gathered(1, 1)
            weighted(0, 0, None)
            silu(1, 1, True)
            gathered(2, 0)
            weighted(1, 1, None)
            with sc.Fori(1, pairs) as r:
                silu(r * 2, 0)
                gathered(r * 2 + 1, 1)
                weighted(r * 2, 0, r)
                silu(r * 2 + 1, 1)
                gathered(r * 2 + 2, 0)
                weighted(r * 2 + 1, 1, r)
            for i in range(NT):
                root(1, 4 + NT + i)

        @block.vector
        def _(ve):
            v = nc.vector
            chain = Chain(ve, dve)
            link = chain.link
            asked = [0]

            def rooted(n):
                asked[0] += 1
                ve.wait_ge(std_ready, asked[0])
                link(v.reciprocal(rstd[:, 0:n], std[:, 0:n]))

            def statistics(x, i, width):
                parts = width // 512
                for n in range(parts):
                    link(v.bn_stats(bst[:, 12 * i + 6 * n:12 * i + 6 * n + 6], x[:, n * 512:(n + 1) * 512]))
                link(v.bn_aggr(mv[:, 2 * i:2 * i + 2], bst[:, 12 * i:12 * i + 6 * parts]))

            def normalised(x, i, r, gain, offset, out=None):
                link(v.tensor_scalar(x, x, mv[:, 2 * i:2 * i + 1], rstd[:, r:r + 1], ALU.subtract, ALU.mult))
                link(v.tensor_tensor(x, x, gain, ALU.mult))
                return v.tensor_tensor(x if out is None else out, x, offset, ALU.add)

            def variances(n):
                v.tensor_scalar(std[:, 0:n], mv[:, 1:2 * n:2], LN_EPS, None, ALU.add).then_inc(var_ready, 1)

            for i in range(NT):
                ve.wait_ge(s_x[i], 16)
                statistics(x_in[:, i, :], i, D)
            variances(NT)
            rooted(NT)
            ve.wait_ge(s_rows, 32)
            for i in range(NT):
                normalised(x_in[:, i, :], i, i, rows[:, 0:D], rows[:, D:]).then_inc(x1_ready, 1)
            ve.wait_ge(lb_filled, 1)
            n1 = 4 * H
            link(v.tensor_copy(lbw[:, 0:n1], pX[:, 0:n1]))

            def layer(o, l):
                return lbw[:, o:o + n1].rearrange("p (a l h) -> p a l h", a=2, l=2)[:, :, l, :]

            two = lambda ap: ap.rearrange("p (a h) -> p a h", a=2)
            link(v.tensor_tensor(two(lbs[:, :]), layer(0, 0), layer(0, 1), ALU.max))
            for l in range(2):
                last = v.tensor_tensor(layer(n1, l), layer(0, l), two(lbs[:, :]), ALU.subtract)
                if l == 0:
                    link(last)
            last.then_inc(lb_sub, 1)
            ve.wait_ge(lb_exp, 1)
            link(v.tensor_tensor(two(lbs[:, :]), layer(2 * n1, 0), layer(2 * n1, 1), ALU.add))
            link(v.reciprocal(lbc[:, :], lbs[:, :]))
            link(v.tensor_tensor(two(lbs[:, :]), layer(2 * n1, 0), two(lbc[:, :]), ALU.mult))
            link(v.tensor_scalar(lbc[:, :], lbs[:, :], -1.0, 1.0, ALU.mult, ALU.add))
            ve.wait_ge(g_evicted, 2 * NT)
            for i in range(NT):
                statistics(vn_tok[:, i, :], i, AW)
            variances(NT)
            rooted(NT)
            ve.wait_ge(s_aln, 32)
            for i in range(NT):
                last = normalised(vn_tok[:, i, :], i, i, rows[:, 0:AW], rows[:, AW:2 * AW])
                if i < NT - 1:
                    link(last)
            last.then_inc(v_normed, 1)
            for g in range(AG):
                ve.wait_ge(mix_filled, g + 1)
                u_g = u_tok[:, :, g * AGD:(g + 1) * AGD]
                v.scalar_tensor_tensor(out=u_g, in0=slabs(pB[:, (g % 2) * 512:(g % 2) * 512 + NT * AGD], NT),
                                       scalar=sbt[:, g:g + 1], in1=u_g, op0=ALU.add, op1=ALU.mult).then_inc(a_ready, 1)
            ve.wait_ge(g_evicted, 6 * NT)
            for i in range(NT):
                link(v.tensor_tensor(g_tok[:, i, :], g_tok[:, i, :], nrow, ALU.mult))

            def both(name, half, fwd, bwd, n=T):
                return at(rEF, OFF[name] + fwd, [[T + bwd - fwd, 2], [2 * half, T // (2 * half)], [1, half]])

            def one(name, half, fwd, bwd):
                return at(rEF, OFF[name] + fwd, [[bwd - fwd, 2], [2 * half, T // (2 * half)], [1, half]])

            def total(half, fwd, bwd):
                return at(rEF, OFF["P"] + fwd, [[T + bwd - fwd, 2], [2 * half, T // (2 * half)], [0, half]])

            def masked_in(h, j):
                mask = con[:, K_MASK + j * P:K_MASK + (j + 1) * P].bitcast(I32)
                v.copy_predicated(at(rEF, OFF["AT"], [[HALF, 2], [P, 3], [1, P]]),
                                  bass.AP(mask.tensor, mask.offset, [list(mask.ap[0]), [0, 2], [0, 3], [1, P]]),
                                  at(pair[(j + 1) % 2], 0, [[512, 2], [P, 3], [1, P]])).then_inc(hg_used, 1)

            chain.restart()
            with ve.Fori(0, H) as h:
                ve.wait_ge(g_evicted, h * 6 + (36 + 6))
                link(v.tensor_copy(hv("q"), q_next))
                for a in range(2):
                    last = v.tensor_scalar(hv("P", 2)[:, a * T:(a + 1) * T], sig_next[:, a * T:(a + 1) * T],
                                           lbc[:, bass.ds(h + a * H, 1)], lbs[:, bass.ds(h + a * H, 1)],
                                           ALU.mult, ALU.add)
                    if a == 0:
                        link(last)
                last.then_inc(cur_taken, 1)
                ve.wait_ge(cur_taken, h + 1)
                link(v.tensor_scalar(hv("k", 2), hv("P", 2), -1.0, 1.0, ALU.mult, ALU.add))
                link(v.tensor_tensor(hv("prod"), hv("k", 2)[:, 0:T], hv("k", 2)[:, T:], ALU.add))
                v.tensor_tensor(hv("prod"), hv("prod"), hv("q"), ALU.mult).then_inc(diag_ready, 1)
                link(v.memset(hv("S", 2), 1.0))
                for j in range(LEVELS):
                    half = 1 << j
                    link(v.tensor_tensor(one(f"Q{j % 2}", half, half, 0), one("q", half, half, 0),
                                         both("P", half, half, 0), ALU.mult))
                    v.tensor_tensor(one(f"K{j % 2}", half, 0, half), both("k", half, 0, half),
                                    both("S", half, 0, half), ALU.mult).then_inc(lvl_ready, 1)
                    link(v.tensor_tensor(both("S", half, 0, half), both("S", half, 0, half),
                                         total(half, 2 * half - 1, 0), ALU.mult))
                    if j > 0:
                        ve.wait_ge(hg_filled, h * FILLS + (j + 1))
                    link(v.tensor_tensor(both("P", half, half, 0), both("P", half, half, 0),
                                         total(half, half - 1, half), ALU.mult))
                    if j == 0:
                        ve.wait_ge(hg_filled, h * FILLS + 1)
                        eye = bass.AP(ident.tensor, ident.offset, [list(ident.ap[0]), [0, 2], [0, 3], [1, P]])
                        v.tensor_tensor(at(rEF, OFF["AT"], [[HALF, 2], [P, 3], [1, P]]),
                                        at(pair[0], 0, [[512, 2], [P, 3], [1, P]]), eye, ALU.mult).then_inc(hg_used, 1)
                        ve.wait_ge(hg_used, h * FILLS + 1)
                    else:
                        masked_in(h, j - 1)
                        ve.wait_ge(hg_used, h * FILLS + (j + 1))
                v.tensor_tensor(hv("S", 2), hv("S", 2), hv("k", 2), ALU.mult).then_inc(ke_ready, 1)
                ve.wait_ge(ke_ready, h * 2 + 1)
                v.tensor_tensor(slabs(hv("k", 2), 2), at(rEF, OFF["q"], [[0, 2], [1, T]]),
                                slabs(hv("P", 2), 2), ALU.mult).then_inc(ke_ready, 1)
                ve.wait_ge(hg_filled, h * FILLS + (LEVELS + 1))
                link(v.memset(std[:, 0:1], 0.0))
                masked_in(h, LEVELS - 1)
                ve.wait_ge(hg_filled, h * FILLS + 9)
                v.tensor_copy(keT, slabs(pair[0][:, :], 8)).then_inc(hg_used, 1)
                ve.wait_ge(hg_filled, h * FILLS + 10)
                corners = [[4 * P, 2], [3 * P, 2], [1, P]]
                link(v.tensor_copy(at(ew, 8 * P, corners), at(pair[1], 0, corners)))
                for s in (1, 2, 5, 6):
                    i = FWD_TILES[s] if s < 4 else BWD_TILES[s - 4]
                    edge = i * P + P - 1 if s < 4 else T + i * P
                    last = v.scalar_tensor_tensor(out=states[:, s, :], in0=states[:, s - 1, :],
                                                  scalar=hv("P", 2)[:, edge:edge + 1],
                                                  in1=pair[1][:, s * P:(s + 1) * P], op0=ALU.mult, op1=ALU.add)
                    if s < 6:
                        link(last)
                last.then_inc(st_ready, 1)
                ve.wait_ge(st_ready, h + 1)
                v.memset(std[:, 0:1], 0.0).then_inc(hg_used, 1)
                ve.wait_ge(hg_filled, h * FILLS + 11)
                out = o_tok[:, :, bass.ds(h * DK, DK)]
                for n in range(2):
                    last = v.tensor_copy(out[:, 3 * n:3 * n + 3, :], slabs(pair[0][:, n * 512:n * 512 + HALF], 3))
                    if n == 0:
                        link(last)
                last.then_inc(hg_used, 1)
                chain.restart()
            ve.wait_ge(hg_used, H * FILLS)

            square = ew[:, 2 * D:3 * D]
            for i in range(NT):
                link(v.tensor_tensor(square, o_tok[:, i, :], o_tok[:, i, :], ALU.mult))
                link(v.tensor_reduce(std[:, i * H:(i + 1) * H], slabs(square, H), AX.X, ALU.add))
            v.tensor_scalar(std[:, 0:NT * H], std[:, 0:NT * H], 1.0 / DK, RMS_EPS, ALU.mult, ALU.add).then_inc(var_ready, 1)
            rooted(NT * H)
            for i in range(NT):
                link(v.tensor_tensor(slabs(o_tok[:, i, :], H), slabs(o_tok[:, i, :], H),
                                     at(rstd, i * H, [[1, H], [0, DK]]), ALU.mult))
                v.tensor_tensor(o_tok[:, i, :], o_tok[:, i, :], g_tok[:, i, :], ALU.mult).then_inc(r_done, 1)
            ve.wait_ge(g_evicted, 36 + 6 * H + 4 * KC)
            chain.restart()
            with ve.Fori(0, KC) as f:
                ve.wait_ge(pa_filled, f + 1)
                gate_a = sga[:, bass.ds(f, 1), :].rearrange("p a (n t) -> p (a n) t", n=2)
                gate_b = sgb[:, bass.ds(f, 1), :].rearrange("p a (n t) -> p (a n) t", n=2)
                v.tensor_tensor(slabs(ew[:, 0:T], 2), slabs(pA[:, :], 2)[:, :, 0:HALF], gate_a, ALU.mult).then_inc(pa_taken, 1)
                ve.wait_ge(pb_filled, f + 1)
                v.tensor_tensor(slabs(ew[:, T:2 * T], 2), slabs(pB[:, :], 2)[:, :, 0:HALF], gate_b, ALU.mult).then_inc(pb_taken, 1)
                ve.wait_ge(pa_taken, f + 1)
                ve.wait_ge(pb_taken, f + 1)
                v.tensor_tensor(mT[:, bass.ds(f, 1), :].rearrange("p a t -> p (a t)"), ew[:, 0:T], ew[:, T:2 * T],
                                ALU.add).then_inc(m_ready, 1)
                ve.wait_ge(m_ready, f + 1)
            ve.wait_ge(s_ln1, 32)
            for i in range(NT):
                ve.wait_ge(of_filled, i + 1)
                ve.wait_ge(s_x[i], 32)
                v.scalar_tensor_tensor(out=x2[:, i, :], in0=x1_back[:, i, :], scalar=ALPHA, in1=pair[i % 2][:, :],
                                       op0=ALU.mult, op1=ALU.add).then_inc(z_taken, 1)
                ve.wait_ge(z_taken, i + 1)
                statistics(x2[:, i, :], 0, D)
                variances(1)
                rooted(1)
                normalised(x2[:, i, :], 0, 0, rows[:, 0:D], rows[:, D:]).then_inc(x2_ready, 1)

            def shared_hidden(i):
                ve.wait_ge(sh_silu, i + 1)
                if i >= 1:
                    ve.wait_ge(sh_ht, i)
                v.tensor_tensor(hid, silu_g[0], pX[:, F:2 * F], ALU.mult).then_inc(sh_h, 1)

            def shared_added(i):
                ve.wait_ge(sh_y, i + 1)
                v.scalar_tensor_tensor(out=acc[:, i, :], in0=x2[:, i, :], scalar=ALPHA, in1=pB[:, :],
                                       op0=ALU.mult, op1=ALU.add).then_inc(sh_acc, 1)

            def v3(ap, b, c):
                return ap.rearrange("p (a b c) -> p a b c", b=b, c=c)

            def per(region_view, dims):
                return bass.AP(region_view.tensor, region_view.offset, [list(region_view.ap[0])] + dims)

            def group_scores():
                ve.wait_ge(sc_ready, 1)
                ve.wait_ge(s_ln2, 48)
                link(v.tensor_tensor(slabs(biased, NT), slabs(score, NT), per(bias[:, :], [[0, NT], [1, E]]), ALU.add))
                link(v.tensor_reduce(best, slabs(biased, NT * EG), AX.X, ALU.max))
                spread = lambda ap: per(ap, [[1, NT * EG], [0, E // EG]])
                link(v.tensor_tensor(slabs(allowed, NT * EG), slabs(biased, NT * EG), spread(best), ALU.is_equal))
                link(v.tensor_reduce(gcnt, slabs(allowed, NT * EG), AX.X, ALU.add))
                link(v.scalar_tensor_tensor(out=allowed, in0=allowed, scalar=-BIG, in1=biased, op0=ALU.mult, op1=ALU.add))
                link(v.tensor_reduce(second, slabs(allowed, NT * EG), AX.X, ALU.max))
                link(v.tensor_scalar(gcnt, gcnt, 2.0, 1.0, ALU.is_ge, ALU.subtract))
                link(v.scalar_tensor_tensor(out=gcnt, in0=gcnt, scalar=BIG, in1=best, op0=ALU.mult, op1=ALU.add))
                link(v.tensor_tensor(second, second, gcnt, ALU.max))
                link(v.tensor_tensor(gsum, best, second, ALU.add))

            def group_choice():
                for i in range(NT):
                    o = slice(8 * i, 8 * i + 8)
                    link(v.max(out=gtop[:, o], in_=gsum[:, o]))
                    link(v.max_index(out=gidx[:, o].bitcast(U32), in_max=gtop[:, o], in_values=gsum[:, o]))
                link(v.tensor_copy(gidxf, gidx.bitcast(U32)))
                link(v.tensor_tensor(v3(work[:, 0:NT * EG * TOPG], EG, TOPG), per(iota, [[0, NT], [1, EG], [0, TOPG]]),
                                     per(gidxf, [[8, NT], [0, EG], [1, TOPG]]), ALU.is_equal))
                link(v.tensor_reduce(gmask, slabs(work[:, 0:NT * EG * TOPG], NT * EG), AX.X, ALU.add))
                link(v.tensor_scalar(gmask, gmask, 1.0, BIG, ALU.subtract, ALU.mult))
                link(v.tensor_tensor(slabs(allowed, NT * EG), slabs(biased, NT * EG),
                                     per(gmask, [[1, NT * EG], [0, E // EG]]), ALU.add))

            def expert_choice():
                for i in range(NT):
                    o = slice(8 * i, 8 * i + 8)
                    link(v.max(out=etop[:, o], in_=allowed[:, i * E:(i + 1) * E]))
                    link(v.max_index(out=eidx[:, o].bitcast(U32), in_max=etop[:, o], in_values=allowed[:, i * E:(i + 1) * E]))
                link(v.tensor_copy(eidxf, eidx.bitcast(U32)))
                link(v.tensor_tensor(v3(onehot, TOPK, E), per(iota, [[0, NT], [0, TOPK], [1, E]]),
                                     per(eidxf, [[8, NT], [1, TOPK], [0, E]]), ALU.is_equal))
                v.tensor_reduce(select, per(onehot, [[TOPK * E, NT], [1, E], [E, TOPK]]), AX.X,
                                ALU.add).then_inc(sel_ready, 1)

            def expert_gates():
                link(v.tensor_tensor(v3(work, TOPK, E), v3(onehot, TOPK, E),
                                     per(score, [[E, NT], [0, TOPK], [1, E]]), ALU.mult))
                link(v.tensor_reduce(gatew, slabs(work, NK), AX.X, ALU.add))
                link(v.tensor_reduce(wsum, slabs(gatew, NT), AX.X, ALU.add))
                link(v.reciprocal(wsum, wsum))
                link(v.scalar_tensor_tensor(out=slabs(gate, NT), in0=slabs(gatew, NT), scalar=SCALE,
                                            in1=per(wsum, [[1, NT], [0, TOPK]]), op0=ALU.mult, op1=ALU.mult))

            def slots():
                ve.wait_ge(pos_filled, 1)
                cnt = pA[:, NT * E:(NT + 1) * E]
                link(v.tensor_scalar(nblk, cnt, 0.0, None, ALU.is_gt))
                for b in range(1, NT):
                    link(v.scalar_tensor_tensor(out=nblk, in0=cnt, scalar=float(P * b), in1=nblk, op0=ALU.is_gt, op1=ALU.add))
                link(v.tensor_tensor_scan(incl, ones[:, 0:E], nblk, 0.0, ALU.mult, ALU.add))
                link(v.tensor_tensor(base, incl, nblk, ALU.subtract))
                link(v.scalar_tensor_tensor(out=slabs(posd, NT), in0=per(base, [[0, NT], [1, E]]), scalar=float(P),
                                            in1=slabs(pA[:, 0:NT * E], NT), op0=ALU.mult, op1=ALU.add))
                link(v.tensor_scalar(work[:, 0:E], incl, con[:, K_IOTAP:K_IOTAP + 1], None, ALU.is_le))
                link(v.tensor_reduce(bexp[:, :], work[:, 0:E], AX.X, ALU.add))
                v.tensor_scalar(bexp[:, :], bexp[:, :], float(E - 1), None, ALU.min).then_inc(blk_ready, 1)
                link(v.tensor_scalar(nbi[0:1, 2:3], incl[0:1, E - 1:E], 1.0, None, ALU.add))
                link(v.tensor_scalar(nbi[0:1, 0:1], nbi[0:1, 2:3], 1, None, ALU.logical_shift_right))
                link(v.tensor_scalar(nbi[0:1, 1:2], nbi[0:1, 0:1], 2.0, -1.0, ALU.mult, ALU.add))
                link(v.tensor_tensor(v3(work, TOPK, E), v3(onehot, TOPK, E),
                                     per(posd, [[E, NT], [0, TOPK], [1, E]]), ALU.mult))
                link(v.tensor_reduce(slot, slabs(work, NK), AX.X, ALU.add))
                link(v.tensor_copy(slotl.bitcast(I32), slot))
                link(v.tensor_scalar(sloth.bitcast(I32), slotl.bitcast(I32), 7, None, ALU.logical_shift_right))
                link(v.tensor_scalar(slotl.bitcast(I32), slotl.bitcast(I32), P - 1, None, ALU.bitwise_and))
                link(v.tensor_copy(low, slotl.bitcast(I32)))
                link(v.tensor_copy(high, sloth.bitcast(I32)))

            def slot_onehots(x):
                if x >= 4:
                    ve.wait_ge(oh_used, x - 3)
                link(v.tensor_scalar(oh_place(x), iota, low[:, x:x + 1], None, ALU.is_equal))
                blocks = iota[:, 0:NCOL]
                link(v.tensor_scalar(oh_block(x)[:, 0:NCOL], blocks, high[:, x:x + 1],
                                     con[:, K_DST + x:K_DST + x + 1], ALU.is_equal, ALU.mult))
                v.tensor_scalar(oh_block(x)[:, NCOL:], blocks, high[:, x:x + 1], gate[:, x:x + 1],
                                ALU.is_equal, ALU.mult).then_inc(oh_ready, 1)

            shared_hidden(0)
            group_scores()
            group_choice()
            shared_hidden(1)
            shared_added(0)
            expert_choice()
            shared_hidden(2)
            shared_added(1)
            expert_gates()
            shared_hidden(3)
            shared_added(2)
            slots()
            shared_hidden(4)
            shared_added(3)
            shared_hidden(5)
            shared_added(4)
            shared_added(5)
            for x in range(NK):
                slot_onehots(x)
            ve.wait_ge(blk_filled, 1)
            link(v.tensor_copy(blki[0:1, 0:P], pX[0:1, 512:512 + P]))
            link(v.tensor_copy(tblg[:, 0:NCOL], pX[:, NCOL:2 * NCOL]))
            link(v.tensor_scalar(tbld[:, 0:NCOL], pX[:, 0:NCOL], 0.5, float(NOWHERE), ALU.is_lt, ALU.mult))
            link(v.scalar_tensor_tensor(out=tbld[:, 0:NCOL], in0=pX[:, 0:NCOL], scalar=-1.0, in1=tbld[:, 0:NCOL],
                                        op0=ALU.add, op1=ALU.add))
            link(v.tensor_copy(tbldi[:, 0:NCOL], tbld[:, 0:NCOL]))
            v.tensor_scalar(tblti[:, 0:NCOL], tbldi[:, 0:NCOL], 3, None, ALU.logical_shift_right).then_inc(tb_ready, 1)

            ve.wait_ge(tb_ready, 1)
            pairs = ve.value_load(nbi[0:1, 0:1], min_val=MIN_BLOCKS // 2, max_val=NBMAX // 2)

            def hidden(b, n, first=False):
                ve.wait_ge(silu_ready, b + 1)
                if not first:
                    ve.wait_ge(y_filled, b - 1)
                v.tensor_tensor(hT[n], slabs(silu_g[n], 2), slabs(pA[:, n * 512 + F:n * 512 + 2 * F], 2),
                                ALU.mult).then_inc(h_ready, 1)

            def gate_column(b, n, first=False):
                if not first:
                    ve.wait_ge(y_ready, b - 1)
                v.tensor_copy(gcol[n], tblg[:, bass.ds(b, 1)]).then_inc(gc_ready, 1)

            for n in range(2):
                hidden(n, n, True)
                gate_column(n, n, True)
            with ve.Fori(1, pairs) as r:
                for n in range(2):
                    hidden(r * 2 + n, n)
                    gate_column(r * 2 + n, n)
            land = [slabs(rCD[:, n * TOPK * D:(n + 1) * TOPK * D], TOPK) for n in range(2)]
            routed = rA[:, D:2 * D]
            for i in range(NT):
                ve.wait_ge(s_yb[i % 2], 16 * (i // 2 + 1))
                v.tensor_reduce(routed, land[i % 2].rearrange("p k n -> p n k"), AX.X, ALU.add).then_inc(yb_used, 1)
                ve.wait_ge(yb_used, i + 1)
                link(v.tensor_tensor(acc[:, i, :], acc[:, i, :], routed, ALU.add))
                statistics(acc[:, i, :], 0, D)
                variances(1)
                rooted(1)
                normalised(acc[:, i, :], 0, 0, hw[:, 0:D], hw[:, D:2 * D]).then_inc(out_ready, 1)

        @block.gpsimd
        def _(po):
            g = nc.gpsimd
            po.wait_ge(of_filled, NT)
            g.memset(xg[0], 0.0).then_inc(xg_clear, 1)
            po.wait_ge(x2_stored, 16 * NT)
            po.wait_ge(tb_ready, 1)
            g.memset(xg[1], 0.0).then_inc(xg_clear, 1)
            po.wait_ge(xg_clear, 2)
            pairs = po.value_load(nbi[0:1, 0:1], min_val=MIN_BLOCKS // 2, max_val=NBMAX // 2)
            last_block = po.value_load(nbi[0:1, 1:2], min_val=MIN_BLOCKS - 1, max_val=NBMAX - 1)

            def gather(b, n, chain, first=False):
                if not first:
                    po.wait_ge(xt_filled, b - 1)
                chain.link(g.tensor_copy(tokcol[n], tblti[:, bass.ds(b, 1)]))
                g.indirect_dma_start(xg[n], None, d["x2_dram"], bass.IndirectOffsetOnAxis(tokcol[n], 0),
                                     bounds_check=T - 1, oob_is_err=False).then_inc(xg_loaded[n], 16)

            def scatter(b, n, chain):
                po.wait_ge(y_ready, b + 1)
                chain.link(g.tensor_copy(dstcol[n], tbldi[:, bass.ds(b, 1)]))
                g.indirect_dma_start(d["y_dram"], bass.IndirectOffsetOnAxis(dstcol[n], 0), yrow[n], None,
                                     bounds_check=T * KSTRIDE - 1, oob_is_err=False).then_inc(y_stored[n], 16)

            chain = Chain(po, pool)
            gather(0, 0, chain, True)
            gather(1, 1, chain, True)
            gather(2, 0, chain)
            gather(3, 1, chain)
            scatter(0, 0, chain)
            chain.restart()
            with po.Fori(1, pairs) as r:
                gather(r * 2 + 2, 0, chain)
                scatter(r * 2 - 1, 1, chain)
                gather(r * 2 + 3, 1, chain)
                scatter(r * 2, 0, chain)
                chain.restart()
            scatter(last_block, 1, chain)
            for n in range(2):
                po.wait_ge(xg_loaded[n], pairs * 16 + 16)


_INS = ("x_prompt", "x_sample", "ln_in_g", "ln_in_b", "w_in", "a_ln_g", "a_ln_b", "a_ws", "a_sb",
        "hg_lb_logits", "hg_norm_g", "w_pa", "w_pb", "w_o", "ln1_g", "ln1_b", "w_router", "router_bias",
        "w_e_gate", "w_e_up", "w_e_down", "w_sh_gate", "w_sh_up", "w_sh_down", "ln2_g", "ln2_b")
_ROWS = {"ln_in_g", "ln_in_b", "a_ln_g", "a_ln_b", "hg_norm_g", "ln1_g", "ln1_b", "router_bias", "ln2_g", "ln2_b"}


def kernel(**inputs):
    import concourse.bacc as bacc
    from concourse.bass_utils import run_bass_kernel_spmd

    nc = bacc.Bacc("TRN2", target_bir_lowering=False, num_devices=1)
    arrays, d = {}, {}
    for name in _INS:
        a = np.ascontiguousarray(inputs[name])
        if name in _ROWS:
            a = a.reshape(1, -1)
        elif name != "hg_lb_logits":
            a = a.reshape(a.shape[1:])
        arrays[name] = a
    arrays["consts"] = constants()
    for name, a in arrays.items():
        d[name] = nc.dram_tensor(name, a.shape, mybir.dt.from_np(a.dtype), kind="ExternalInput").ap()
    d["y_prompt"] = nc.dram_tensor("y_prompt", (SEQ, D), F32, kind="ExternalOutput").ap()
    d["y_sample"] = nc.dram_tensor("y_sample", (DEC_SEQ, D), F32, kind="ExternalOutput").ap()
    d["x1_dram"] = nc.dram_tensor("x1_dram", (T, D), F32).ap()
    d["x2_dram"] = nc.dram_tensor("x2_dram", (T, D), F32).ap()
    d["y_dram"] = nc.dram_tensor("y_dram", (T * KSTRIDE, D), F32).ap()
    build(nc, d)
    r = run_bass_kernel_spmd(nc, [arrays], core_ids=[0]).results[0]
    return r["y_prompt"].reshape(1, SEQ, D), r["y_sample"].reshape(1, DEC_SEQ, D)
```

```python
from contextlib import ExitStack

import numpy as np

import concourse.bass as bass
import concourse.mybir as mybir

F32 = mybir.dt.float32
I32 = mybir.dt.int32
U32 = mybir.dt.uint32
ALU = mybir.AluOpType
ACT = mybir.ActivationFunctionType
AX = mybir.AxisListType

P = 128
D = 1024
SEQ, DEC_SEQ = 512, 256
T = SEQ + DEC_SEQ
NT = T // P
NTP = SEQ // P
KC = D // P
HALF = T // 2
AW = 512
AG = 8
AGD = AW // AG
H = 8
DK = 128
LEVELS = 7
E = 64
EG = 8
TOPK = 6
TOPG = 4
F = 256
KSTRIDE = 8
MIN_BLOCKS = T * TOPK // P
NBMAX = MIN_BLOCKS + E
NCOL = NBMAX + 2
SCALE = 2.5
ALPHA = 2.0 ** 0.25
LN_EPS = 1e-5
RMS_EPS = 1e-6
BIG = 1e30
NOWHERE = 1 << 20
C_U, C_V, C_Q, C_FF, C_FB, C_I, C_G, C_GA, C_GB = 0, 512, 1024, 2048, 3072, 4096, 5120, 6144, 7168

K_IDENT = 0
K_ONES = K_IDENT + P
K_TRI = K_ONES + P
K_IOTA = K_TRI + P
K_MASK = K_IOTA + P
K_IOTAP = K_MASK + LEVELS * P
K_DST = K_IOTAP + 1
NCONST = K_DST + NT * TOPK

FILLS = 11
USES = 8
PRE = 5 * NT
PARTS = 6 * KC
POST = PRE + 6 * H + NT
FWD_TILES = (0, 1, 2, 4)
BWD_TILES = (3, 2, 1, 5)


def constants():
    c = np.zeros((P, NCONST), np.float32)
    p = np.arange(P)
    c[:, K_IDENT:K_IDENT + P] = np.eye(P)
    c[:, K_ONES:K_ONES + P] = 1.0
    c[:, K_TRI:K_TRI + P] = p[:, None] < p[None, :]
    c[:, K_IOTA:K_IOTA + P] = p[None, :]
    for j in range(LEVELS):
        same = (p[:, None] >> (j + 1)) == (p[None, :] >> (j + 1))
        c[:, K_MASK + j * P:K_MASK + (j + 1) * P] = same & ((p[:, None] >> j) != (p[None, :] >> j))
    c[:, K_IOTAP] = p
    for i in range(NT):
        for k in range(TOPK):
            c[:, K_DST + i * TOPK + k] = (i * P + p) * KSTRIDE + k + 1
    return c


class Chain:

    def __init__(self, eng, sem):
        self.eng, self.sem, self.n = eng, sem, 0

    def link(self, ins):
        self.n += 1
        ins.then_inc(self.sem, 1)
        self.eng.wait_ge(self.sem, self.n)

    def restart(self):
        self.eng.wait_ge(self.sem, self.n)
        self.eng.sem_clear(self.sem)
        self.n = 0


def build(nc, d):
    with ExitStack() as ctx:
        def sb(name, words, dt=F32):
            return ctx.enter_context(nc.sbuf_tensor(name, [P, words], dt))

        def ps(name, words):
            return ctx.enter_context(nc.psum_tensor(name, [P, words], F32))

        def sem(name):
            return ctx.enter_context(nc.semaphore(name))

        con = sb("con", NCONST)
        rA = sb("rA", KC * T)
        rB = sb("rB", KC * T)
        rCD = sb("rCD", 2 * KC * T)
        rEF = sb("rEF", 2 * KC * T)
        aTr = sb("aTr", 4 * T)
        hw = sb("hw", 3 * KC * P)
        ew = sb("ew", 6 * D)
        rows = sb("rows", 2 * D)
        lbs = sb("lbs", 2 * H)
        lbc = sb("lbc", 2 * H)
        sbt = sb("sbt", AG)
        lbraw = sb("lbraw", P)
        blki = lbraw[:, :].bitcast(I32)
        lbw = sb("lbw", 4 * 4 * H)
        bias = sb("bias", E)
        bst = sb("bst", 12 * NT)
        mv = sb("mv", 2 * NT)
        std = sb("std", NT * H)
        rstd = sb("rstd", NT * H)
        bexp = sb("bexp", 1)
        nbi = sb("nbi", 8, I32)

        ident = con[:, K_IDENT:K_IDENT + P]
        ones = con[:, K_ONES:K_ONES + P]
        tri = con[:, K_TRI:K_TRI + P]
        iota = con[:, K_IOTA:K_IOTA + P]

        def slabs(ap, c):
            return ap.rearrange("p (c n) -> p c n", c=c)

        def at(region, offset, dims):
            ap = region[:, :]
            return bass.AP(ap.tensor, ap.offset + offset, [list(ap.ap[0])] + [list(x) for x in dims])

        x1T = slabs(rA[:, :], KC)
        mT = x1T
        v_tok = slabs(rB[:, :], NT)
        rT = slabs(rB[:, :], KC)
        x2 = slabs(rB[:, :], NT)
        x_in = slabs(rCD[:, 0:NT * D], NT)
        g_tok = slabs(rCD[:, 0:NT * D], NT)
        o_tok = slabs(rCD[:, NT * D:], NT)
        u_tok = slabs(rCD[:, NT * D:NT * D + NT * AW], NT)
        vn_tok = slabs(rCD[:, NT * D + NT * AW:], NT)
        wo_sb = slabs(rCD[:, 0:KC * D], KC)
        wsh = slabs(rCD[:, KC * D:KC * D + KC * 2 * F], KC)
        strip = [slabs(rEF[:, n * KC * 512:(n + 1) * KC * 512], KC) for n in range(2)]
        ws_sb = slabs(rEF[:, 2 * KC * 512:2 * KC * 512 + AG * P], AG)
        wsT = slabs(rEF[:, 2 * KC * 512 + AG * P:2 * KC * 512 + 2 * AG * P], AG)
        sga = slabs(rEF[:, 0:KC * T], KC)
        sgb = slabs(rEF[:, KC * T:], KC)
        x1_back = slabs(rEF[:, 0:NT * D], NT)
        acc = x1_back
        x2T = slabs(rEF[:, KC * T:], KC)
        aT = slabs(aTr[:, :], 4)
        wsh_d = slabs(aTr[:, 0:2 * D], 2)
        hw3 = [slabs(hw[:, m * KC * P:(m + 1) * KC * P], KC) for m in range(3)]
        nrow = ew[:, 3 * D:4 * D]

        g_strip = [slabs(r, KC // 2) for r in (ew[:, 4 * D:6 * D], rows[:, :])]

        q_next, sig_next = rEF[:, 0:T], rEF[:, T:3 * T]
        OFF = {"q": 3 * T, "P": 4 * T, "k": 6 * T, "S": 8 * T, "Q0": 10 * T, "Q1": 11 * T,
               "K0": 12 * T, "K1": 13 * T, "prod": 14 * T, "AT": 15 * T}
        keT = slabs(ew[:, 0:8 * P], 8)
        states = slabs(ew[:, 8 * P:16 * P], 8)

        def hv(name, n=1):
            return rEF[:, OFF[name]:OFF[name] + n * T]

        cut = [0]

        def scratch(n):
            cut[0] += n
            assert cut[0] <= KC * D
            return rCD[:, cut[0] - n:cut[0]]

        NK = NT * TOPK
        onehot, work = scratch(NK * E), scratch(NK * E)
        score, biased, allowed, select, posd = (scratch(NT * E) for _ in range(5))
        best, second, gsum, gcnt, gmask = (scratch(NT * EG) for _ in range(5))
        gtop, gidx, gidxf, etop, eidx, eidxf = (scratch(NT * 8) for _ in range(6))
        gate, gatew, slot, slotl, sloth, low, high = (scratch(NK) for _ in range(7))
        wsum, nblk, incl, base = scratch(NT), scratch(E), scratch(E), scratch(E)

        def oh_place(x):
            return rows[:, (x % 4) * (P + 2 * NCOL):][:, 0:P]

        def oh_block(x):
            return rows[:, (x % 4) * (P + 2 * NCOL) + P:][:, 0:2 * NCOL]

        weights = (ew[:, :], rEF[:, KC * T:])
        wg, wu, wd = [[slabs(w[:, n * 2 * D:(n + 1) * 2 * D], c) for w in weights]
                      for n, c in ((0, KC), (1, KC), (2, 2))]
        work2 = (rA[:, 0:3 * D + 4 * F], rB[:, 0:3 * D + 4 * F])
        xg = [w[:, 0:D] for w in work2]
        xT = [slabs(w[:, D:2 * D], KC) for w in work2]
        yrow = [w[:, 2 * D:3 * D] for w in work2]
        silu_g = [w[:, 3 * D:3 * D + F] for w in work2]
        hT = [slabs(w[:, 3 * D + F:3 * D + 2 * F], 2) for w in work2]
        hid = rA[:, 3 * D + 2 * F:3 * D + 3 * F]
        hidT = slabs(rA[:, 3 * D + 3 * F:3 * D + 4 * F], 2)
        land = [slabs(r, TOPK) for r in (rCD[:, 0:TOPK * D], rCD[:, TOPK * D:], rB[:, :])]
        tblg = rA[:, 4 * D:4 * D + P]
        tbld = rA[:, 4 * D + P:4 * D + 2 * P]
        tbldi = rA[:, 4 * D + 2 * P:4 * D + 3 * P].bitcast(I32)
        tblti = rA[:, 4 * D + 3 * P:4 * D + 4 * P].bitcast(I32)
        tokcol, dstcol = ([rA[:, 4 * D + 4 * P + 2 * m + n:][:, 0:1].bitcast(I32) for n in range(2)]
                          for m in range(2))
        gcol = [rA[:, 4 * D + 4 * P + 4 + n:][:, 0:1] for n in range(2)]
        lgT = rA[:, 4 * D + 5 * P:4 * D + 5 * P + T]
        wr_sb = slabs(rA[:, 5 * D + 4 * P:5 * D + 4 * P + KC * E], KC)

        pg = ps("pg", 1024)
        pA = ps("pA", 1024)
        pB = ps("pB", 1024)
        pX = ps("pX", 1024)
        pair = [pA, pB]
        pairY = [pB, pX]

        def big_bank(fill):
            return (pg, pX)[(fill // 2) % 2 if fill < 4 else 0][:, (fill % 2) * 512:(fill % 2) * 512 + 512]

        s_con = sem("constants_loaded")
        s_x = [sem(f"x_loaded{i}") for i in range(NT)]
        s_rows = sem("ln_rows_loaded")
        s_aln = sem("gmlp_ln_rows_loaded")
        s_ln1 = sem("ln1_rows_loaded")
        s_ln2 = sem("ln2_rows_loaded")
        s_misc = sem("small_params_loaded")
        dve = sem("dve_chain")
        pool = sem("pool_chain")
        var_ready = sem("variance_ready")
        std_ready = sem("std_ready")
        x1_ready = sem("x1_ready")
        x1_stored = sem("x1_stored")
        t_filled = sem("transposes_in_psum")
        t_evicted = sem("transposes_in_sbuf")
        s_strip = [sem(f"strip_loaded{n}") for n in range(2)]
        s_hw = [sem(f"column_weights_loaded{m}") for m in range(3)]
        g_filled = sem("product_in_psum")
        g_evicted = sem("product_in_sbuf")
        v_normed = sem("gmlp_v_normed")
        ws_filled = sem("ws_transposed")
        ws_evicted = sem("ws_in_sbuf")
        mix_filled = sem("mix_in_psum")
        a_ready = sem("gmlp_a_ready")
        lb_filled = sem("lb_logits_transposed")
        lb_sub = sem("lb_logits_centred")
        lb_exp = sem("lb_exp_ready")
        cur_taken = sem("gates_taken")
        diag_ready = sem("diag_ready")
        lvl_ready = sem("level_ready")
        ke_ready = sem("k_decayed_ready")
        st_ready = sem("states_ready")
        hg_filled = sem("recurrence_in_psum")
        hg_used = sem("recurrence_psum_used")
        ke_evicted = sem("k_transposed_in_sbuf")
        o_evicted = sem("o_in_sbuf")
        s_cleared = sem("suffix_products_cleared")
        s_gstrip = sem("g_strip_loaded")
        r_done = sem("r_ready")
        rt_evicted = sem("rT_in_sbuf")
        rt_filled = sem("rT_in_psum")
        s_pa = sem("w_pa_loaded")
        s_pb = sem("w_pb_loaded")
        pa_filled = sem("a_projected")
        pb_filled = sem("r_projected")
        pa_taken = sem("a_projection_taken")
        pb_taken = sem("r_projection_taken")
        m_ready = sem("mixed_ready")
        s_wo = sem("w_o_loaded")
        s_x1b = sem("x1_reloaded")
        of_filled = sem("out_projection_in_psum")
        z_taken = sem("out_projection_taken")
        x2_ready = sem("x2_ready")
        x2_stored = sem("x2_stored")
        x2t_filled = sem("x2T_in_psum")
        x2t_evicted = sem("x2T_in_sbuf")
        s_wr = sem("router_loaded")
        s_wsh = sem("shared_expert_loaded")
        lg_filled = sem("logits_in_psum")
        lg_evicted = sem("logits_in_sbuf")
        lgt_filled = sem("logits_token_major")
        sc_ready = sem("scores_ready")
        sel_ready = sem("selection_ready")
        pos_filled = sem("positions_in_psum")
        oh_ready = sem("slot_onehots_ready")
        ohp_ready = sem("place_onehots_ready")
        low_ready = sem("slots_ready")
        oh_used = sem("slot_onehots_used")
        tb_filled = sem("tables_in_psum")
        blk_ready = sem("block_expert_ready")
        blk_filled = sem("block_expert_row")
        blki_ready = sem("block_experts_ready")
        tb_ready = sem("tables_ready")
        sh_gu = sem("shared_gate_up_in_psum")
        sh_silu = sem("shared_silu_ready")
        sh_h = sem("shared_hidden_ready")
        sh_ht = sem("shared_hiddenT_in_psum")
        sh_hte = sem("shared_hiddenT_ready")
        sh_y = sem("shared_down_in_psum")
        sh_acc = sem("shared_added")
        s_wgu = [sem(f"w_gate_up_loaded{n}") for n in range(2)]
        s_wd = [sem(f"w_down_loaded{n}") for n in range(2)]
        gu_filled = sem("gate_up_in_psum")
        silu_ready = sem("silu_ready")
        h_ready = sem("hidden_ready")
        y_filled = sem("down_in_psum")
        y_ready = sem("y_ready")
        gc_ready = sem("gate_column_ready")
        xg_clear = sem("gather_buffer_cleared")
        xg_loaded = [sem(f"rows_gathered{n}") for n in range(2)]
        xt_filled = sem("gathered_T_in_psum")
        xt_ready = sem("gathered_T_ready")
        y_stored = [sem(f"y_scattered{n}") for n in range(2)]
        s_yb = [[sem(f"routed_rows_loaded{n}_{m}") for m in range(2)] for n in range(3)]
        yb_used = sem("last_routed_rows_added")
        sum_filled = sem("routed_rows_summed")
        sum_taken = sem("routed_sums_taken")
        out_ready = sem("out_ready")
        out_stored = sem("out_stored")

        block = ctx.enter_context(nc.Block())

        @block.sync
        def _(sp):
            w_in = d["w_in"].rearrange("(p c) n -> p c n", c=KC)

            sp.dma_start(x_in[:, 0, :], d["x_prompt"][0:P, :]).then_inc(s_x[0], 16)
            sp.dma_start(con[:, :], d["consts"]).then_inc(s_con, 16)
            sp.dma_start(rows[:, 0:D], d["ln_in_g"].to_broadcast([P, D])).then_inc(s_rows, 16)
            sp.dma_start(rows[:, D:], d["ln_in_b"].to_broadcast([P, D])).then_inc(s_rows, 16)

            def load_x(i):
                src = d["x_prompt"][i * P:(i + 1) * P, :] if i < NTP else \
                    d["x_sample"][(i - NTP) * P:(i - NTP + 1) * P, :]
                sp.dma_start(x_in[:, i, :], src).then_inc(s_x[i], 16)

            load_x(1)
            for n, c0 in enumerate((C_U, C_V, C_I, C_I + 512, C_G)):
                if n >= 2:
                    sp.wait_ge(g_filled, NT * (n - 1))
                sp.dma_start(strip[n % 2], w_in[:, :, c0:c0 + 512]).then_inc(s_strip[n % 2], 16)
                if n == 0:
                    for i in range(2, NT):
                        load_x(i)
                    sp.dma_start(ws_sb, d["a_ws"].rearrange("g t s -> t g s")).then_inc(s_misc, 16)
                    sp.dma_start(sbt[:, :], d["a_sb"]).then_inc(s_misc, 16)
                    sp.dma_start(nrow, d["hg_norm_g"].to_broadcast([P, D])).then_inc(s_misc, 16)
                    sp.dma_start(lbraw[0:4 * H, :], d["hg_lb_logits"].rearrange(
                        "a l (h k) -> (a l h) k", h=H)).then_inc(s_misc, 16)
            sp.wait_ge(x1_ready, NT)
            for i in range(NT):
                sp.dma_start(d["x1_dram"][i * P:(i + 1) * P, :], x_in[:, i, :]).then_inc(x1_stored, 16)
            sp.dma_start(rows[:, 0:AW], d["a_ln_g"].to_broadcast([P, AW])).then_inc(s_aln, 16)
            sp.dma_start(rows[:, AW:2 * AW], d["a_ln_b"].to_broadcast([P, AW])).then_inc(s_aln, 16)
            for m, c0 in enumerate((C_Q, C_FF, C_FB)):
                sp.dma_start(hw3[m], w_in[:, :, c0:c0 + DK]).then_inc(s_hw[m], 16)
            sp.wait_ge(v_normed, 1)
            for m in range(2):
                sp.dma_start(g_strip[m], w_in[:, 4 * m:4 * m + 4, C_G + 512:C_G + D]).then_inc(s_gstrip, 16)
            with sp.Fori(1, H) as h:
                for m, c0 in enumerate((C_Q, C_FF, C_FB)):
                    sp.wait_ge(g_filled, PRE + 2 * (m + 1) + (h - 1) * 6)
                    sp.dma_start(hw3[m], w_in[:, :, bass.ds(c0 + h * DK, DK)]).then_inc(s_hw[m], 16)
            for m, c0 in enumerate((C_GA, C_GB)):
                sp.wait_ge(g_filled, PRE + 6 * H - 4 + 2 * m)
                sp.dma_start(hw3[m], w_in[:, :, c0:c0 + P]).then_inc(s_hw[m], 16)
            with sp.Fori(1, KC) as f:
                for m, c0 in enumerate((C_GA, C_GB)):
                    sp.wait_ge(g_filled, POST + 2 * (m + 1) + (f - 1) * 4)
                    sp.dma_start(hw3[m], w_in[:, :, bass.ds(c0 + f * P, P)]).then_inc(s_hw[m], 16)
            w_pa = d["w_pa"].rearrange("(p c) n -> p c n", c=4)
            w_pb = d["w_pb"].rearrange("(p c) n -> p c n", c=KC)
            sp.wait_ge(g_filled, POST + 4 * KC)
            sp.dma_start(hw3[0][:, 0:4, :], w_pa[:, :, 0:P]).then_inc(s_pa, 16)
            sp.dma_start(hw3[1], w_pb[:, :, 0:P]).then_inc(s_pb, 16)
            with sp.Fori(1, KC) as f:
                sp.wait_ge(pa_filled, f)
                sp.dma_start(hw3[0][:, 0:4, :], w_pa[:, :, bass.ds(f * P, P)]).then_inc(s_pa, 16)
                sp.wait_ge(pb_filled, f)
                sp.dma_start(hw3[1], w_pb[:, :, bass.ds(f * P, P)]).then_inc(s_pb, 16)
            sp.wait_ge(rt_filled, NT)
            sp.dma_start(wo_sb, d["w_o"].rearrange("(c p) n -> p c n", p=P)).then_inc(s_wo, 16)
            sp.dma_start(wsh[:, :, 0:F], d["w_sh_gate"].rearrange("(p c) n -> p c n", c=KC)).then_inc(s_wsh, 16)
            sp.dma_start(wsh[:, :, F:], d["w_sh_up"].rearrange("(p c) n -> p c n", c=KC)).then_inc(s_wsh, 16)
            sp.dma_start(rows[:, 0:D], d["ln1_g"].to_broadcast([P, D])).then_inc(s_ln1, 16)
            sp.dma_start(rows[:, D:], d["ln1_b"].to_broadcast([P, D])).then_inc(s_ln1, 16)
            sp.wait_ge(pa_filled, KC)
            sp.dma_start(wsh_d, d["w_sh_down"].rearrange("(j p) n -> p j n", p=P)).then_inc(s_wsh, 16)
            sp.wait_ge(m_ready, KC)
            sp.wait_ge(x1_stored, 16 * NT)
            for i in range(NT):
                sp.dma_start(x1_back[:, i, :], d["x1_dram"][i * P:(i + 1) * P, :]).then_inc(s_x[i], 16)
            sp.dma_start(hw[:, 0:D], d["ln2_g"].to_broadcast([P, D])).then_inc(s_ln2, 16)
            sp.dma_start(hw[:, D:2 * D], d["ln2_b"].to_broadcast([P, D])).then_inc(s_ln2, 16)
            sp.dma_start(bias[:, :], d["router_bias"].to_broadcast([P, E])).then_inc(s_ln2, 16)
            for i in range(NT):
                sp.wait_ge(x2_ready, i + 1)
                sp.dma_start(d["x2_dram"][i * P:(i + 1) * P, :], x2[:, i, :]).then_inc(x2_stored, 16)
            sp.wait_ge(of_filled, NT)
            sp.dma_start(wr_sb, d["w_router"].rearrange("(p c) n -> p c n", c=KC)).then_inc(s_wr, 16)

            wg_d = d["w_e_gate"].rearrange("e (p c) n -> e p c n", c=KC)
            wu_d = d["w_e_up"].rearrange("e (p c) n -> e p c n", c=KC)
            wd_d = d["w_e_down"].rearrange("e (j p) n -> e p j n", p=P)

            def load_expert(b, n, first=False):
                e = sp.value_load(blki[0:1, bass.ds(b, 1)], min_val=0, max_val=E - 1)
                if not first:
                    sp.wait_ge(gu_filled, b - 1)
                for src, dst in ((wg_d, wg[n]), (wu_d, wu[n])):
                    sp.dma_start(dst, src[bass.ds(e, 1), :, :, :].rearrange("e p c n -> (e p) c n")).then_inc(s_wgu[n], 16)
                if not first:
                    sp.wait_ge(y_filled, b - 1)
                sp.dma_start(wd[n], wd_d[bass.ds(e, 1), :, :, :].rearrange("e p j n -> (e p) j n")).then_inc(s_wd[n], 16)

            sp.wait_ge(blki_ready, 1)
            load_expert(0, 0, True)
            sp.wait_ge(sh_gu, NT)
            load_expert(1, 1, True)
            sp.wait_ge(tb_ready, 1)
            pairs = sp.value_load(nbi[0:1, 0:1], min_val=MIN_BLOCKS // 2, max_val=NBMAX // 2)
            gathers = sp.value_load(nbi[0:1, 3:4], min_val=8 * MIN_BLOCKS, max_val=8 * NBMAX + 16)
            with sp.Fori(1, pairs) as r:
                load_expert(r * 2, 0)
                load_expert(r * 2 + 1, 1)
            sp.wait_ge(y_stored[0], pairs * 16)
            sp.wait_ge(y_stored[1], pairs * 16)
            sp.wait_ge(xg_loaded[1], gathers)
            yb = d["y_dram"].rearrange("(t k) n -> t k n", k=KSTRIDE)
            for i in range(NT):
                if i >= 3:
                    sp.wait_ge(sum_filled, i - 2)
                    sp.wait_ge(yb_used, i - 2)
                for m in range(2):
                    three = slice(3 * m, 3 * m + 3)
                    sp.dma_start(land[i % 3][:, three, :], yb[i * P:(i + 1) * P, three, :]).then_inc(s_yb[i % 3][m], 16)
            for i in range(NT):
                sp.wait_ge(out_ready, i + 1)
                dst = d["y_prompt"][i * P:(i + 1) * P, :] if i < NTP else \
                    d["y_sample"][(i - NTP) * P:(i - NTP + 1) * P, :]
                sp.dma_start(dst, acc[:, i, :]).then_inc(out_stored, 16)
            sp.wait_ge(out_stored, 16 * NT)

        @block.tensor
        def _(pe):
            mm, tr = nc.tensor.matmul, nc.tensor.transpose

            pe.wait_ge(s_con, 16)

            def x1_transposed(i):
                pe.wait_ge(x1_ready, i + 1)
                if i >= 2:
                    pe.wait_ge(t_evicted, i - 1)
                for c in range(KC):
                    last = tr(pair[i % 2][:, c * P:(c + 1) * P], x_in[:, i, c:D:KC], ident)
                last.then_inc(t_filled, 1)

            x1_transposed(0)
            for n in range(5):
                pe.wait_ge(s_strip[n % 2], 16 * (n // 2 + 1))
                for i in range(NT):
                    fill = n * NT + i
                    if n == 0:
                        if i < NT - 1:
                            x1_transposed(i + 1)
                        pe.wait_ge(t_evicted, i + 1)
                    if fill >= NT:
                        pe.wait_ge(g_evicted, fill - 1)
                    elif fill >= 4:
                        pe.wait_ge(g_evicted, fill - 3)
                    for c in range(KC):
                        last = mm(big_bank(fill), x1T[:, c, i * P:(i + 1) * P],
                                  strip[n % 2][:, c, :], start=(c == 0), stop=(c == KC - 1))
                    last.then_inc(g_filled, 1)
                if n == 1:
                    pe.wait_ge(s_misc, 64)
                    tr(pX[:, 0:4 * H], lbraw[0:4 * H, :], ident[0:4 * H, 0:4 * H]).then_inc(lb_filled, 1)
                    for g in range(AG):
                        last = tr(pA[:, g * P:(g + 1) * P], ws_sb[:, g, :], ident)
                    last.then_inc(ws_filled, 1)
            pe.wait_ge(ws_evicted, 1)
            pe.wait_ge(v_normed, 1)
            for g in range(AG):
                if g >= 2:
                    pe.wait_ge(a_ready, g - 1)
                mm(pB[:, (g % 2) * 512:(g % 2) * 512 + NT * AGD], wsT[:, g, :],
                   vn_tok[:, :, g * AGD:(g + 1) * AGD], start=True, stop=True).then_inc(mix_filled, 1)

            def head_products(nxt, first, end):
                for y in range(first, end):
                    x, c = y // KC, y % KC
                    m, n = x // 2, x % 2
                    if c == 0:
                        if n == 0:
                            pe.wait_ge(s_hw[m], nxt * 16 + 16)
                        pe.wait_ge(g_evicted, nxt * 6 + (PRE + x - 1))
                    last = mm(pg[:, n * 512:n * 512 + HALF], hw3[m][:, c, :], x1T[:, c, n * HALF:(n + 1) * HALF],
                              start=(c == 0), stop=(c == KC - 1))
                    if c == KC - 1:
                        last.then_inc(g_filled, 1)

            def g_products(first, end):
                for y in range(first, end):
                    i, c = y // KC, y % KC
                    if c == 0:
                        if i == 0:
                            pe.wait_ge(s_gstrip, 32)
                        pe.wait_ge(g_evicted, PRE + 6 * H + i - 1)
                    last = mm(pg[:, (i % 2) * 512:(i % 2) * 512 + 512], x1T[:, c, i * P:(i + 1) * P],
                              g_strip[c // 4][:, c % 4, :], start=(c == 0), stop=(c == KC - 1))
                    if c == KC - 1:
                        last.then_inc(g_filled, 1)

            head_products(0, 0, PARTS)
            pe.wait_ge(a_ready, AG)
            for i in range(NT):
                if i >= 2:
                    pe.wait_ge(t_evicted, NT + i - 1)
                for c in range(4):
                    last = tr(pair[i % 2][:, c * P:(c + 1) * P], u_tok[:, i, c:AW:4], ident)
                last.then_inc(t_filled, 1)
            pe.wait_ge(t_evicted, 2 * NT)

            def recurrence(h, products, first=False):
                def start(step):
                    if step == 0:
                        if not first:
                            pe.wait_ge(o_evicted, h)
                    elif 2 <= step < 10:
                        pe.wait_ge(hg_used, h * USES + (step - 1))
                    return pair[step % 2]

                def diag():
                    buf = start(0)
                    pe.wait_ge(diag_ready, h + 1)
                    for n in range(2):
                        last = mm(buf[:, n * 512:n * 512 + HALF], ones,
                                  hv("prod")[:, n * HALF:(n + 1) * HALF], start=True, stop=True)
                    last.then_inc(hg_filled, 1)

                def level(j):
                    buf = start(j + 1)
                    pe.wait_ge(lvl_ready, h * LEVELS + (j + 1))
                    kt = hv(f"K{j % 2}")
                    qt = hv(f"Q{j % 2}")
                    for i in range(NT):
                        o = (i // 3) * 512 + (i % 3) * P
                        last = mm(buf[:, o:o + P], kt[:, i * P:(i + 1) * P], qt[:, i * P:(i + 1) * P],
                                  start=True, stop=True)
                    last.then_inc(hg_filled, 1)

                def k_transposed():
                    buf = start(8)
                    pe.wait_ge(ke_ready, 2 * h + 1)
                    for s in range(8):
                        i = FWD_TILES[s] if s < 4 else BWD_TILES[s - 4]
                        o = (s // 4) * T + i * P
                        last = tr(buf[:, s * P:(s + 1) * P], hv("S", 2)[:, o:o + P], ident)
                    last.then_inc(hg_filled, 1)

                def increments():
                    buf = start(9)
                    pe.wait_ge(ke_evicted, h + 1)
                    for s in range(8):
                        i = FWD_TILES[s] if s < 4 else BWD_TILES[s - 4]
                        last = mm(buf[:, s * P:(s + 1) * P], keT[:, s, :], v_tok[:, i, bass.ds(h * DK, DK)],
                                  start=True, stop=True)
                    last.then_inc(hg_filled, 1)

                def outputs():
                    buf = start(10)
                    pe.wait_ge(ke_ready, 2 * h + 2)
                    pe.wait_ge(st_ready, h + 1)
                    qe = hv("k", 2)
                    for i in range(NT):
                        o = (i // 3) * 512 + (i % 3) * P
                        terms = [(hv("AT")[:, i * P:(i + 1) * P], v_tok[:, i, bass.ds(h * DK, DK)])]
                        if i not in (0, NTP):
                            s = FWD_TILES.index(i - 1)
                            terms.append((qe[:, i * P:(i + 1) * P], states[:, s, :]))
                        if i not in (NTP - 1, NT - 1):
                            s = 4 + BWD_TILES.index(i + 1)
                            terms.append((qe[:, T + i * P:T + (i + 1) * P], states[:, s, :]))
                        for n, (a, b) in enumerate(terms):
                            last = mm(buf[:, o:o + P], a, b, start=(n == 0), stop=(n == len(terms) - 1))
                    last.then_inc(hg_filled, 1)

                products(0, 10)
                diag()
                level(0)
                products(10, 14)
                for j in range(1, LEVELS):
                    level(j)
                    products(9 + 5 * j, 14 + 5 * j)
                k_transposed()
                products(44, PARTS)
                increments()
                outputs()

            recurrence(0, lambda first, end: head_products(1, first, end), True)
            with pe.Fori(1, H - 1) as h:
                recurrence(h, lambda first, end: head_products(h + 1, first, end))
            recurrence(H - 1, g_products)

            def gate_products(f):
                for m in range(2):
                    pe.wait_ge(s_hw[m], 16 * H + 16 + f * 16)
                    for n in range(2):
                        x = 2 * m + n
                        pe.wait_ge(g_evicted, f * 4 + (POST + x - 1))
                        for c in range(KC):
                            last = mm(pg[:, n * 512:n * 512 + HALF], hw3[m][:, c, :],
                                      x1T[:, c, n * HALF:(n + 1) * HALF], start=(c == 0), stop=(c == KC - 1))
                        last.then_inc(g_filled, 1)

            with pe.Fori(0, KC) as f:
                gate_products(f)
            pe.wait_ge(o_evicted, H)
            for i in range(NT):
                pe.wait_ge(r_done, i + 1)
                if i >= 2:
                    pe.wait_ge(rt_evicted, i - 1)
                for c in range(KC):
                    last = tr(pair[i % 2][:, c * P:(c + 1) * P], o_tok[:, i, c:D:KC], ident)
                last.then_inc(rt_filled, 1)
            pe.wait_ge(rt_evicted, NT)
            def projections(f, first=False):
                pe.wait_ge(s_pa, f * 16 + 16)
                if not first:
                    pe.wait_ge(pa_taken, f)
                for n in range(2):
                    for c in range(4):
                        last = mm(pA[:, n * 512:n * 512 + HALF], hw3[0][:, c, :], aT[:, c, n * HALF:(n + 1) * HALF],
                                  start=(c == 0), stop=(c == 3))
                last.then_inc(pa_filled, 1)
                pe.wait_ge(s_pb, f * 16 + 16)
                if not first:
                    pe.wait_ge(pb_taken, f)
                for n in range(2):
                    for c in range(KC):
                        last = mm(pB[:, n * 512:n * 512 + HALF], hw3[1][:, c, :], rT[:, c, n * HALF:(n + 1) * HALF],
                                  start=(c == 0), stop=(c == KC - 1))
                last.then_inc(pb_filled, 1)

            projections(0, True)
            with pe.Fori(1, KC) as f:
                projections(f)
            pe.wait_ge(m_ready, KC)
            pe.wait_ge(s_wo, 16)

            def x2_transposed(i):
                pe.wait_ge(x2_ready, i + 1)
                if i >= 1:
                    pe.wait_ge(x2t_evicted, i)
                for c in range(KC):
                    last = tr(pg[:, c * P:(c + 1) * P], x2[:, i, c:D:KC], ident)
                last.then_inc(x2t_filled, 1)

            pe.wait_ge(g_evicted, POST + 4 * KC)
            for i in range(NT):
                if i >= 2:
                    pe.wait_ge(z_taken, i - 1)
                for n in range(2):
                    for c in range(KC):
                        last = mm(pair[i % 2][:, n * 512:(n + 1) * 512], mT[:, c, i * P:(i + 1) * P],
                                  wo_sb[:, c, n * 512:(n + 1) * 512], start=(c == 0), stop=(c == KC - 1))
                last.then_inc(of_filled, 1)
                if i >= 1:
                    x2_transposed(i - 1)

            def shared_up(i):
                for c in range(KC):
                    last = mm(pX[:, 0:512], x2T[:, c, i * P:(i + 1) * P], wsh[:, c, :],
                              start=(c == 0), stop=(c == KC - 1))
                last.then_inc(sh_gu, 1)

            pe.wait_ge(s_wsh, 48)
            pe.wait_ge(x2t_evicted, 1)
            shared_up(0)
            x2_transposed(NT - 1)
            pe.wait_ge(s_wr, 16)
            pe.wait_ge(x2t_evicted, NT)
            pe.wait_ge(z_taken, NT)
            for n in range(2):
                for c in range(KC):
                    last = mm(pA[0:E, n * 512:n * 512 + HALF], wr_sb[:, c, :], x2T[:, c, n * HALF:(n + 1) * HALF],
                              start=(c == 0), stop=(c == KC - 1))
            last.then_inc(lg_filled, 1)

            def shared_turn(i):
                pe.wait_ge(sh_h, i + 1)
                if i >= 1:
                    pe.wait_ge(sh_hte, i)
                for j in range(2):
                    last = tr(pX[:, 512 + j * P:512 + (j + 1) * P], hid[:, j * P:(j + 1) * P], ident)
                last.then_inc(sh_ht, 1)

            def shared_down(i):
                pe.wait_ge(sh_hte, i + 1)
                if i >= 1:
                    pe.wait_ge(sh_acc, i)
                for n in range(2):
                    for j in range(2):
                        last = mm(pB[:, n * 512:(n + 1) * 512], hidT[:, j, :], wsh_d[:, j, n * 512:(n + 1) * 512],
                                  start=(j == 0), stop=(j == 1))
                last.then_inc(sh_y, 1)

            def positions():
                pe.wait_ge(sel_ready, 1)
                sel = slabs(select, NT)
                for i in range(NT):
                    for j in range(i + 1):
                        mm(pA[:, i * E:(i + 1) * E], tri if j == i else ones, sel[:, j, :],
                           start=(j == 0), stop=(j == i))
                for j in range(NT):
                    last = mm(pA[:, NT * E:(NT + 1) * E], ones, sel[:, j, :],
                              start=(j == 0), stop=(j == NT - 1))
                last.then_inc(pos_filled, 1)

            def slot_tables(first, end):
                for x in range(first, end):
                    pe.wait_ge(oh_ready, 2 * x + 2)
                    pe.wait_ge(ohp_ready, x + 1)
                    mm(pg[:, 0:2 * NCOL], oh_place(x), oh_block(x), start=(x == 0),
                       stop=(x == NT * TOPK - 1)).then_inc(oh_used, 1)

            pe.wait_ge(lg_evicted, 1)
            for i in range(NT):
                last = tr(pA[:, i * E:(i + 1) * E], lgT[0:E, i * P:(i + 1) * P], ident[0:E, 0:E])
            last.then_inc(lgt_filled, 1)
            shared_turn(0)
            for i in range(1, NT):
                shared_up(i)
                shared_down(i - 1)
                shared_turn(i)
                if i == 3:
                    positions()
                if i == 4:
                    pe.wait_ge(blk_ready, 1)
                    tr(pg[0:1, 512:512 + P], bexp[:, :], ident).then_inc(blk_filled, 1)
                    slot_tables(0, 4)
            slot_tables(4, 8)
            shared_down(NT - 1)
            slot_tables(8, NT * TOPK)

            pe.wait_ge(tb_ready, 1)
            pairs = pe.value_load(nbi[0:1, 0:1], min_val=MIN_BLOCKS // 2, max_val=NBMAX // 2)

            def gathered_turn(n, loads):
                pe.wait_ge(xg_loaded[n], loads * 16)
                for c in range(KC):
                    last = tr(pg[:, c * P:(c + 1) * P], xg[n][:, c:D:KC], ident)
                last.then_inc(xt_filled, 1)

            def up(b, n, r):
                pe.wait_ge(xt_ready, b + 1)
                pe.wait_ge(s_wgu[n], r * 32 + 32)
                for m, w in ((0, wg[n]), (1, wu[n])):
                    for j in range(2):
                        o = n * 512 + (2 * m + j) * P
                        for c in range(KC):
                            last = mm(pA[:, o:o + P], w[:, c, j * P:(j + 1) * P], xT[n][:, c, :],
                                      start=(c == 0), stop=(c == KC - 1))
                last.then_inc(gu_filled, 1)

            def down(b, n, r, first=False):
                pe.wait_ge(h_ready, b + 1)
                pe.wait_ge(s_wd[n], r * 16 + 16)
                if not first:
                    pe.wait_ge(y_ready, b - 1)
                for m in range(2):
                    for j in range(2):
                        last = mm(pairY[n][:, m * 512:(m + 1) * 512], hT[n][:, j, :],
                                  wd[n][:, j, m * 512:(m + 1) * 512], start=(j == 0), stop=(j == 1))
                last.then_inc(y_filled, 1)

            def expert_block(b, n, r, first=False):
                up(b, n, r)
                gathered_turn(1 - n, r + 1 + n)
                down(b, n, r, first)

            gathered_turn(0, 1)
            for n in range(2):
                expert_block(n, n, 0, True)
            with pe.Fori(1, pairs) as r:
                for n in range(2):
                    expert_block(r * 2 + n, n, r)
            for i in range(NT):
                pe.wait_ge(s_yb[i % 3][0], 16 * (i // 3 + 1))
                if i == 0:
                    pe.wait_ge(y_ready, pairs * 2)
                else:
                    pe.wait_ge(sum_taken, max(i - 1, 1))
                for k in range(TOPK - 1):
                    if k == 3:
                        pe.wait_ge(s_yb[i % 3][1], 16 * (i // 3 + 1))
                    for n in range(2):
                        last = mm(pairY[i % 2][:, n * 512:(n + 1) * 512], ident,
                                  land[i % 3][:, k, n * 512:(n + 1) * 512], start=(k == 0), stop=(k == TOPK - 2))
                last.then_inc(sum_filled, 1)

        @block.scalar
        def _(sc):
            fn = nc.scalar.activation

            def root(n, times):
                sc.wait_ge(var_ready, times)
                fn(std[:, 0:n], std[:, 0:n], ACT.Sqrt).then_inc(std_ready, 1)

            def x1_turned(i):
                root(1, i + 1)
                sc.wait_ge(t_filled, i + 1)
                fn(x1T[:, :, i * P:(i + 1) * P], slabs(pair[i % 2][:, :], KC), ACT.Copy).then_inc(t_evicted, 1)

            for i in range(NT):
                x1_turned(i)
            outs = ((u_tok, 0, ACT.Gelu_apprx_tanh), (vn_tok, 0, ACT.Gelu_apprx_tanh), (v_tok, 0, ACT.Copy),
                    (v_tok, 512, ACT.Copy), (g_tok, 0, ACT.Silu))
            for n, (dst, c0, func) in enumerate(outs):
                if n == 4:
                    sc.wait_ge(x1_stored, 16 * NT)
                for i in range(NT):
                    fill = n * NT + i
                    sc.wait_ge(g_filled, fill + 1)
                    fn(dst[:, i, c0:c0 + 512], big_bank(fill), func).then_inc(g_evicted, 1)
                if n == 1:
                    sc.wait_ge(lb_sub, 1)
                    fn(lbw[:, 2 * 4 * H:3 * 4 * H], lbw[:, 4 * H:2 * 4 * H], ACT.Exp).then_inc(lb_exp, 1)
                    sc.wait_ge(ws_filled, 1)
                    fn(wsT, slabs(pA[:, :], AG), ACT.Copy).then_inc(ws_evicted, 1)
                if n == 2:
                    root(NT, NT + 1)

            def head_gates(nxt, x):
                m, n = x // 2, x % 2
                sc.wait_ge(g_filled, nxt * 6 + (PRE + x + 1))
                dst = q_next if m == 0 else sig_next[:, (m - 1) * T:m * T]
                fn(dst[:, n * HALF:(n + 1) * HALF], pg[:, n * 512:n * 512 + HALF],
                   ACT.Silu if m == 0 else ACT.Sigmoid).then_inc(g_evicted, 1)

            for x in range(6):
                head_gates(0, x)
            for i in range(NT):
                sc.wait_ge(t_filled, NT + i + 1)
                fn(aT[:, :, i * P:(i + 1) * P], slabs(pair[i % 2][:, 0:4 * P], 4), ACT.Copy).then_inc(t_evicted, 1)
            def clear_suffixes():
                rounds = 2 * T // P
                fn(slabs(hv("S", 2), rounds), bass.AP(ones.tensor, ones.offset, [
                    list(ones.ap[0]), [0, rounds], [1, P]]), ACT.Copy).then_inc(s_cleared, 1)

            def second_g(i):
                sc.wait_ge(g_filled, PRE + 6 * H + i + 1)
                fn(g_tok[:, i, 512:D], pg[:, (i % 2) * 512:(i % 2) * 512 + 512], ACT.Silu).then_inc(g_evicted, 1)

            def head(h, evict, last=False):
                sc.wait_ge(cur_taken, h + 1)
                for x in range(5):
                    evict(x)
                sc.wait_ge(hg_filled, h * FILLS + 9)
                fn(keT, slabs(pair[0][:, :], 8), ACT.Copy).then_inc(ke_evicted, 1)
                if not last:
                    clear_suffixes()
                evict(5)
                sc.wait_ge(hg_filled, h * FILLS + 11)
                fn(o_tok[:, :, bass.ds(h * DK, DK)].rearrange("p (a b) k -> p a b k", a=2),
                   at(pair[0], 0, [[512, 2], [P, 3], [1, P]]), ACT.Copy).then_inc(o_evicted, 1)

            clear_suffixes()
            with sc.Fori(0, H - 1) as h:
                head(h, lambda x: head_gates(h + 1, x))
            head(H - 1, second_g, True)

            def merge_gates(f):
                for x in range(4):
                    n = x % 2
                    sc.wait_ge(g_filled, f * 4 + (POST + x + 1))
                    dst = sga if x < 2 else sgb
                    out = dst[:, bass.ds(f, 1), n * HALF:(n + 1) * HALF].rearrange("p a n -> p (a n)")
                    fn(out, pg[:, n * 512:n * 512 + HALF], ACT.Sigmoid).then_inc(g_evicted, 1)

            merge_gates(0)
            merge_gates(1)
            root(NT * H, NT + 2)
            with sc.Fori(2, KC) as f:
                merge_gates(f)
            for i in range(NT):
                sc.wait_ge(rt_filled, i + 1)
                fn(rT[:, :, i * P:(i + 1) * P], slabs(pair[i % 2][:, :], KC), ACT.Copy).then_inc(rt_evicted, 1)

            def x2_turned(i):
                sc.wait_ge(x2t_filled, i + 1)
                fn(x2T[:, :, i * P:(i + 1) * P], slabs(pg[:, :], KC), ACT.Copy).then_inc(x2t_evicted, 1)

            for i in range(NT):
                if i >= 1:
                    x2_turned(i - 1)
                root(1, NT + 3 + i)
            x2_turned(NT - 1)
            sc.wait_ge(lg_filled, 1)
            fn(lgT[0:E, :].rearrange("p (n t) -> p n t", n=2),
               slabs(pA[0:E, :], 2)[:, :, 0:HALF], ACT.Copy).then_inc(lg_evicted, 1)
            for i in range(NT):
                sc.wait_ge(sh_gu, i + 1)
                if i >= 1:
                    sc.wait_ge(sh_h, i)
                fn(silu_g[0], pX[:, 0:F], ACT.Silu).then_inc(sh_silu, 1)
                if i == 0:
                    sc.wait_ge(lgt_filled, 1)
                    fn(score, pA[:, 0:NT * E], ACT.Sigmoid).then_inc(sc_ready, 1)
                sc.wait_ge(sh_ht, i + 1)
                if i >= 1:
                    sc.wait_ge(sh_y, i)
                fn(hidT, slabs(pX[:, 512:512 + F], 2), ACT.Copy).then_inc(sh_hte, 1)

            sc.wait_ge(tb_ready, 1)
            pairs = sc.value_load(nbi[0:1, 0:1], min_val=MIN_BLOCKS // 2, max_val=NBMAX // 2)

            def gathered(b, n):
                sc.wait_ge(xt_filled, b + 1)
                fn(xT[n], slabs(pg[:, :], KC), ACT.Copy).then_inc(xt_ready, 1)

            def silu(b, n, first=False):
                sc.wait_ge(gu_filled, b + 1)
                if not first:
                    sc.wait_ge(h_ready, b - 1)
                fn(silu_g[n], pA[:, n * 512:n * 512 + F], ACT.Silu).then_inc(silu_ready, 1)

            def weighted(b, n, stores):
                sc.wait_ge(y_filled, b + 1)
                sc.wait_ge(gc_ready, b + 1)
                if stores is not None:
                    sc.wait_ge(y_stored[n], stores * 16)
                fn(yrow[n], pairY[n][:, :], ACT.Copy, scale=gcol[n]).then_inc(y_ready, 1)

            gathered(0, 0)
            silu(0, 0, True)
            gathered(1, 1)
            weighted(0, 0, None)
            silu(1, 1, True)
            gathered(2, 0)
            weighted(1, 1, None)
            with sc.Fori(1, pairs) as r:
                silu(r * 2, 0)
                gathered(r * 2 + 1, 1)
                weighted(r * 2, 0, r)
                silu(r * 2 + 1, 1)
                gathered(r * 2 + 2, 0)
                weighted(r * 2 + 1, 1, r)
            for i in range(NT):
                root(1, 2 * NT + 3 + i)

        @block.vector
        def _(ve):
            v = nc.vector
            chain = Chain(ve, dve)
            link = chain.link
            asked = [0]

            def rooted(n):
                asked[0] += 1
                ve.wait_ge(std_ready, asked[0])
                link(v.reciprocal(rstd[:, 0:n], std[:, 0:n]))

            def statistics(x, i, width):
                parts = width // 512
                for n in range(parts):
                    link(v.bn_stats(bst[:, 12 * i + 6 * n:12 * i + 6 * n + 6], x[:, n * 512:(n + 1) * 512]))
                link(v.bn_aggr(mv[:, 2 * i:2 * i + 2], bst[:, 12 * i:12 * i + 6 * parts]))

            def normalised(x, i, r, gain, offset, out=None):
                link(v.tensor_scalar(x, x, mv[:, 2 * i:2 * i + 1], rstd[:, r:r + 1], ALU.subtract, ALU.mult))
                link(v.tensor_tensor(x, x, gain, ALU.mult))
                return v.tensor_tensor(x if out is None else out, x, offset, ALU.add)

            def variances(n):
                v.tensor_scalar(std[:, 0:n], mv[:, 1:2 * n:2], LN_EPS, None, ALU.add).then_inc(var_ready, 1)

            for i in range(NT):
                ve.wait_ge(s_x[i], 16)
                statistics(x_in[:, i, :], i, D)
                v.tensor_scalar(std[:, 0:1], mv[:, 2 * i + 1:2 * i + 2], LN_EPS, None, ALU.add).then_inc(var_ready, 1)
                rooted(1)
                if i == 0:
                    ve.wait_ge(s_rows, 32)
                normalised(x_in[:, i, :], i, 0, rows[:, 0:D], rows[:, D:]).then_inc(x1_ready, 1)
            ve.wait_ge(lb_filled, 1)
            n1 = 4 * H
            link(v.tensor_copy(lbw[:, 0:n1], pX[:, 0:n1]))

            def layer(o, l):
                return lbw[:, o:o + n1].rearrange("p (a l h) -> p a l h", a=2, l=2)[:, :, l, :]

            two = lambda ap: ap.rearrange("p (a h) -> p a h", a=2)
            link(v.tensor_tensor(two(lbs[:, :]), layer(0, 0), layer(0, 1), ALU.max))
            for l in range(2):
                last = v.tensor_tensor(layer(n1, l), layer(0, l), two(lbs[:, :]), ALU.subtract)
                if l == 0:
                    link(last)
            last.then_inc(lb_sub, 1)
            ve.wait_ge(lb_exp, 1)
            link(v.tensor_tensor(two(lbs[:, :]), layer(2 * n1, 0), layer(2 * n1, 1), ALU.add))
            link(v.reciprocal(lbc[:, :], lbs[:, :]))
            link(v.tensor_tensor(two(lbs[:, :]), layer(2 * n1, 0), two(lbc[:, :]), ALU.mult))
            link(v.tensor_scalar(lbc[:, :], lbs[:, :], -1.0, 1.0, ALU.mult, ALU.add))
            ve.wait_ge(g_evicted, 2 * NT)
            for i in range(NT):
                statistics(vn_tok[:, i, :], i, AW)
            variances(NT)
            rooted(NT)
            ve.wait_ge(s_aln, 32)
            for i in range(NT):
                last = normalised(vn_tok[:, i, :], i, i, rows[:, 0:AW], rows[:, AW:2 * AW])
                if i < NT - 1:
                    link(last)
            last.then_inc(v_normed, 1)
            for g in range(AG):
                ve.wait_ge(mix_filled, g + 1)
                u_g = u_tok[:, :, g * AGD:(g + 1) * AGD]
                v.scalar_tensor_tensor(out=u_g, in0=slabs(pB[:, (g % 2) * 512:(g % 2) * 512 + NT * AGD], NT),
                                       scalar=sbt[:, g:g + 1], in1=u_g, op0=ALU.add, op1=ALU.mult).then_inc(a_ready, 1)
            def g_scaled(half):
                cols = slice(half * 512, half * 512 + 512)
                for i in range(NT):
                    link(v.tensor_tensor(g_tok[:, i, cols], g_tok[:, i, cols], nrow[:, cols], ALU.mult))

            ve.wait_ge(g_evicted, PRE)
            g_scaled(0)

            def both(name, half, fwd, bwd, n=T):
                return at(rEF, OFF[name] + fwd, [[T + bwd - fwd, 2], [2 * half, T // (2 * half)], [1, half]])

            def one(name, half, fwd, bwd):
                return at(rEF, OFF[name] + fwd, [[bwd - fwd, 2], [2 * half, T // (2 * half)], [1, half]])

            def total(half, fwd, bwd):
                return at(rEF, OFF["P"] + fwd, [[T + bwd - fwd, 2], [2 * half, T // (2 * half)], [0, half]])

            def masked_in(h, j):
                mask = con[:, K_MASK + j * P:K_MASK + (j + 1) * P].bitcast(I32)
                v.copy_predicated(at(rEF, OFF["AT"], [[HALF, 2], [P, 3], [1, P]]),
                                  bass.AP(mask.tensor, mask.offset, [list(mask.ap[0]), [0, 2], [0, 3], [1, P]]),
                                  at(pair[(j + 1) % 2], 0, [[512, 2], [P, 3], [1, P]])).then_inc(hg_used, 1)

            chain.restart()
            def gates_taken(h):
                ve.wait_ge(g_evicted, h * 6 + (PRE + 6))
                link(v.tensor_copy(hv("q"), q_next))
                for a in range(2):
                    last = v.tensor_scalar(hv("P", 2)[:, a * T:(a + 1) * T], sig_next[:, a * T:(a + 1) * T],
                                           lbc[:, bass.ds(h + a * H, 1)], lbs[:, bass.ds(h + a * H, 1)],
                                           ALU.mult, ALU.add)
                    if a == 0:
                        link(last)
                last.then_inc(cur_taken, 1)
                ve.wait_ge(cur_taken, h + 1)

            def diagonal(h, first=False):
                if not first:
                    ve.wait_ge(hg_filled, h * FILLS)
                link(v.tensor_scalar(hv("k", 2), hv("P", 2), -1.0, 1.0, ALU.mult, ALU.add))
                link(v.tensor_tensor(hv("prod"), hv("k", 2)[:, 0:T], hv("k", 2)[:, T:], ALU.add))
                v.tensor_tensor(hv("prod"), hv("prod"), hv("q"), ALU.mult).then_inc(diag_ready, 1)

            def head(h):
                for j in range(LEVELS):
                    half = 1 << j
                    link(v.tensor_tensor(one(f"Q{j % 2}", half, half, 0), one("q", half, half, 0),
                                         both("P", half, half, 0), ALU.mult))
                    if j == 0:
                        ve.wait_ge(s_cleared, h + 1)
                    v.tensor_tensor(one(f"K{j % 2}", half, 0, half), both("k", half, 0, half),
                                    both("S", half, 0, half), ALU.mult).then_inc(lvl_ready, 1)
                    link(v.tensor_tensor(both("S", half, 0, half), both("S", half, 0, half),
                                         total(half, 2 * half - 1, 0), ALU.mult))
                    if j > 0:
                        ve.wait_ge(hg_filled, h * FILLS + (j + 1))
                    link(v.tensor_tensor(both("P", half, half, 0), both("P", half, half, 0),
                                         total(half, half - 1, half), ALU.mult))
                    if j == 0:
                        ve.wait_ge(hg_filled, h * FILLS + 1)
                        eye = bass.AP(ident.tensor, ident.offset, [list(ident.ap[0]), [0, 2], [0, 3], [1, P]])
                        v.tensor_tensor(at(rEF, OFF["AT"], [[HALF, 2], [P, 3], [1, P]]),
                                        at(pair[0], 0, [[512, 2], [P, 3], [1, P]]), eye, ALU.mult).then_inc(hg_used, 1)
                        ve.wait_ge(hg_used, h * USES + 1)
                    else:
                        masked_in(h, j - 1)
                        ve.wait_ge(hg_used, h * USES + (j + 1))
                v.tensor_tensor(hv("S", 2), hv("S", 2), hv("k", 2), ALU.mult).then_inc(ke_ready, 1)
                ve.wait_ge(ke_ready, h * 2 + 1)
                v.tensor_tensor(slabs(hv("k", 2), 2), at(rEF, OFF["q"], [[0, 2], [1, T]]),
                                slabs(hv("P", 2), 2), ALU.mult).then_inc(ke_ready, 1)
                ve.wait_ge(hg_filled, h * FILLS + (LEVELS + 1))
                link(v.memset(std[:, 0:1], 0.0))
                masked_in(h, LEVELS - 1)
                ve.wait_ge(hg_filled, h * FILLS + 10)
                corners = [[4 * P, 2], [3 * P, 2], [1, P]]
                link(v.tensor_copy(at(ew, 8 * P, corners), at(pair[1], 0, corners)))
                for s in (1, 2, 5, 6):
                    i = FWD_TILES[s] if s < 4 else BWD_TILES[s - 4]
                    edge = i * P + P - 1 if s < 4 else T + i * P
                    last = v.scalar_tensor_tensor(out=states[:, s, :], in0=states[:, s - 1, :],
                                                  scalar=hv("P", 2)[:, edge:edge + 1],
                                                  in1=pair[1][:, s * P:(s + 1) * P], op0=ALU.mult, op1=ALU.add)
                    if s < 6:
                        link(last)
                last.then_inc(st_ready, 1)
                ve.wait_ge(st_ready, h + 1)

            gates_taken(0)
            diagonal(0, True)
            chain.restart()
            with ve.Fori(0, H - 1) as h:
                head(h)
                gates_taken(h + 1)
                diagonal(h + 1)
                chain.restart()
            head(H - 1)
            ve.wait_ge(g_evicted, POST)
            g_scaled(1)
            ve.wait_ge(o_evicted, H)

            square = ew[:, 2 * D:3 * D]
            for i in range(NT):
                link(v.tensor_tensor(square, o_tok[:, i, :], o_tok[:, i, :], ALU.mult))
                link(v.tensor_reduce(std[:, i * H:(i + 1) * H], slabs(square, H), AX.X, ALU.add))
            v.tensor_scalar(std[:, 0:NT * H], std[:, 0:NT * H], 1.0 / DK, RMS_EPS, ALU.mult, ALU.add).then_inc(var_ready, 1)
            rooted(NT * H)
            for i in range(NT):
                link(v.tensor_tensor(slabs(o_tok[:, i, :], H), slabs(o_tok[:, i, :], H),
                                     at(rstd, i * H, [[1, H], [0, DK]]), ALU.mult))
                v.tensor_tensor(o_tok[:, i, :], o_tok[:, i, :], g_tok[:, i, :], ALU.mult).then_inc(r_done, 1)
            ve.wait_ge(g_evicted, POST + 4 * KC)
            chain.restart()
            with ve.Fori(0, KC) as f:
                ve.wait_ge(pa_filled, f + 1)
                gate_a = sga[:, bass.ds(f, 1), :].rearrange("p a (n t) -> p (a n) t", n=2)
                gate_b = sgb[:, bass.ds(f, 1), :].rearrange("p a (n t) -> p (a n) t", n=2)
                v.tensor_tensor(slabs(ew[:, 0:T], 2), slabs(pA[:, :], 2)[:, :, 0:HALF], gate_a, ALU.mult).then_inc(pa_taken, 1)
                ve.wait_ge(pb_filled, f + 1)
                v.tensor_tensor(slabs(ew[:, T:2 * T], 2), slabs(pB[:, :], 2)[:, :, 0:HALF], gate_b, ALU.mult).then_inc(pb_taken, 1)
                ve.wait_ge(pa_taken, f + 1)
                ve.wait_ge(pb_taken, f + 1)
                v.tensor_tensor(mT[:, bass.ds(f, 1), :].rearrange("p a t -> p (a t)"), ew[:, 0:T], ew[:, T:2 * T],
                                ALU.add).then_inc(m_ready, 1)
                ve.wait_ge(m_ready, f + 1)
            ve.wait_ge(s_ln1, 32)
            for i in range(NT):
                ve.wait_ge(of_filled, i + 1)
                ve.wait_ge(s_x[i], 32)
                v.scalar_tensor_tensor(out=x2[:, i, :], in0=x1_back[:, i, :], scalar=ALPHA, in1=pair[i % 2][:, :],
                                       op0=ALU.mult, op1=ALU.add).then_inc(z_taken, 1)
                ve.wait_ge(z_taken, i + 1)
                statistics(x2[:, i, :], 0, D)
                variances(1)
                rooted(1)
                normalised(x2[:, i, :], 0, 0, rows[:, 0:D], rows[:, D:]).then_inc(x2_ready, 1)

            def shared_hidden(i):
                ve.wait_ge(sh_silu, i + 1)
                if i >= 1:
                    ve.wait_ge(sh_ht, i)
                v.tensor_tensor(hid, silu_g[0], pX[:, F:2 * F], ALU.mult).then_inc(sh_h, 1)

            def shared_added(i):
                ve.wait_ge(sh_y, i + 1)
                v.scalar_tensor_tensor(out=acc[:, i, :], in0=x2[:, i, :], scalar=ALPHA, in1=pB[:, :],
                                       op0=ALU.mult, op1=ALU.add).then_inc(sh_acc, 1)

            def v3(ap, b, c):
                return ap.rearrange("p (a b c) -> p a b c", b=b, c=c)

            def per(region_view, dims):
                return bass.AP(region_view.tensor, region_view.offset, [list(region_view.ap[0])] + dims)

            def group_scores():
                ve.wait_ge(sc_ready, 1)
                ve.wait_ge(s_ln2, 48)
                link(v.tensor_tensor(slabs(biased, NT), slabs(score, NT), per(bias[:, :], [[0, NT], [1, E]]), ALU.add))
                link(v.tensor_reduce(best, slabs(biased, NT * EG), AX.X, ALU.max))
                spread = lambda ap: per(ap, [[1, NT * EG], [0, E // EG]])
                link(v.tensor_tensor(slabs(allowed, NT * EG), slabs(biased, NT * EG), spread(best), ALU.is_equal))
                link(v.tensor_reduce(gcnt, slabs(allowed, NT * EG), AX.X, ALU.add))
                link(v.scalar_tensor_tensor(out=allowed, in0=allowed, scalar=-BIG, in1=biased, op0=ALU.mult, op1=ALU.add))
                link(v.tensor_reduce(second, slabs(allowed, NT * EG), AX.X, ALU.max))
                link(v.tensor_scalar(gcnt, gcnt, 2.0, 1.0, ALU.is_ge, ALU.subtract))
                link(v.scalar_tensor_tensor(out=gcnt, in0=gcnt, scalar=BIG, in1=best, op0=ALU.mult, op1=ALU.add))
                link(v.tensor_tensor(second, second, gcnt, ALU.max))
                link(v.tensor_tensor(gsum, best, second, ALU.add))

            def group_choice():
                for i in range(NT):
                    o = slice(8 * i, 8 * i + 8)
                    link(v.max(out=gtop[:, o], in_=gsum[:, o]))
                    link(v.max_index(out=gidx[:, o].bitcast(U32), in_max=gtop[:, o], in_values=gsum[:, o]))
                link(v.tensor_copy(gidxf, gidx.bitcast(U32)))
                link(v.tensor_tensor(v3(work[:, 0:NT * EG * TOPG], EG, TOPG), per(iota, [[0, NT], [1, EG], [0, TOPG]]),
                                     per(gidxf, [[8, NT], [0, EG], [1, TOPG]]), ALU.is_equal))
                link(v.tensor_reduce(gmask, slabs(work[:, 0:NT * EG * TOPG], NT * EG), AX.X, ALU.add))
                link(v.tensor_scalar(gmask, gmask, 1.0, BIG, ALU.subtract, ALU.mult))
                link(v.tensor_tensor(slabs(allowed, NT * EG), slabs(biased, NT * EG),
                                     per(gmask, [[1, NT * EG], [0, E // EG]]), ALU.add))

            def expert_choice():
                for i in range(NT):
                    o = slice(8 * i, 8 * i + 8)
                    link(v.max(out=etop[:, o], in_=allowed[:, i * E:(i + 1) * E]))
                    link(v.max_index(out=eidx[:, o].bitcast(U32), in_max=etop[:, o], in_values=allowed[:, i * E:(i + 1) * E]))
                link(v.tensor_copy(eidxf, eidx.bitcast(U32)))
                link(v.tensor_tensor(v3(onehot, TOPK, E), per(iota, [[0, NT], [0, TOPK], [1, E]]),
                                     per(eidxf, [[8, NT], [1, TOPK], [0, E]]), ALU.is_equal))
                v.tensor_reduce(select, per(onehot, [[TOPK * E, NT], [1, E], [E, TOPK]]), AX.X,
                                ALU.add).then_inc(sel_ready, 1)

            def expert_gates():
                link(v.tensor_tensor(v3(work, TOPK, E), v3(onehot, TOPK, E),
                                     per(score, [[E, NT], [0, TOPK], [1, E]]), ALU.mult))
                link(v.tensor_reduce(gatew, slabs(work, NK), AX.X, ALU.add))
                link(v.tensor_reduce(wsum, slabs(gatew, NT), AX.X, ALU.add))
                link(v.reciprocal(wsum, wsum))
                link(v.scalar_tensor_tensor(out=slabs(gate, NT), in0=slabs(gatew, NT), scalar=SCALE,
                                            in1=per(wsum, [[1, NT], [0, TOPK]]), op0=ALU.mult, op1=ALU.mult))

            def slots():
                ve.wait_ge(pos_filled, 1)
                cnt = pA[:, NT * E:(NT + 1) * E]
                link(v.tensor_scalar(nblk, cnt, 0.0, None, ALU.is_gt))
                for b in range(1, NT):
                    link(v.scalar_tensor_tensor(out=nblk, in0=cnt, scalar=float(P * b), in1=nblk, op0=ALU.is_gt, op1=ALU.add))
                link(v.tensor_tensor_scan(incl, ones[:, 0:E], nblk, 0.0, ALU.mult, ALU.add))
                link(v.tensor_tensor(base, incl, nblk, ALU.subtract))
                link(v.scalar_tensor_tensor(out=slabs(posd, NT), in0=per(base, [[0, NT], [1, E]]), scalar=float(P),
                                            in1=slabs(pA[:, 0:NT * E], NT), op0=ALU.mult, op1=ALU.add))
                link(v.tensor_scalar(work[:, 0:E], incl, con[:, K_IOTAP:K_IOTAP + 1], None, ALU.is_le))
                link(v.tensor_reduce(bexp[:, :], work[:, 0:E], AX.X, ALU.add))
                v.tensor_scalar(bexp[:, :], bexp[:, :], float(E - 1), None, ALU.min).then_inc(blk_ready, 1)
                link(v.tensor_scalar(nbi[0:1, 2:3], incl[0:1, E - 1:E], 1.0, None, ALU.add))
                link(v.tensor_scalar(nbi[0:1, 0:1], nbi[0:1, 2:3], 1, None, ALU.logical_shift_right))
                link(v.tensor_scalar(nbi[0:1, 1:2], nbi[0:1, 0:1], 2.0, -1.0, ALU.mult, ALU.add))
                link(v.tensor_scalar(nbi[0:1, 3:4], nbi[0:1, 0:1], 16.0, 16.0, ALU.mult, ALU.add))
                link(v.tensor_tensor(v3(work, TOPK, E), v3(onehot, TOPK, E),
                                     per(posd, [[E, NT], [0, TOPK], [1, E]]), ALU.mult))
                link(v.tensor_reduce(slot, slabs(work, NK), AX.X, ALU.add))
                link(v.tensor_copy(slotl.bitcast(I32), slot))
                link(v.tensor_scalar(sloth.bitcast(I32), slotl.bitcast(I32), 7, None, ALU.logical_shift_right))
                link(v.tensor_scalar(slotl.bitcast(I32), slotl.bitcast(I32), P - 1, None, ALU.bitwise_and))
                v.tensor_copy(low, slotl.bitcast(I32)).then_inc(low_ready, 1)
                link(v.tensor_copy(high, sloth.bitcast(I32)))

            def slot_onehots(x):
                if x >= 4:
                    ve.wait_ge(oh_used, x - 3)
                blocks = iota[:, 0:NCOL]
                v.tensor_scalar(oh_block(x)[:, 0:NCOL], blocks, high[:, x:x + 1],
                                con[:, K_DST + x:K_DST + x + 1], ALU.is_equal, ALU.mult).then_inc(oh_ready, 1)
                v.tensor_scalar(oh_block(x)[:, NCOL:], blocks, high[:, x:x + 1], gate[:, x:x + 1],
                                ALU.is_equal, ALU.mult).then_inc(oh_ready, 1)

            shared_hidden(0)
            group_scores()
            group_choice()
            shared_hidden(1)
            shared_added(0)
            expert_choice()
            shared_hidden(2)
            shared_added(1)
            expert_gates()
            shared_hidden(3)
            shared_added(2)
            slots()
            shared_hidden(4)
            shared_added(3)
            ve.wait_ge(blk_filled, 1)
            v.tensor_copy(blki[0:1, 0:P], pg[0:1, 512:512 + P]).then_inc(blki_ready, 1)
            for x in range(NK):
                if x == 4:
                    shared_hidden(5)
                    shared_added(4)
                if x == 12:
                    shared_added(5)
                slot_onehots(x)
            ve.wait_ge(oh_used, NK)
            link(v.tensor_copy(tblg[:, 0:NCOL], pg[:, NCOL:2 * NCOL]))
            link(v.tensor_scalar(tbld[:, 0:NCOL], pg[:, 0:NCOL], 0.5, float(NOWHERE), ALU.is_lt, ALU.mult))
            link(v.scalar_tensor_tensor(out=tbld[:, 0:NCOL], in0=pg[:, 0:NCOL], scalar=-1.0, in1=tbld[:, 0:NCOL],
                                        op0=ALU.add, op1=ALU.add))
            link(v.tensor_copy(tbldi[:, 0:NCOL], tbld[:, 0:NCOL]))
            v.tensor_scalar(tblti[:, 0:NCOL], tbldi[:, 0:NCOL], 3, None, ALU.logical_shift_right).then_inc(tb_ready, 1)

            ve.wait_ge(tb_ready, 1)
            pairs = ve.value_load(nbi[0:1, 0:1], min_val=MIN_BLOCKS // 2, max_val=NBMAX // 2)

            def hidden(b, n, first=False):
                ve.wait_ge(silu_ready, b + 1)
                if not first:
                    ve.wait_ge(y_filled, b - 1)
                v.tensor_tensor(hT[n], slabs(silu_g[n], 2), slabs(pA[:, n * 512 + F:n * 512 + 2 * F], 2),
                                ALU.mult).then_inc(h_ready, 1)

            def gate_column(b, n, first=False):
                if not first:
                    ve.wait_ge(y_ready, b - 1)
                v.tensor_copy(gcol[n], tblg[:, bass.ds(b, 1)]).then_inc(gc_ready, 1)

            for n in range(2):
                hidden(n, n, True)
                gate_column(n, n, True)
            with ve.Fori(1, pairs) as r:
                for n in range(2):
                    hidden(r * 2 + n, n)
                    gate_column(r * 2 + n, n)
            for i in range(NT):
                ve.wait_ge(s_yb[i % 3][1], 16 * (i // 3 + 1))
                v.tensor_tensor(acc[:, i, :], acc[:, i, :], land[i % 3][:, TOPK - 1, :], ALU.add).then_inc(yb_used, 1)
                ve.wait_ge(yb_used, i + 1)
                ve.wait_ge(sum_filled, i + 1)
                v.tensor_tensor(acc[:, i, :], acc[:, i, :], pairY[i % 2][:, :], ALU.add).then_inc(sum_taken, 1)
                ve.wait_ge(sum_taken, i + 1)
                statistics(acc[:, i, :], 0, D)
                variances(1)
                rooted(1)
                normalised(acc[:, i, :], 0, 0, hw[:, 0:D], hw[:, D:2 * D]).then_inc(out_ready, 1)

        @block.gpsimd
        def _(po):
            g = nc.gpsimd

            po.wait_ge(of_filled, NT)
            g.memset(xg[0], 0.0).then_inc(xg_clear, 1)
            po.wait_ge(x2_stored, 16 * NT)
            po.wait_ge(low_ready, 1)
            for x in range(NT * TOPK):
                if x >= 4:
                    po.wait_ge(oh_used, x - 3)
                g.tensor_scalar(oh_place(x), iota, low[:, x:x + 1], None, ALU.is_equal).then_inc(ohp_ready, 1)
            po.wait_ge(sh_acc, NT)
            g.memset(xg[1], 0.0).then_inc(xg_clear, 1)
            po.wait_ge(xg_clear, 2)
            po.wait_ge(tb_ready, 1)
            pairs = po.value_load(nbi[0:1, 0:1], min_val=MIN_BLOCKS // 2, max_val=NBMAX // 2)
            last_block = po.value_load(nbi[0:1, 1:2], min_val=MIN_BLOCKS - 1, max_val=NBMAX - 1)

            def gather(b, n, chain, first=False):
                if not first:
                    po.wait_ge(xt_filled, b - 1)
                chain.link(g.tensor_copy(tokcol[n], tblti[:, bass.ds(b, 1)]))
                g.indirect_dma_start(xg[n], None, d["x2_dram"], bass.IndirectOffsetOnAxis(tokcol[n], 0),
                                     bounds_check=T - 1, oob_is_err=False).then_inc(xg_loaded[n], 16)

            def scatter(b, n, chain):
                po.wait_ge(y_ready, b + 1)
                chain.link(g.tensor_copy(dstcol[n], tbldi[:, bass.ds(b, 1)]))
                g.indirect_dma_start(d["y_dram"], bass.IndirectOffsetOnAxis(dstcol[n], 0), yrow[n], None,
                                     bounds_check=T * KSTRIDE - 1, oob_is_err=False).then_inc(y_stored[n], 16)

            chain = Chain(po, pool)
            gather(0, 0, chain, True)
            gather(1, 1, chain, True)
            gather(2, 0, chain)
            gather(3, 1, chain)
            scatter(0, 0, chain)
            chain.restart()
            with po.Fori(1, pairs) as r:
                gather(r * 2 + 2, 0, chain)
                scatter(r * 2 - 1, 1, chain)
                gather(r * 2 + 3, 1, chain)
                scatter(r * 2, 0, chain)
                chain.restart()
            scatter(last_block, 1, chain)
            for n in range(2):
                po.wait_ge(xg_loaded[n], pairs * 16 + 16)


_INS = ("x_prompt", "x_sample", "ln_in_g", "ln_in_b", "w_in", "a_ln_g", "a_ln_b", "a_ws", "a_sb",
        "hg_lb_logits", "hg_norm_g", "w_pa", "w_pb", "w_o", "ln1_g", "ln1_b", "w_router", "router_bias",
        "w_e_gate", "w_e_up", "w_e_down", "w_sh_gate", "w_sh_up", "w_sh_down", "ln2_g", "ln2_b")
_ROWS = {"ln_in_g", "ln_in_b", "a_ln_g", "a_ln_b", "hg_norm_g", "ln1_g", "ln1_b", "router_bias", "ln2_g", "ln2_b"}


def kernel(**inputs):
    import concourse.bacc as bacc
    from concourse.bass_utils import run_bass_kernel_spmd

    nc = bacc.Bacc("TRN2", target_bir_lowering=False, num_devices=1)
    arrays, d = {}, {}
    for name in _INS:
        a = np.ascontiguousarray(inputs[name])
        if name in _ROWS:
            a = a.reshape(1, -1)
        elif name != "hg_lb_logits":
            a = a.reshape(a.shape[1:])
        arrays[name] = a
    arrays["consts"] = constants()
    for name, a in arrays.items():
        d[name] = nc.dram_tensor(name, a.shape, mybir.dt.from_np(a.dtype), kind="ExternalInput").ap()
    d["y_prompt"] = nc.dram_tensor("y_prompt", (SEQ, D), F32, kind="ExternalOutput").ap()
    d["y_sample"] = nc.dram_tensor("y_sample", (DEC_SEQ, D), F32, kind="ExternalOutput").ap()
    d["x1_dram"] = nc.dram_tensor("x1_dram", (T, D), F32).ap()
    d["x2_dram"] = nc.dram_tensor("x2_dram", (T, D), F32).ap()
    d["y_dram"] = nc.dram_tensor("y_dram", (T * KSTRIDE, D), F32).ap()
    build(nc, d)
    r = run_bass_kernel_spmd(nc, [arrays], core_ids=[0]).results[0]
    return r["y_prompt"].reshape(1, SEQ, D), r["y_sample"].reshape(1, DEC_SEQ, D)
```

```python
from contextlib import ExitStack

import numpy as np

import concourse.bass as bass
import concourse.mybir as mybir

F32 = mybir.dt.float32
I32 = mybir.dt.int32
U32 = mybir.dt.uint32
ALU = mybir.AluOpType
ACT = mybir.ActivationFunctionType
AX = mybir.AxisListType

P = 128
D = 1024
SEQ, DEC_SEQ = 512, 256
T = SEQ + DEC_SEQ
NT = T // P
NTP = SEQ // P
KC = D // P
HALF = T // 2
AW = 512
AG = 8
AGD = AW // AG
H = 8
DK = 128
LEVELS = 7
E = 64
EG = 8
TOPK = 6
TOPG = 4
F = 256
KSTRIDE = 8
MIN_BLOCKS = T * TOPK // P
NBMAX = MIN_BLOCKS + E
NCOL = NBMAX + 2
SCALE = 2.5
ALPHA = 2.0 ** 0.25
LN_EPS = 1e-5
RMS_EPS = 1e-6
BIG = 1e30
NOWHERE = 1 << 20
C_U, C_V, C_Q, C_FF, C_FB, C_I, C_G, C_GA, C_GB = 0, 512, 1024, 2048, 3072, 4096, 5120, 6144, 7168

K_IDENT = 0
K_ONES = K_IDENT + P
K_TRI = K_ONES + P
K_IOTA = K_TRI + P
K_MASK = K_IOTA + P
K_IOTAP = K_MASK + LEVELS * P
K_DST = K_IOTAP + 1
NCONST = K_DST + NT * TOPK

FILLS = 11
USES = 8
PRE = 5 * NT
PARTS = 6 * KC
POST = PRE + 6 * H + NT
BESIDE = (0, 7, 11, 16, 22, 27, 33, 38, 44, 46, 48)
FWD_TILES = (0, 1, 2, 4)
BWD_TILES = (3, 2, 1, 5)


def constants():
    c = np.zeros((P, NCONST), np.float32)
    p = np.arange(P)
    c[:, K_IDENT:K_IDENT + P] = np.eye(P)
    c[:, K_ONES:K_ONES + P] = 1.0
    c[:, K_TRI:K_TRI + P] = p[:, None] < p[None, :]
    c[:, K_IOTA:K_IOTA + P] = p[None, :]
    for j in range(LEVELS):
        same = (p[:, None] >> (j + 1)) == (p[None, :] >> (j + 1))
        c[:, K_MASK + j * P:K_MASK + (j + 1) * P] = same & ((p[:, None] >> j) != (p[None, :] >> j))
    c[:, K_IOTAP] = p
    for i in range(NT):
        for k in range(TOPK):
            c[:, K_DST + i * TOPK + k] = (i * P + p) * KSTRIDE + k + 1
    return c


class Chain:

    def __init__(self, eng, sem):
        self.eng, self.sem, self.n = eng, sem, 0

    def link(self, ins):
        self.n += 1
        ins.then_inc(self.sem, 1)
        self.eng.wait_ge(self.sem, self.n)

    def restart(self):
        self.eng.wait_ge(self.sem, self.n)
        self.eng.sem_clear(self.sem)
        self.n = 0


def build(nc, d):
    with ExitStack() as ctx:
        def sb(name, words, dt=F32):
            return ctx.enter_context(nc.sbuf_tensor(name, [P, words], dt))

        def ps(name, words):
            return ctx.enter_context(nc.psum_tensor(name, [P, words], F32))

        def sem(name):
            return ctx.enter_context(nc.semaphore(name))

        con = sb("con", NCONST)
        rA = sb("rA", KC * T)
        rB = sb("rB", KC * T)
        rCD = sb("rCD", 2 * KC * T)
        rEF = sb("rEF", 2 * KC * T)
        aTr = sb("aTr", 4 * T)
        hw = sb("hw", 3 * KC * P)
        ew = sb("ew", 6 * D)
        rows = sb("rows", 2 * D)
        lbs = sb("lbs", 2 * H)
        lbc = sb("lbc", 2 * H)
        sbt = sb("sbt", AG)
        lbraw = sb("lbraw", P)
        blki = lbraw[:, :].bitcast(I32)
        lbw = sb("lbw", 4 * 4 * H)
        bias = sb("bias", E)
        bst = sb("bst", 12 * NT)
        mv = sb("mv", 2 * NT)
        std = sb("std", NT * H)
        rstd = sb("rstd", NT * H)
        bexp = sb("bexp", 1)
        nbi = sb("nbi", 8, I32)

        ident = con[:, K_IDENT:K_IDENT + P]
        ones = con[:, K_ONES:K_ONES + P]
        tri = con[:, K_TRI:K_TRI + P]
        iota = con[:, K_IOTA:K_IOTA + P]

        def slabs(ap, c):
            return ap.rearrange("p (c n) -> p c n", c=c)

        def at(region, offset, dims):
            ap = region[:, :]
            return bass.AP(ap.tensor, ap.offset + offset, [list(ap.ap[0])] + [list(x) for x in dims])

        x1T = slabs(rA[:, :], KC)
        mT = x1T
        v_tok = slabs(rB[:, :], NT)
        rT = slabs(rB[:, :], KC)
        x2 = slabs(rB[:, :], NT)
        x_in = slabs(rCD[:, 0:NT * D], NT)
        g_tok = slabs(rCD[:, 0:NT * D], NT)
        o_tok = slabs(rCD[:, NT * D:], NT)
        u_tok = slabs(rCD[:, NT * D:NT * D + NT * AW], NT)
        vn_tok = slabs(rCD[:, NT * D + NT * AW:], NT)
        wo_sb = slabs(rCD[:, 0:KC * D], KC)
        wsh = slabs(rCD[:, KC * D:KC * D + KC * 2 * F], KC)
        strip = [slabs(rEF[:, n * KC * 512:(n + 1) * KC * 512], KC) for n in range(2)]
        ws_sb = slabs(rEF[:, 2 * KC * 512:2 * KC * 512 + AG * P], AG)
        wsT = slabs(rEF[:, 2 * KC * 512 + AG * P:2 * KC * 512 + 2 * AG * P], AG)
        sga = slabs(rEF[:, 0:KC * T], KC)
        sgb = slabs(rEF[:, KC * T:], KC)
        x1_back = slabs(rEF[:, 0:NT * D], NT)
        acc = x1_back
        x2T = slabs(rEF[:, KC * T:], KC)
        aT = slabs(aTr[:, :], 4)
        wsh_d = slabs(aTr[:, 0:2 * D], 2)
        hw3 = [slabs(hw[:, m * KC * P:(m + 1) * KC * P], KC) for m in range(3)]
        nrow = ew[:, 3 * D:4 * D]

        g_strip = [slabs(r, KC // 2) for r in (ew[:, 4 * D:6 * D], rows[:, :])]

        q_next, sig_next = rEF[:, 0:T], rEF[:, T:3 * T]
        OFF = {"q": 3 * T, "P": 4 * T, "k": 6 * T, "S": 8 * T, "Q0": 10 * T, "Q1": 11 * T,
               "K0": 12 * T, "K1": 13 * T, "prod": 14 * T, "AT": 15 * T}
        keT = slabs(ew[:, 0:8 * P], 8)
        states = slabs(ew[:, 8 * P:16 * P], 8)

        def hv(name, n=1):
            return rEF[:, OFF[name]:OFF[name] + n * T]

        cut = {"ew": 0, "hw": 2 * D + KC * E + P}

        def scratch(n, name="ew"):
            region = {"ew": ew, "hw": hw}[name]
            cut[name] += n
            assert cut[name] <= {"ew": 6 * D, "hw": 3 * D}[name]
            return region[:, cut[name] - n:cut[name]]

        NK = NT * TOPK
        wr_sb = slabs(hw[:, 2 * D:2 * D + KC * E], KC)
        lgT = hw[:, 2 * D + KC * E:2 * D + KC * E + P]
        onehot, work = scratch(NK * E), scratch(NK * E)
        score, select, posd = (scratch(NT * E) for _ in range(3))
        biased, allowed = scratch(E), scratch(E)

        def chosen_before(i):
            return select[:, 0:E] if i == 1 else posd[:, (i - 1) * E:i * E]

        best, second, gsum, gcnt, gmask = (scratch(EG) for _ in range(5))
        gtop, gidx, gidxf, etop, eidx, eidxf = (scratch(8) for _ in range(6))
        gatew, wsum = scratch(TOPK), scratch(1)
        slot, slotl, sloth = (scratch(NK) for _ in range(3))
        gate, low, high = (scratch(NK, "hw") for _ in range(3))
        nblk, incl, base = (scratch(E, "hw") for _ in range(3))

        OH = P + 2 * NCOL
        OH_FLIGHT = KC * D // OH

        def oh_place(x):
            return rCD[:, (x % OH_FLIGHT) * OH:][:, 0:P]

        def oh_block(x):
            return rCD[:, (x % OH_FLIGHT) * OH + P:][:, 0:2 * NCOL]

        weights = (ew[:, :], rEF[:, KC * T:])
        wg, wu, wd = [[slabs(w[:, n * 2 * D:(n + 1) * 2 * D], c) for w in weights]
                      for n, c in ((0, KC), (1, KC), (2, 2))]
        work2 = (rA[:, 0:3 * D + 4 * F], rB[:, 0:3 * D + 4 * F])
        xg = [w[:, 0:D] for w in work2]
        xT = [slabs(w[:, D:2 * D], KC) for w in work2]
        yrow = [w[:, 2 * D:3 * D] for w in work2]
        silu_g = [w[:, 3 * D:3 * D + F] for w in work2]
        hT = [slabs(w[:, 3 * D + F:3 * D + 2 * F], 2) for w in work2]
        hid = rA[:, 3 * D + 2 * F:3 * D + 3 * F]
        hidT = slabs(rA[:, 3 * D + 3 * F:3 * D + 4 * F], 2)
        land = [slabs(r, TOPK) for r in (rCD[:, 0:TOPK * D], rCD[:, TOPK * D:], rB[:, :])]
        tblg = rA[:, 4 * D:4 * D + P]
        tbld = rA[:, 4 * D + P:4 * D + 2 * P]
        tbldi = rA[:, 4 * D + 2 * P:4 * D + 3 * P].bitcast(I32)
        tblti = rA[:, 4 * D + 3 * P:4 * D + 4 * P].bitcast(I32)
        tokcol, dstcol = ([rA[:, 4 * D + 4 * P + 2 * m + n:][:, 0:1].bitcast(I32) for n in range(2)]
                          for m in range(2))
        gcol = [rA[:, 4 * D + 4 * P + 4 + n:][:, 0:1] for n in range(2)]

        pg = ps("pg", 1024)
        pA = ps("pA", 1024)
        pB = ps("pB", 1024)
        pX = ps("pX", 1024)
        pair = [pA, pB]
        pairY = [pB, pX]

        def logits_at(i):
            return pX[0:E, 0:P] if i < NT - 2 else pA[0:E, (i - NT + 2) * P:(i - NT + 3) * P]

        def turned_logits_at(i):
            return pX[:, 512:512 + E] if i < NT - 2 else pA[:, 512 + (i - NT + 2) * E:512 + (i - NT + 3) * E]

        def big_bank(fill):
            return (pg, pX)[(fill // 2) % 2 if fill < 4 else 0][:, (fill % 2) * 512:(fill % 2) * 512 + 512]

        s_con = sem("constants_loaded")
        s_x = [sem(f"x_loaded{i}") for i in range(NT)]
        s_rows = sem("ln_rows_loaded")
        s_aln = sem("gmlp_ln_rows_loaded")
        s_ln1 = sem("ln1_rows_loaded")
        s_ln2 = sem("ln2_rows_loaded")
        s_misc = sem("small_params_loaded")
        dve = sem("dve_chain")
        pool = sem("pool_chain")
        var_ready = sem("variance_ready")
        std_ready = sem("std_ready")
        x1_ready = sem("x1_ready")
        x1_stored = sem("x1_stored")
        t_filled = sem("transposes_in_psum")
        t_evicted = sem("transposes_in_sbuf")
        s_strip = [sem(f"strip_loaded{n}") for n in range(2)]
        s_hw = [sem(f"column_weights_loaded{m}") for m in range(3)]
        g_filled = sem("product_in_psum")
        g_evicted = sem("product_in_sbuf")
        v_normed = sem("gmlp_v_normed")
        ws_filled = sem("ws_transposed")
        ws_evicted = sem("ws_in_sbuf")
        mix_filled = sem("mix_in_psum")
        a_ready = sem("gmlp_a_ready")
        lb_filled = sem("lb_logits_transposed")
        lb_sub = sem("lb_logits_centred")
        lb_exp = sem("lb_exp_ready")
        cur_taken = sem("gates_taken")
        diag_ready = sem("diag_ready")
        lvl_ready = sem("level_ready")
        ke_ready = sem("k_decayed_ready")
        st_ready = sem("states_ready")
        hg_filled = sem("recurrence_in_psum")
        hg_used = sem("recurrence_psum_used")
        ke_evicted = sem("k_transposed_in_sbuf")
        o_evicted = sem("o_in_sbuf")
        s_cleared = sem("suffix_products_cleared")
        s_gstrip = sem("g_strip_loaded")
        r_done = sem("r_ready")
        rt_evicted = sem("rT_in_sbuf")
        rt_filled = sem("rT_in_psum")
        s_pa = sem("w_pa_loaded")
        s_pb = sem("w_pb_loaded")
        pa_filled = sem("a_projected")
        pb_filled = sem("r_projected")
        pa_taken = sem("a_projection_taken")
        pb_taken = sem("r_projection_taken")
        m_ready = sem("mixed_ready")
        s_wo = sem("w_o_loaded")
        of_filled = sem("out_projection_in_psum")
        z_taken = sem("out_projection_taken")
        x2_ready = sem("x2_ready")
        x2_stored = sem("x2_stored")
        x2t_filled = sem("x2T_in_psum")
        x2t_evicted = sem("x2T_in_sbuf")
        s_wr = sem("router_loaded")
        s_wsh = sem("shared_expert_loaded")
        lg_filled = sem("logits_in_psum")
        lg_evicted = sem("logits_in_sbuf")
        lgt_filled = sem("logits_token_major")
        sc_ready = sem("scores_ready")
        before_ready = sem("selections_before_ready")
        sel_ready = sem("selection_ready")
        pos_filled = sem("positions_in_psum")
        oh_ready = sem("slot_onehots_ready")
        ohp_ready = sem("place_onehots_ready")
        low_ready = sem("slots_ready")
        oh_used = sem("slot_onehots_used")
        blk_ready = sem("block_expert_ready")
        blk_filled = sem("block_expert_row")
        blki_ready = sem("block_experts_ready")
        tb_ready = sem("tables_ready")
        sh_gu = sem("shared_gate_up_in_psum")
        sh_silu = sem("shared_silu_ready")
        sh_h = sem("shared_hidden_ready")
        sh_ht = sem("shared_hiddenT_in_psum")
        sh_hte = sem("shared_hiddenT_ready")
        sh_y = sem("shared_down_in_psum")
        sh_acc = sem("shared_added")
        s_wgu = [sem(f"w_gate_up_loaded{n}") for n in range(2)]
        s_wd = [sem(f"w_down_loaded{n}") for n in range(2)]
        gu_filled = sem("gate_up_in_psum")
        silu_ready = sem("silu_ready")
        h_ready = sem("hidden_ready")
        y_filled = sem("down_in_psum")
        y_ready = sem("y_ready")
        gc_ready = sem("gate_column_ready")
        xg_clear = sem("gather_buffer_cleared")
        xg_loaded = [sem(f"rows_gathered{n}") for n in range(2)]
        xt_filled = sem("gathered_T_in_psum")
        xt_ready = sem("gathered_T_ready")
        y_stored = [sem(f"y_scattered{n}") for n in range(2)]
        s_yb = [[sem(f"routed_rows_loaded{n}_{m}") for m in range(2)] for n in range(3)]
        yb_used = sem("last_routed_rows_added")
        sum_filled = sem("routed_rows_summed")
        sum_taken = sem("routed_sums_taken")
        out_ready = sem("out_ready")
        out_stored = sem("out_stored")

        block = ctx.enter_context(nc.Block())

        @block.sync
        def _(sp):
            w_in = d["w_in"].rearrange("(p c) n -> p c n", c=KC)

            sp.dma_start(x_in[:, 0, :], d["x_prompt"][0:P, :]).then_inc(s_x[0], 16)
            sp.dma_start(con[:, :], d["consts"]).then_inc(s_con, 16)
            sp.dma_start(rows[:, 0:D], d["ln_in_g"].to_broadcast([P, D])).then_inc(s_rows, 16)
            sp.dma_start(rows[:, D:], d["ln_in_b"].to_broadcast([P, D])).then_inc(s_rows, 16)

            def load_x(i):
                src = d["x_prompt"][i * P:(i + 1) * P, :] if i < NTP else \
                    d["x_sample"][(i - NTP) * P:(i - NTP + 1) * P, :]
                sp.dma_start(x_in[:, i, :], src).then_inc(s_x[i], 16)

            load_x(1)
            for n, c0 in enumerate((C_U, C_V, C_I, C_I + 512, C_G)):
                if n >= 2:
                    sp.wait_ge(g_filled, NT * (n - 1))
                sp.dma_start(strip[n % 2], w_in[:, :, c0:c0 + 512]).then_inc(s_strip[n % 2], 16)
                if n == 0:
                    for i in range(2, NT):
                        load_x(i)
                    sp.dma_start(ws_sb, d["a_ws"].rearrange("g t s -> t g s")).then_inc(s_misc, 16)
                    sp.dma_start(sbt[:, :], d["a_sb"]).then_inc(s_misc, 16)
                    sp.dma_start(nrow, d["hg_norm_g"].to_broadcast([P, D])).then_inc(s_misc, 16)
                    sp.dma_start(lbraw[0:4 * H, :], d["hg_lb_logits"].rearrange(
                        "a l (h k) -> (a l h) k", h=H)).then_inc(s_misc, 16)
            sp.wait_ge(x1_ready, NT)
            for i in range(NT):
                sp.dma_start(d["x1_dram"][i * P:(i + 1) * P, :], x_in[:, i, :]).then_inc(x1_stored, 16)
            sp.dma_start(rows[:, 0:AW], d["a_ln_g"].to_broadcast([P, AW])).then_inc(s_aln, 16)
            sp.dma_start(rows[:, AW:2 * AW], d["a_ln_b"].to_broadcast([P, AW])).then_inc(s_aln, 16)
            for m, c0 in enumerate((C_Q, C_FF, C_FB)):
                sp.dma_start(hw3[m], w_in[:, :, c0:c0 + DK]).then_inc(s_hw[m], 16)
            sp.wait_ge(v_normed, 1)
            for m in range(2):
                sp.dma_start(g_strip[m], w_in[:, 4 * m:4 * m + 4, C_G + 512:C_G + D]).then_inc(s_gstrip, 16)
            with sp.Fori(1, H) as h:
                for m, c0 in enumerate((C_Q, C_FF, C_FB)):
                    sp.wait_ge(g_filled, PRE + 2 * (m + 1) + (h - 1) * 6)
                    sp.dma_start(hw3[m], w_in[:, :, bass.ds(c0 + h * DK, DK)]).then_inc(s_hw[m], 16)
            for m, c0 in enumerate((C_GA, C_GB)):
                sp.wait_ge(g_filled, PRE + 6 * H - 4 + 2 * m)
                sp.dma_start(hw3[m], w_in[:, :, c0:c0 + P]).then_inc(s_hw[m], 16)
            with sp.Fori(1, KC) as f:
                for m, c0 in enumerate((C_GA, C_GB)):
                    sp.wait_ge(g_filled, POST + 2 * (m + 1) + (f - 1) * 4)
                    sp.dma_start(hw3[m], w_in[:, :, bass.ds(c0 + f * P, P)]).then_inc(s_hw[m], 16)
            w_pa = d["w_pa"].rearrange("(p c) n -> p c n", c=4)
            w_pb = d["w_pb"].rearrange("(p c) n -> p c n", c=KC)
            sp.wait_ge(g_filled, POST + 4 * KC)
            sp.dma_start(hw3[0][:, 0:4, :], w_pa[:, :, 0:P]).then_inc(s_pa, 16)
            sp.dma_start(hw3[1], w_pb[:, :, 0:P]).then_inc(s_pb, 16)
            with sp.Fori(1, KC) as f:
                sp.wait_ge(pa_filled, f)
                sp.dma_start(hw3[0][:, 0:4, :], w_pa[:, :, bass.ds(f * P, P)]).then_inc(s_pa, 16)
                sp.wait_ge(pb_filled, f)
                sp.dma_start(hw3[1], w_pb[:, :, bass.ds(f * P, P)]).then_inc(s_pb, 16)
            sp.wait_ge(rt_filled, NT)
            sp.dma_start(wo_sb, d["w_o"].rearrange("(c p) n -> p c n", p=P)).then_inc(s_wo, 16)
            sp.dma_start(wsh[:, :, 0:F], d["w_sh_gate"].rearrange("(p c) n -> p c n", c=KC)).then_inc(s_wsh, 16)
            sp.dma_start(wsh[:, :, F:], d["w_sh_up"].rearrange("(p c) n -> p c n", c=KC)).then_inc(s_wsh, 16)
            sp.dma_start(rows[:, 0:D], d["ln1_g"].to_broadcast([P, D])).then_inc(s_ln1, 16)
            sp.dma_start(rows[:, D:], d["ln1_b"].to_broadcast([P, D])).then_inc(s_ln1, 16)
            sp.dma_start(wr_sb, d["w_router"].rearrange("(p c) n -> p c n", c=KC)).then_inc(s_wr, 16)
            sp.dma_start(bias[:, :], d["router_bias"].to_broadcast([P, E])).then_inc(s_wr, 16)
            sp.wait_ge(pa_filled, KC)
            sp.dma_start(wsh_d, d["w_sh_down"].rearrange("(j p) n -> p j n", p=P)).then_inc(s_wsh, 16)
            sp.wait_ge(m_ready, KC)
            sp.wait_ge(x1_stored, 16 * NT)
            for i in range(NT):
                sp.dma_start(x1_back[:, i, :], d["x1_dram"][i * P:(i + 1) * P, :]).then_inc(s_x[i], 16)
            sp.dma_start(hw[:, 0:D], d["ln2_g"].to_broadcast([P, D])).then_inc(s_ln2, 16)
            sp.dma_start(hw[:, D:2 * D], d["ln2_b"].to_broadcast([P, D])).then_inc(s_ln2, 16)
            for i in range(NT):
                sp.wait_ge(x2_ready, i + 1)
                sp.dma_start(d["x2_dram"][i * P:(i + 1) * P, :], x2[:, i, :]).then_inc(x2_stored, 16)

            wg_d = d["w_e_gate"].rearrange("e (p c) n -> e p c n", c=KC)
            wu_d = d["w_e_up"].rearrange("e (p c) n -> e p c n", c=KC)
            wd_d = d["w_e_down"].rearrange("e (j p) n -> e p j n", p=P)

            def load_expert(b, n, first=False):
                e = sp.value_load(blki[0:1, bass.ds(b, 1)], min_val=0, max_val=E - 1)
                if not first:
                    sp.wait_ge(gu_filled, b - 1)
                for src, dst in ((wg_d, wg[n]), (wu_d, wu[n])):
                    sp.dma_start(dst, src[bass.ds(e, 1), :, :, :].rearrange("e p c n -> (e p) c n")).then_inc(s_wgu[n], 16)
                if not first:
                    sp.wait_ge(y_filled, b - 1)
                sp.dma_start(wd[n], wd_d[bass.ds(e, 1), :, :, :].rearrange("e p j n -> (e p) j n")).then_inc(s_wd[n], 16)

            sp.wait_ge(blki_ready, 1)
            sp.wait_ge(oh_ready, 1)
            load_expert(0, 0, True)
            sp.wait_ge(sh_gu, NT)
            load_expert(1, 1, True)
            sp.wait_ge(tb_ready, 1)
            pairs = sp.value_load(nbi[0:1, 0:1], min_val=MIN_BLOCKS // 2, max_val=NBMAX // 2)
            gathers = sp.value_load(nbi[0:1, 3:4], min_val=8 * MIN_BLOCKS, max_val=8 * NBMAX + 16)
            with sp.Fori(1, pairs) as r:
                load_expert(r * 2, 0)
                load_expert(r * 2 + 1, 1)
            sp.wait_ge(y_stored[0], pairs * 16)
            sp.wait_ge(y_stored[1], pairs * 16)
            sp.wait_ge(xg_loaded[1], gathers)
            yb = d["y_dram"].rearrange("(t k) n -> t k n", k=KSTRIDE)
            for i in range(NT):
                if i >= 3:
                    sp.wait_ge(sum_filled, i - 2)
                    sp.wait_ge(yb_used, i - 2)
                for m in range(2):
                    three = slice(3 * m, 3 * m + 3)
                    sp.dma_start(land[i % 3][:, three, :], yb[i * P:(i + 1) * P, three, :]).then_inc(s_yb[i % 3][m], 16)
            for i in range(NT):
                sp.wait_ge(out_ready, i + 1)
                dst = d["y_prompt"][i * P:(i + 1) * P, :] if i < NTP else \
                    d["y_sample"][(i - NTP) * P:(i - NTP + 1) * P, :]
                sp.dma_start(dst, acc[:, i, :]).then_inc(out_stored, 16)
            sp.wait_ge(out_stored, 16 * NT)

        @block.tensor
        def _(pe):
            mm, tr = nc.tensor.matmul, nc.tensor.transpose

            pe.wait_ge(s_con, 16)

            def x1_transposed(i):
                pe.wait_ge(x1_ready, i + 1)
                if i >= 2:
                    pe.wait_ge(t_evicted, i - 1)
                for c in range(KC):
                    last = tr(pair[i % 2][:, c * P:(c + 1) * P], x_in[:, i, c:D:KC], ident)
                last.then_inc(t_filled, 1)

            x1_transposed(0)
            for n in range(5):
                pe.wait_ge(s_strip[n % 2], 16 * (n // 2 + 1))
                for i in range(NT):
                    fill = n * NT + i
                    if n == 0:
                        if i < NT - 1:
                            x1_transposed(i + 1)
                        pe.wait_ge(t_evicted, i + 1)
                    if fill >= NT:
                        pe.wait_ge(g_evicted, fill - 1)
                    elif fill >= 4:
                        pe.wait_ge(g_evicted, fill - 3)
                    for c in range(KC):
                        last = mm(big_bank(fill), x1T[:, c, i * P:(i + 1) * P],
                                  strip[n % 2][:, c, :], start=(c == 0), stop=(c == KC - 1))
                    last.then_inc(g_filled, 1)
                if n == 1:
                    pe.wait_ge(s_misc, 64)
                    tr(pX[:, 0:4 * H], lbraw[0:4 * H, :], ident[0:4 * H, 0:4 * H]).then_inc(lb_filled, 1)
                    for g in range(AG):
                        last = tr(pA[:, g * P:(g + 1) * P], ws_sb[:, g, :], ident)
                    last.then_inc(ws_filled, 1)
            pe.wait_ge(ws_evicted, 1)
            pe.wait_ge(v_normed, 1)
            for g in range(AG):
                if g >= 2:
                    pe.wait_ge(a_ready, g - 1)
                mm(pB[:, (g % 2) * 512:(g % 2) * 512 + NT * AGD], wsT[:, g, :],
                   vn_tok[:, :, g * AGD:(g + 1) * AGD], start=True, stop=True).then_inc(mix_filled, 1)

            def head_products(nxt, first, end):
                for y in range(first, end):
                    x, c = y // KC, y % KC
                    m, n = x // 2, x % 2
                    if c == 0:
                        if n == 0:
                            pe.wait_ge(s_hw[m], nxt * 16 + 16)
                        pe.wait_ge(g_evicted, nxt * 6 + (PRE + x - 1))
                    last = mm(pg[:, n * 512:n * 512 + HALF], hw3[m][:, c, :], x1T[:, c, n * HALF:(n + 1) * HALF],
                              start=(c == 0), stop=(c == KC - 1))
                    if c == KC - 1:
                        last.then_inc(g_filled, 1)

            def g_products(first, end):
                for y in range(first, end):
                    i, c = y // KC, y % KC
                    if c == 0:
                        if i == 0:
                            pe.wait_ge(s_gstrip, 32)
                        pe.wait_ge(g_evicted, PRE + 6 * H + i - 1)
                    last = mm(pg[:, (i % 2) * 512:(i % 2) * 512 + 512], x1T[:, c, i * P:(i + 1) * P],
                              g_strip[c // 4][:, c % 4, :], start=(c == 0), stop=(c == KC - 1))
                    if c == KC - 1:
                        last.then_inc(g_filled, 1)

            head_products(0, 0, PARTS)
            pe.wait_ge(a_ready, AG)
            for i in range(NT):
                if i >= 2:
                    pe.wait_ge(t_evicted, NT + i - 1)
                for c in range(4):
                    last = tr(pair[i % 2][:, c * P:(c + 1) * P], u_tok[:, i, c:AW:4], ident)
                last.then_inc(t_filled, 1)
            pe.wait_ge(t_evicted, 2 * NT)

            def recurrence(h, products, first=False):
                def start(step):
                    if step == 0:
                        if not first:
                            pe.wait_ge(o_evicted, h)
                    elif 2 <= step < 10:
                        pe.wait_ge(hg_used, h * USES + (step - 1))
                    return pair[step % 2]

                def diag():
                    buf = start(0)
                    pe.wait_ge(diag_ready, h + 1)
                    for n in range(2):
                        last = mm(buf[:, n * 512:n * 512 + HALF], ones,
                                  hv("prod")[:, n * HALF:(n + 1) * HALF], start=True, stop=True)
                    last.then_inc(hg_filled, 1)

                def level(j):
                    buf = start(j + 1)
                    pe.wait_ge(lvl_ready, h * LEVELS + (j + 1))
                    kt = hv(f"K{j % 2}")
                    qt = hv(f"Q{j % 2}")
                    for i in range(NT):
                        o = (i // 3) * 512 + (i % 3) * P
                        last = mm(buf[:, o:o + P], kt[:, i * P:(i + 1) * P], qt[:, i * P:(i + 1) * P],
                                  start=True, stop=True)
                    last.then_inc(hg_filled, 1)

                def k_transposed():
                    buf = start(8)
                    pe.wait_ge(ke_ready, 2 * h + 1)
                    for s in range(8):
                        i = FWD_TILES[s] if s < 4 else BWD_TILES[s - 4]
                        o = (s // 4) * T + i * P
                        last = tr(buf[:, s * P:(s + 1) * P], hv("S", 2)[:, o:o + P], ident)
                    last.then_inc(hg_filled, 1)

                def increments():
                    buf = start(9)
                    pe.wait_ge(ke_evicted, h + 1)
                    for s in range(8):
                        i = FWD_TILES[s] if s < 4 else BWD_TILES[s - 4]
                        last = mm(buf[:, s * P:(s + 1) * P], keT[:, s, :], v_tok[:, i, bass.ds(h * DK, DK)],
                                  start=True, stop=True)
                    last.then_inc(hg_filled, 1)

                def outputs():
                    buf = start(10)
                    pe.wait_ge(ke_ready, 2 * h + 2)
                    pe.wait_ge(st_ready, h + 1)
                    qe = hv("k", 2)
                    for i in range(NT):
                        o = (i // 3) * 512 + (i % 3) * P
                        terms = [(hv("AT")[:, i * P:(i + 1) * P], v_tok[:, i, bass.ds(h * DK, DK)])]
                        if i not in (0, NTP):
                            s = FWD_TILES.index(i - 1)
                            terms.append((qe[:, i * P:(i + 1) * P], states[:, s, :]))
                        if i not in (NTP - 1, NT - 1):
                            s = 4 + BWD_TILES.index(i + 1)
                            terms.append((qe[:, T + i * P:T + (i + 1) * P], states[:, s, :]))
                        for n, (a, b) in enumerate(terms):
                            last = mm(buf[:, o:o + P], a, b, start=(n == 0), stop=(n == len(terms) - 1))
                    last.then_inc(hg_filled, 1)

                def beside(n):
                    products(BESIDE[n], BESIDE[n + 1])

                beside(0)
                diag()
                for j in range(LEVELS):
                    level(j)
                    beside(1 + j)
                k_transposed()
                beside(1 + LEVELS)
                increments()
                beside(2 + LEVELS)
                outputs()

            recurrence(0, lambda first, end: head_products(1, first, end), True)
            with pe.Fori(1, H - 1) as h:
                recurrence(h, lambda first, end: head_products(h + 1, first, end))
            recurrence(H - 1, g_products)

            def gate_products(f):
                for m in range(2):
                    pe.wait_ge(s_hw[m], 16 * H + 16 + f * 16)
                    for n in range(2):
                        x = 2 * m + n
                        pe.wait_ge(g_evicted, f * 4 + (POST + x - 1))
                        for c in range(KC):
                            last = mm(pg[:, n * 512:n * 512 + HALF], hw3[m][:, c, :],
                                      x1T[:, c, n * HALF:(n + 1) * HALF], start=(c == 0), stop=(c == KC - 1))
                        last.then_inc(g_filled, 1)

            with pe.Fori(0, KC) as f:
                gate_products(f)
            pe.wait_ge(o_evicted, H)
            for i in range(NT):
                pe.wait_ge(r_done, i + 1)
                if i >= 2:
                    pe.wait_ge(rt_evicted, i - 1)
                for c in range(KC):
                    last = tr(pair[i % 2][:, c * P:(c + 1) * P], o_tok[:, i, c:D:KC], ident)
                last.then_inc(rt_filled, 1)
            pe.wait_ge(rt_evicted, NT)
            def projections(f, first=False):
                pe.wait_ge(s_pa, f * 16 + 16)
                if not first:
                    pe.wait_ge(pa_taken, f)
                for n in range(2):
                    for c in range(4):
                        last = mm(pA[:, n * 512:n * 512 + HALF], hw3[0][:, c, :], aT[:, c, n * HALF:(n + 1) * HALF],
                                  start=(c == 0), stop=(c == 3))
                last.then_inc(pa_filled, 1)
                pe.wait_ge(s_pb, f * 16 + 16)
                if not first:
                    pe.wait_ge(pb_taken, f)
                for n in range(2):
                    for c in range(KC):
                        last = mm(pB[:, n * 512:n * 512 + HALF], hw3[1][:, c, :], rT[:, c, n * HALF:(n + 1) * HALF],
                                  start=(c == 0), stop=(c == KC - 1))
                last.then_inc(pb_filled, 1)

            projections(0, True)
            with pe.Fori(1, KC) as f:
                projections(f)
            pe.wait_ge(pa_taken, KC)
            pe.wait_ge(s_wo, 16)

            def x2_transposed(i):
                pe.wait_ge(x2_ready, i + 1)
                if i >= 1:
                    pe.wait_ge(x2t_evicted, i)
                for c in range(KC):
                    last = tr(pg[:, c * P:(c + 1) * P], x2[:, i, c:D:KC], ident)
                last.then_inc(x2t_filled, 1)

            def router(i):
                if i == 0:
                    pe.wait_ge(s_wr, 32)
                else:
                    pe.wait_ge(lg_evicted, i)
                if i == NT - 2:
                    pe.wait_ge(z_taken, NT - 1)
                pe.wait_ge(x2t_evicted, i + 1)
                for c in range(KC):
                    last = mm(logits_at(i), wr_sb[:, c, :], x2T[:, c, i * P:(i + 1) * P],
                              start=(c == 0), stop=(c == KC - 1))
                last.then_inc(lg_filled, 1)

            def router_turn(i):
                pe.wait_ge(lg_evicted, i + 1)
                if i >= 1:
                    pe.wait_ge(sc_ready, i)
                tr(turned_logits_at(i), lgT[0:E, :], ident[0:E, 0:E]).then_inc(lgt_filled, 1)

            pe.wait_ge(g_evicted, POST + 4 * KC)
            for i in range(NT):
                if i >= 2:
                    pe.wait_ge(z_taken, i - 1)
                for n in range(2):
                    for c in range(KC):
                        if i == 0 and n == 0:
                            pe.wait_ge(m_ready, c + 1)
                        last = mm(pair[i % 2][:, n * 512:(n + 1) * 512], mT[:, c, i * P:(i + 1) * P],
                                  wo_sb[:, c, n * 512:(n + 1) * 512], start=(c == 0), stop=(c == KC - 1))
                    if n == 0:
                        if i >= 1:
                            x2_transposed(i - 1)
                        if i >= 2:
                            router_turn(i - 2)
                last.then_inc(of_filled, 1)
                if i >= 1:
                    router(i - 1)

            def shared_up(i):
                for c in range(KC):
                    last = mm(pX[:, 0:512], x2T[:, c, i * P:(i + 1) * P], wsh[:, c, :],
                              start=(c == 0), stop=(c == KC - 1))
                last.then_inc(sh_gu, 1)

            def shared_turn(i):
                pe.wait_ge(sh_h, i + 1)
                if i >= 1:
                    pe.wait_ge(sh_hte, i)
                for j in range(2):
                    last = tr(pX[:, 512 + j * P:512 + (j + 1) * P], hid[:, j * P:(j + 1) * P], ident)
                last.then_inc(sh_ht, 1)

            def shared_down(i):
                pe.wait_ge(sh_hte, i + 1)
                if i >= 1:
                    pe.wait_ge(sh_acc, i)
                for n in range(2):
                    for j in range(2):
                        last = mm(pB[:, n * 512:(n + 1) * 512], hidT[:, j, :], wsh_d[:, j, n * 512:(n + 1) * 512],
                                  start=(j == 0), stop=(j == 1))
                last.then_inc(sh_y, 1)

            def positions(first, end):
                for i in range(first, end):
                    pe.wait_ge(sel_ready, min(i + 1, NT))
                    if i >= 2:
                        pe.wait_ge(before_ready, i - 1)
                    o = pA[:, i * E:(i + 1) * E]
                    if i < NT:
                        last = mm(o, tri, select[:, i * E:(i + 1) * E], start=True, stop=(i == 0))
                    if i >= 1:
                        last = mm(o, ones, chosen_before(i), start=(i == NT), stop=True)
                if end == NT + 1:
                    last.then_inc(pos_filled, 1)

            def slot_tables(first, end):
                for x in range(first, end):
                    pe.wait_ge(oh_ready, 2 * x + 2)
                    pe.wait_ge(ohp_ready, x + 1)
                    mm(pg[:, 0:2 * NCOL], oh_place(x), oh_block(x), start=(x == 0),
                       stop=(x == NT * TOPK - 1)).then_inc(oh_used, 1)

            pe.wait_ge(s_wsh, 48)
            shared_up(0)
            x2_transposed(NT - 1)
            router_turn(NT - 2)
            shared_turn(0)
            router(NT - 1)
            for i in range(1, NT):
                shared_up(i)
                if i == 1:
                    router_turn(NT - 1)
                if i == 2:
                    positions(4, NT + 1)
                if i == NT - 1:
                    slot_tables(0, 12)
                shared_down(i - 1)
                shared_turn(i)
                if i == 1:
                    positions(0, 4)
                if i == 3:
                    pe.wait_ge(blk_ready, 1)
                    tr(pg[0:1, 512:512 + P], bexp[:, :], ident).then_inc(blk_filled, 1)
            slot_tables(12, 24)
            shared_down(NT - 1)
            slot_tables(24, NT * TOPK)

            pe.wait_ge(tb_ready, 1)
            pairs = pe.value_load(nbi[0:1, 0:1], min_val=MIN_BLOCKS // 2, max_val=NBMAX // 2)

            def gathered_turn(n, loads):
                pe.wait_ge(xg_loaded[n], loads * 16)
                for c in range(KC):
                    last = tr(pg[:, c * P:(c + 1) * P], xg[n][:, c:D:KC], ident)
                last.then_inc(xt_filled, 1)

            def up(b, n, r):
                pe.wait_ge(xt_ready, b + 1)
                pe.wait_ge(s_wgu[n], r * 32 + 32)
                for m, w in ((0, wg[n]), (1, wu[n])):
                    for j in range(2):
                        o = n * 512 + (2 * m + j) * P
                        for c in range(KC):
                            last = mm(pA[:, o:o + P], w[:, c, j * P:(j + 1) * P], xT[n][:, c, :],
                                      start=(c == 0), stop=(c == KC - 1))
                last.then_inc(gu_filled, 1)

            def down(b, n, r, first=False):
                pe.wait_ge(h_ready, b + 1)
                pe.wait_ge(s_wd[n], r * 16 + 16)
                if not first:
                    pe.wait_ge(y_ready, b - 1)
                for m in range(2):
                    for j in range(2):
                        last = mm(pairY[n][:, m * 512:(m + 1) * 512], hT[n][:, j, :],
                                  wd[n][:, j, m * 512:(m + 1) * 512], start=(j == 0), stop=(j == 1))
                last.then_inc(y_filled, 1)

            def expert_block(b, n, r, first=False):
                up(b, n, r)
                gathered_turn(1 - n, r + 1 + n)
                down(b, n, r, first)

            gathered_turn(0, 1)
            for n in range(2):
                expert_block(n, n, 0, True)
            with pe.Fori(1, pairs) as r:
                for n in range(2):
                    expert_block(r * 2 + n, n, r)
            for i in range(NT):
                pe.wait_ge(s_yb[i % 3][0], 16 * (i // 3 + 1))
                if i == 0:
                    pe.wait_ge(y_ready, pairs * 2)
                else:
                    pe.wait_ge(sum_taken, max(i - 1, 1))
                for k in range(TOPK - 1):
                    if k == 3:
                        pe.wait_ge(s_yb[i % 3][1], 16 * (i // 3 + 1))
                    for n in range(2):
                        last = mm(pairY[i % 2][:, n * 512:(n + 1) * 512], ident,
                                  land[i % 3][:, k, n * 512:(n + 1) * 512], start=(k == 0), stop=(k == TOPK - 2))
                last.then_inc(sum_filled, 1)

        @block.scalar
        def _(sc):
            fn = nc.scalar.activation

            def root(n, times):
                sc.wait_ge(var_ready, times)
                fn(std[:, 0:n], std[:, 0:n], ACT.Sqrt).then_inc(std_ready, 1)

            def x1_turned(i):
                root(1, i + 1)
                sc.wait_ge(t_filled, i + 1)
                fn(x1T[:, :, i * P:(i + 1) * P], slabs(pair[i % 2][:, :], KC), ACT.Copy).then_inc(t_evicted, 1)

            for i in range(NT):
                x1_turned(i)
            outs = ((u_tok, 0, ACT.Gelu_apprx_tanh), (vn_tok, 0, ACT.Gelu_apprx_tanh), (v_tok, 0, ACT.Copy),
                    (v_tok, 512, ACT.Copy), (g_tok, 0, ACT.Silu))
            for n, (dst, c0, func) in enumerate(outs):
                if n == 4:
                    sc.wait_ge(x1_stored, 16 * NT)
                for i in range(NT):
                    fill = n * NT + i
                    sc.wait_ge(g_filled, fill + 1)
                    fn(dst[:, i, c0:c0 + 512], big_bank(fill), func).then_inc(g_evicted, 1)
                if n == 1:
                    sc.wait_ge(lb_sub, 1)
                    fn(lbw[:, 2 * 4 * H:3 * 4 * H], lbw[:, 4 * H:2 * 4 * H], ACT.Exp).then_inc(lb_exp, 1)
                    sc.wait_ge(ws_filled, 1)
                    fn(wsT, slabs(pA[:, :], AG), ACT.Copy).then_inc(ws_evicted, 1)
                if n == 2:
                    root(NT, NT + 1)

            def head_gates(nxt, x):
                m, n = x // 2, x % 2
                sc.wait_ge(g_filled, nxt * 6 + (PRE + x + 1))
                dst = q_next if m == 0 else sig_next[:, (m - 1) * T:m * T]
                fn(dst[:, n * HALF:(n + 1) * HALF], pg[:, n * 512:n * 512 + HALF],
                   ACT.Silu if m == 0 else ACT.Sigmoid).then_inc(g_evicted, 1)

            for x in range(6):
                head_gates(0, x)
            for i in range(NT):
                sc.wait_ge(t_filled, NT + i + 1)
                fn(aT[:, :, i * P:(i + 1) * P], slabs(pair[i % 2][:, 0:4 * P], 4), ACT.Copy).then_inc(t_evicted, 1)
            def clear_suffixes():
                rounds = 2 * T // P
                fn(slabs(hv("S", 2), rounds), bass.AP(ones.tensor, ones.offset, [
                    list(ones.ap[0]), [0, rounds], [1, P]]), ACT.Copy).then_inc(s_cleared, 1)

            def second_g(i):
                sc.wait_ge(g_filled, PRE + 6 * H + i + 1)
                fn(g_tok[:, i, 512:D], pg[:, (i % 2) * 512:(i % 2) * 512 + 512], ACT.Silu).then_inc(g_evicted, 1)

            def head(h, evict, last=False):
                sc.wait_ge(cur_taken, h + 1)
                for x in range(5):
                    evict(x)
                sc.wait_ge(hg_filled, h * FILLS + 9)
                fn(keT, slabs(pair[0][:, :], 8), ACT.Copy).then_inc(ke_evicted, 1)
                evict(5)
                if not last:
                    clear_suffixes()
                sc.wait_ge(hg_filled, h * FILLS + 11)
                fn(o_tok[:, :, bass.ds(h * DK, DK)].rearrange("p (a b) k -> p a b k", a=2),
                   at(pair[0], 0, [[512, 2], [P, 3], [1, P]]), ACT.Copy).then_inc(o_evicted, 1)

            clear_suffixes()
            with sc.Fori(0, H - 1) as h:
                head(h, lambda x: head_gates(h + 1, x))
            head(H - 1, second_g, True)

            def merge_gates(f):
                for x in range(4):
                    n = x % 2
                    sc.wait_ge(g_filled, f * 4 + (POST + x + 1))
                    dst = sga if x < 2 else sgb
                    out = dst[:, bass.ds(f, 1), n * HALF:(n + 1) * HALF].rearrange("p a n -> p (a n)")
                    fn(out, pg[:, n * 512:n * 512 + HALF], ACT.Sigmoid).then_inc(g_evicted, 1)

            merge_gates(0)
            merge_gates(1)
            root(NT * H, NT + 2)
            with sc.Fori(2, KC) as f:
                merge_gates(f)
            for i in range(NT):
                sc.wait_ge(rt_filled, i + 1)
                fn(rT[:, :, i * P:(i + 1) * P], slabs(pair[i % 2][:, :], KC), ACT.Copy).then_inc(rt_evicted, 1)

            def x2_turned(i):
                sc.wait_ge(x2t_filled, i + 1)
                fn(x2T[:, :, i * P:(i + 1) * P], slabs(pg[:, :], KC), ACT.Copy).then_inc(x2t_evicted, 1)

            def logits_out(i):
                sc.wait_ge(lg_filled, i + 1)
                if i >= 1:
                    sc.wait_ge(lgt_filled, i)
                fn(lgT[0:E, :], logits_at(i), ACT.Copy).then_inc(lg_evicted, 1)

            def scores(i):
                sc.wait_ge(lgt_filled, i + 1)
                fn(score[:, i * E:(i + 1) * E], turned_logits_at(i), ACT.Sigmoid).then_inc(sc_ready, 1)

            for i in range(NT):
                if i >= 1:
                    x2_turned(i - 1)
                if i >= 2:
                    scores(i - 2)
                if i >= 1:
                    logits_out(i - 1)
                root(1, NT + 3 + i)

            def shared_silu(i):
                sc.wait_ge(sh_gu, i + 1)
                if i >= 1:
                    sc.wait_ge(sh_h, i)
                fn(silu_g[0], pX[:, 0:F], ACT.Silu).then_inc(sh_silu, 1)

            def shared_turned(i):
                sc.wait_ge(sh_ht, i + 1)
                if i >= 1:
                    sc.wait_ge(sh_y, i)
                fn(hidT, slabs(pX[:, 512:512 + F], 2), ACT.Copy).then_inc(sh_hte, 1)

            shared_silu(0)
            x2_turned(NT - 1)
            scores(NT - 2)
            shared_turned(0)
            logits_out(NT - 1)
            for i in range(1, NT):
                shared_silu(i)
                if i == 1:
                    scores(NT - 1)
                shared_turned(i)

            sc.wait_ge(tb_ready, 1)
            pairs = sc.value_load(nbi[0:1, 0:1], min_val=MIN_BLOCKS // 2, max_val=NBMAX // 2)

            def gathered(b, n):
                sc.wait_ge(xt_filled, b + 1)
                fn(xT[n], slabs(pg[:, :], KC), ACT.Copy).then_inc(xt_ready, 1)

            def silu(b, n, first=False):
                sc.wait_ge(gu_filled, b + 1)
                if not first:
                    sc.wait_ge(h_ready, b - 1)
                fn(silu_g[n], pA[:, n * 512:n * 512 + F], ACT.Silu).then_inc(silu_ready, 1)

            def weighted(b, n, stores):
                sc.wait_ge(y_filled, b + 1)
                sc.wait_ge(gc_ready, b + 1)
                if stores is not None:
                    sc.wait_ge(y_stored[n], stores * 16)
                fn(yrow[n], pairY[n][:, :], ACT.Copy, scale=gcol[n]).then_inc(y_ready, 1)

            gathered(0, 0)
            silu(0, 0, True)
            gathered(1, 1)
            weighted(0, 0, None)
            silu(1, 1, True)
            gathered(2, 0)
            weighted(1, 1, None)
            with sc.Fori(1, pairs) as r:
                silu(r * 2, 0)
                gathered(r * 2 + 1, 1)
                weighted(r * 2, 0, r)
                silu(r * 2 + 1, 1)
                gathered(r * 2 + 2, 0)
                weighted(r * 2 + 1, 1, r)
            for i in range(NT):
                root(1, 2 * NT + 3 + i)

        @block.vector
        def _(ve):
            v = nc.vector
            chain = Chain(ve, dve)
            link = chain.link
            asked = [0]

            def rooted(n):
                asked[0] += 1
                ve.wait_ge(std_ready, asked[0])
                link(v.reciprocal(rstd[:, 0:n], std[:, 0:n]))

            def statistics(x, i, width):
                parts = width // 512
                for n in range(parts):
                    link(v.bn_stats(bst[:, 12 * i + 6 * n:12 * i + 6 * n + 6], x[:, n * 512:(n + 1) * 512]))
                link(v.bn_aggr(mv[:, 2 * i:2 * i + 2], bst[:, 12 * i:12 * i + 6 * parts]))

            def centred(x, i, gain):
                link(v.scalar_tensor_tensor(out=x, in0=x, scalar=mv[:, 2 * i:2 * i + 1], in1=gain,
                                            op0=ALU.subtract, op1=ALU.mult))

            def normalised(x, r, offset):
                return v.scalar_tensor_tensor(out=x, in0=x, scalar=rstd[:, r:r + 1], in1=offset,
                                              op0=ALU.mult, op1=ALU.add)

            def variances(n):
                v.tensor_scalar(std[:, 0:n], mv[:, 1:2 * n:2], LN_EPS, None, ALU.add).then_inc(var_ready, 1)

            for i in range(NT):
                ve.wait_ge(s_x[i], 16)
                statistics(x_in[:, i, :], i, D)
                v.tensor_scalar(std[:, 0:1], mv[:, 2 * i + 1:2 * i + 2], LN_EPS, None, ALU.add).then_inc(var_ready, 1)
                if i == 0:
                    ve.wait_ge(s_rows, 32)
                centred(x_in[:, i, :], i, rows[:, 0:D])
                rooted(1)
                normalised(x_in[:, i, :], 0, rows[:, D:]).then_inc(x1_ready, 1)
            ve.wait_ge(lb_filled, 1)
            n1 = 4 * H
            link(v.tensor_copy(lbw[:, 0:n1], pX[:, 0:n1]))

            def layer(o, l):
                return lbw[:, o:o + n1].rearrange("p (a l h) -> p a l h", a=2, l=2)[:, :, l, :]

            two = lambda ap: ap.rearrange("p (a h) -> p a h", a=2)
            link(v.tensor_tensor(two(lbs[:, :]), layer(0, 0), layer(0, 1), ALU.max))
            for l in range(2):
                last = v.tensor_tensor(layer(n1, l), layer(0, l), two(lbs[:, :]), ALU.subtract)
                if l == 0:
                    link(last)
            last.then_inc(lb_sub, 1)
            ve.wait_ge(lb_exp, 1)
            link(v.tensor_tensor(two(lbs[:, :]), layer(2 * n1, 0), layer(2 * n1, 1), ALU.add))
            link(v.reciprocal(lbc[:, :], lbs[:, :]))
            link(v.tensor_tensor(two(lbs[:, :]), layer(2 * n1, 0), two(lbc[:, :]), ALU.mult))
            link(v.tensor_scalar(lbc[:, :], lbs[:, :], -1.0, 1.0, ALU.mult, ALU.add))
            ve.wait_ge(g_evicted, 2 * NT)
            for i in range(NT):
                statistics(vn_tok[:, i, :], i, AW)
            variances(NT)
            ve.wait_ge(s_aln, 32)
            for i in range(NT):
                centred(vn_tok[:, i, :], i, rows[:, 0:AW])
            rooted(NT)
            for i in range(NT):
                last = normalised(vn_tok[:, i, :], i, rows[:, AW:2 * AW])
                if i < NT - 1:
                    link(last)
            last.then_inc(v_normed, 1)
            for g in range(AG):
                ve.wait_ge(mix_filled, g + 1)
                u_g = u_tok[:, :, g * AGD:(g + 1) * AGD]
                v.scalar_tensor_tensor(out=u_g, in0=slabs(pB[:, (g % 2) * 512:(g % 2) * 512 + NT * AGD], NT),
                                       scalar=sbt[:, g:g + 1], in1=u_g, op0=ALU.add, op1=ALU.mult).then_inc(a_ready, 1)
            def g_scaled(half):
                cols = slice(half * 512, half * 512 + 512)
                for i in range(NT):
                    link(v.tensor_tensor(g_tok[:, i, cols], g_tok[:, i, cols], nrow[:, cols], ALU.mult))

            ve.wait_ge(g_evicted, PRE)
            g_scaled(0)

            def both(name, half, fwd, bwd, n=T):
                return at(rEF, OFF[name] + fwd, [[T + bwd - fwd, 2], [2 * half, T // (2 * half)], [1, half]])

            def one(name, half, fwd, bwd):
                return at(rEF, OFF[name] + fwd, [[bwd - fwd, 2], [2 * half, T // (2 * half)], [1, half]])

            def total(half, fwd, bwd):
                return at(rEF, OFF["P"] + fwd, [[T + bwd - fwd, 2], [2 * half, T // (2 * half)], [0, half]])

            def masked_in(h, j):
                mask = con[:, K_MASK + j * P:K_MASK + (j + 1) * P].bitcast(I32)
                v.copy_predicated(at(rEF, OFF["AT"], [[HALF, 2], [P, 3], [1, P]]),
                                  bass.AP(mask.tensor, mask.offset, [list(mask.ap[0]), [0, 2], [0, 3], [1, P]]),
                                  at(pair[(j + 1) % 2], 0, [[512, 2], [P, 3], [1, P]])).then_inc(hg_used, 1)

            chain.restart()
            def gates_taken(h):
                ve.wait_ge(g_evicted, h * 6 + (PRE + 6))
                link(v.tensor_copy(hv("q"), q_next))
                for a in range(2):
                    last = v.tensor_scalar(hv("P", 2)[:, a * T:(a + 1) * T], sig_next[:, a * T:(a + 1) * T],
                                           lbc[:, bass.ds(h + a * H, 1)], lbs[:, bass.ds(h + a * H, 1)],
                                           ALU.mult, ALU.add)
                    if a == 0:
                        link(last)
                last.then_inc(cur_taken, 1)
                ve.wait_ge(cur_taken, h + 1)

            def diagonal(h, first=False):
                if not first:
                    ve.wait_ge(hg_filled, h * FILLS)
                link(v.tensor_scalar(hv("k", 2), hv("P", 2), -1.0, 1.0, ALU.mult, ALU.add))
                link(v.tensor_tensor(hv("prod"), hv("k", 2)[:, 0:T], hv("k", 2)[:, T:], ALU.add))
                v.tensor_tensor(hv("prod"), hv("prod"), hv("q"), ALU.mult).then_inc(diag_ready, 1)

            def head(h):
                for j in range(LEVELS):
                    half = 1 << j
                    link(v.tensor_tensor(one(f"Q{j % 2}", half, half, 0), one("q", half, half, 0),
                                         both("P", half, half, 0), ALU.mult))
                    if j == 0:
                        ve.wait_ge(s_cleared, h + 1)
                    v.tensor_tensor(one(f"K{j % 2}", half, 0, half), both("k", half, 0, half),
                                    both("S", half, 0, half), ALU.mult).then_inc(lvl_ready, 1)
                    link(v.tensor_tensor(both("S", half, 0, half), both("S", half, 0, half),
                                         total(half, 2 * half - 1, 0), ALU.mult))
                    if j > 0:
                        ve.wait_ge(hg_filled, h * FILLS + (j + 1))
                    link(v.tensor_tensor(both("P", half, half, 0), both("P", half, half, 0),
                                         total(half, half - 1, half), ALU.mult))
                    if j == 0:
                        ve.wait_ge(hg_filled, h * FILLS + 1)
                        eye = bass.AP(ident.tensor, ident.offset, [list(ident.ap[0]), [0, 2], [0, 3], [1, P]])
                        v.tensor_tensor(at(rEF, OFF["AT"], [[HALF, 2], [P, 3], [1, P]]),
                                        at(pair[0], 0, [[512, 2], [P, 3], [1, P]]), eye, ALU.mult).then_inc(hg_used, 1)
                        ve.wait_ge(hg_used, h * USES + 1)
                    else:
                        masked_in(h, j - 1)
                        ve.wait_ge(hg_used, h * USES + (j + 1))
                v.tensor_tensor(hv("S", 2), hv("S", 2), hv("k", 2), ALU.mult).then_inc(ke_ready, 1)
                ve.wait_ge(ke_ready, h * 2 + 1)
                v.tensor_tensor(slabs(hv("k", 2), 2), at(rEF, OFF["q"], [[0, 2], [1, T]]),
                                slabs(hv("P", 2), 2), ALU.mult).then_inc(ke_ready, 1)
                ve.wait_ge(hg_filled, h * FILLS + (LEVELS + 1))
                link(v.memset(std[:, 0:1], 0.0))
                masked_in(h, LEVELS - 1)
                ve.wait_ge(hg_filled, h * FILLS + 10)
                corners = [[4 * P, 2], [3 * P, 2], [1, P]]
                link(v.tensor_copy(at(ew, 8 * P, corners), at(pair[1], 0, corners)))
                for s in (1, 2, 5, 6):
                    i = FWD_TILES[s] if s < 4 else BWD_TILES[s - 4]
                    edge = i * P + P - 1 if s < 4 else T + i * P
                    last = v.scalar_tensor_tensor(out=states[:, s, :], in0=states[:, s - 1, :],
                                                  scalar=hv("P", 2)[:, edge:edge + 1],
                                                  in1=pair[1][:, s * P:(s + 1) * P], op0=ALU.mult, op1=ALU.add)
                    if s < 6:
                        link(last)
                last.then_inc(st_ready, 1)
                ve.wait_ge(st_ready, h + 1)

            gates_taken(0)
            diagonal(0, True)
            chain.restart()
            with ve.Fori(0, H - 1) as h:
                head(h)
                gates_taken(h + 1)
                diagonal(h + 1)
                chain.restart()
            head(H - 1)
            ve.wait_ge(g_evicted, POST)
            g_scaled(1)
            ve.wait_ge(o_evicted, H)

            square = ew[:, 2 * D:3 * D]
            for i in range(NT):
                link(v.tensor_tensor(square, o_tok[:, i, :], o_tok[:, i, :], ALU.mult))
                link(v.tensor_reduce(std[:, i * H:(i + 1) * H], slabs(square, H), AX.X, ALU.add))
            v.tensor_scalar(std[:, 0:NT * H], std[:, 0:NT * H], 1.0 / DK, RMS_EPS, ALU.mult, ALU.add).then_inc(var_ready, 1)
            rooted(NT * H)
            for i in range(NT):
                link(v.tensor_tensor(slabs(o_tok[:, i, :], H), slabs(o_tok[:, i, :], H),
                                     at(rstd, i * H, [[1, H], [0, DK]]), ALU.mult))
                v.tensor_tensor(o_tok[:, i, :], o_tok[:, i, :], g_tok[:, i, :], ALU.mult).then_inc(r_done, 1)
            ve.wait_ge(g_evicted, POST + 4 * KC)
            chain.restart()
            with ve.Fori(0, KC) as f:
                ve.wait_ge(pa_filled, f + 1)
                gate_a = sga[:, bass.ds(f, 1), :].rearrange("p a (n t) -> p (a n) t", n=2)
                gate_b = sgb[:, bass.ds(f, 1), :].rearrange("p a (n t) -> p (a n) t", n=2)
                v.tensor_tensor(slabs(ew[:, 0:T], 2), slabs(pA[:, :], 2)[:, :, 0:HALF], gate_a,
                                ALU.mult).then_inc(pa_taken, 1)
                ve.wait_ge(pb_filled, f + 1)
                v.tensor_tensor(slabs(ew[:, T:2 * T], 2), slabs(pB[:, :], 2)[:, :, 0:HALF], gate_b,
                                ALU.mult).then_inc(pb_taken, 1)
                ve.wait_ge(pa_taken, f + 1)
                ve.wait_ge(pb_taken, f + 1)
                v.tensor_tensor(mT[:, bass.ds(f, 1), :].rearrange("p a t -> p (a t)"), ew[:, 0:T], ew[:, T:2 * T],
                                ALU.add).then_inc(m_ready, 1)
                ve.wait_ge(m_ready, f + 1)
            def x2_tile(i):
                ve.wait_ge(of_filled, i + 1)
                ve.wait_ge(s_x[i], 32)
                v.scalar_tensor_tensor(out=x2[:, i, :], in0=x1_back[:, i, :], scalar=ALPHA, in1=pair[i % 2][:, :],
                                       op0=ALU.mult, op1=ALU.add).then_inc(z_taken, 1)
                ve.wait_ge(z_taken, i + 1)
                statistics(x2[:, i, :], 0, D)
                variances(1)
                centred(x2[:, i, :], 0, rows[:, 0:D])
                rooted(1)
                normalised(x2[:, i, :], 0, rows[:, D:]).then_inc(x2_ready, 1)

            def shared_hidden(i):
                ve.wait_ge(sh_silu, i + 1)
                if i >= 1:
                    ve.wait_ge(sh_ht, i)
                v.tensor_tensor(hid, silu_g[0], pX[:, F:2 * F], ALU.mult).then_inc(sh_h, 1)

            def shared_added(i):
                ve.wait_ge(sh_y, i + 1)
                v.scalar_tensor_tensor(out=acc[:, i, :], in0=x2[:, i, :], scalar=ALPHA, in1=pB[:, :],
                                       op0=ALU.mult, op1=ALU.add).then_inc(sh_acc, 1)

            def v3(ap, b, c):
                return ap.rearrange("p (a b c) -> p a b c", b=b, c=c)

            def per(region_view, dims):
                return bass.AP(region_view.tensor, region_view.offset, [list(region_view.ap[0])] + dims)

            def group_scores(i):
                ve.wait_ge(sc_ready, i + 1)
                link(v.tensor_tensor(biased, score[:, i * E:(i + 1) * E], bias[:, :], ALU.add))
                link(v.tensor_reduce(best, slabs(biased, EG), AX.X, ALU.max))
                link(v.tensor_tensor(slabs(allowed, EG), slabs(biased, EG), per(best, [[1, EG], [0, E // EG]]), ALU.is_equal))
                link(v.tensor_reduce(gcnt, slabs(allowed, EG), AX.X, ALU.add))
                link(v.scalar_tensor_tensor(out=allowed, in0=allowed, scalar=-BIG, in1=biased, op0=ALU.mult, op1=ALU.add))
                link(v.tensor_reduce(second, slabs(allowed, EG), AX.X, ALU.max))
                link(v.tensor_scalar(gcnt, gcnt, 2.0, 1.0, ALU.is_ge, ALU.subtract))
                link(v.scalar_tensor_tensor(out=gcnt, in0=gcnt, scalar=BIG, in1=best, op0=ALU.mult, op1=ALU.add))
                link(v.tensor_tensor(second, second, gcnt, ALU.max))
                link(v.tensor_tensor(gsum, best, second, ALU.add))

            def group_choice():
                link(v.max(out=gtop, in_=gsum))
                link(v.max_index(out=gidx.bitcast(U32), in_max=gtop, in_values=gsum))
                link(v.tensor_copy(gidxf, gidx.bitcast(U32)))
                link(v.tensor_tensor(slabs(work[:, 0:EG * TOPG], EG), per(iota, [[1, EG], [0, TOPG]]),
                                     per(gidxf, [[0, EG], [1, TOPG]]), ALU.is_equal))
                link(v.tensor_reduce(gmask, slabs(work[:, 0:EG * TOPG], EG), AX.X, ALU.add))
                link(v.tensor_scalar(gmask, gmask, 1.0, BIG, ALU.subtract, ALU.mult))
                link(v.tensor_tensor(slabs(allowed, EG), slabs(biased, EG), per(gmask, [[1, EG], [0, E // EG]]), ALU.add))

            def expert_choice(i):
                mine = onehot[:, i * TOPK * E:(i + 1) * TOPK * E]
                link(v.max(out=etop, in_=allowed))
                link(v.max_index(out=eidx.bitcast(U32), in_max=etop, in_values=allowed))
                link(v.tensor_copy(eidxf, eidx.bitcast(U32)))
                link(v.tensor_tensor(slabs(mine, TOPK), per(iota, [[0, TOPK], [1, E]]),
                                     per(eidxf, [[1, TOPK], [0, E]]), ALU.is_equal))
                v.tensor_reduce(select[:, i * E:(i + 1) * E], per(mine, [[1, E], [E, TOPK]]), AX.X,
                                ALU.add).then_inc(sel_ready, 1)
                if i >= 1:
                    ve.wait_ge(sel_ready, i + 1)
                    v.tensor_tensor(chosen_before(i + 1), chosen_before(i), select[:, i * E:(i + 1) * E],
                                    ALU.add).then_inc(before_ready, 1)
                    ve.wait_ge(before_ready, i)

            def expert_gates(i):
                mine, chosen = (r[:, i * TOPK * E:(i + 1) * TOPK * E] for r in (onehot, work))
                link(v.tensor_tensor(slabs(chosen, TOPK), slabs(mine, TOPK),
                                     per(score[:, i * E:(i + 1) * E], [[0, TOPK], [1, E]]), ALU.mult))
                link(v.tensor_reduce(gatew, slabs(chosen, TOPK), AX.X, ALU.add))
                link(v.tensor_reduce(wsum, gatew, AX.X, ALU.add))
                link(v.reciprocal(wsum, wsum))
                link(v.tensor_scalar(gate[:, i * TOPK:(i + 1) * TOPK], gatew, SCALE, wsum, ALU.mult, ALU.mult))

            def routed(i):
                group_scores(i)
                group_choice()
                expert_choice(i)
                expert_gates(i)

            def slots():
                ve.wait_ge(pos_filled, 1)
                cnt = pA[:, NT * E:(NT + 1) * E]
                link(v.tensor_scalar(nblk, cnt, 0.0, None, ALU.is_gt))
                for b in range(1, NT):
                    link(v.scalar_tensor_tensor(out=nblk, in0=cnt, scalar=float(P * b), in1=nblk, op0=ALU.is_gt, op1=ALU.add))
                link(v.tensor_tensor_scan(incl, ones[:, 0:E], nblk, 0.0, ALU.mult, ALU.add))
                link(v.tensor_tensor(base, incl, nblk, ALU.subtract))
                link(v.scalar_tensor_tensor(out=slabs(posd, NT), in0=per(base, [[0, NT], [1, E]]), scalar=float(P),
                                            in1=slabs(pA[:, 0:NT * E], NT), op0=ALU.mult, op1=ALU.add))
                link(v.tensor_scalar(work[:, 0:E], incl, con[:, K_IOTAP:K_IOTAP + 1], None, ALU.is_le))
                link(v.tensor_reduce(bexp[:, :], work[:, 0:E], AX.X, ALU.add))
                v.tensor_scalar(bexp[:, :], bexp[:, :], float(E - 1), None, ALU.min).then_inc(blk_ready, 1)
                link(v.tensor_scalar(nbi[0:1, 2:3], incl[0:1, E - 1:E], 1.0, None, ALU.add))
                link(v.tensor_scalar(nbi[0:1, 0:1], nbi[0:1, 2:3], 1, None, ALU.logical_shift_right))
                link(v.tensor_scalar(nbi[0:1, 1:2], nbi[0:1, 0:1], 2.0, -1.0, ALU.mult, ALU.add))
                link(v.tensor_scalar(nbi[0:1, 3:4], nbi[0:1, 0:1], 16.0, 16.0, ALU.mult, ALU.add))
                link(v.tensor_tensor(v3(work, TOPK, E), v3(onehot, TOPK, E),
                                     per(posd, [[E, NT], [0, TOPK], [1, E]]), ALU.mult))
                link(v.tensor_reduce(slot, slabs(work, NK), AX.X, ALU.add))
                link(v.tensor_copy(slotl.bitcast(I32), slot))
                link(v.tensor_scalar(sloth.bitcast(I32), slotl.bitcast(I32), 7, None, ALU.logical_shift_right))
                link(v.tensor_scalar(slotl.bitcast(I32), slotl.bitcast(I32), P - 1, None, ALU.bitwise_and))
                v.tensor_copy(low, slotl.bitcast(I32)).then_inc(low_ready, 1)
                link(v.tensor_copy(high, sloth.bitcast(I32)))

            def slot_onehots(x):
                if x >= OH_FLIGHT:
                    ve.wait_ge(oh_used, x - OH_FLIGHT + 1)
                blocks = iota[:, 0:NCOL]
                v.tensor_scalar(oh_block(x)[:, 0:NCOL], blocks, high[:, x:x + 1],
                                con[:, K_DST + x:K_DST + x + 1], ALU.is_equal, ALU.mult).then_inc(oh_ready, 1)
                v.tensor_scalar(oh_block(x)[:, NCOL:], blocks, high[:, x:x + 1], gate[:, x:x + 1],
                                ALU.is_equal, ALU.mult).then_inc(oh_ready, 1)

            ve.wait_ge(s_ln1, 32)
            ve.wait_ge(s_wr, 32)
            for i in range(NT):
                x2_tile(i)
                if 2 <= i < NT - 1:
                    routed(i - 2)
            shared_hidden(0)
            routed(NT - 3)
            group_scores(NT - 2)
            group_choice()
            shared_hidden(1)
            shared_added(0)
            expert_choice(NT - 2)
            expert_gates(NT - 2)
            group_scores(NT - 1)
            group_choice()
            expert_choice(NT - 1)
            shared_hidden(2)
            expert_gates(NT - 1)
            shared_added(1)
            slots()
            shared_hidden(3)
            shared_added(2)
            ve.wait_ge(blk_filled, 1)
            v.tensor_copy(blki[0:1, 0:P], pg[0:1, 512:512 + P]).then_inc(blki_ready, 1)
            for x in range(NK):
                if x == 10:
                    shared_hidden(4)
                if x == 18:
                    shared_added(3)
                if x == 30:
                    shared_hidden(5)
                slot_onehots(x)
            shared_added(4)
            shared_added(5)
            ve.wait_ge(oh_used, NK)
            link(v.tensor_copy(tblg[:, 0:NCOL], pg[:, NCOL:2 * NCOL]))
            link(v.tensor_scalar(tbld[:, 0:NCOL], pg[:, 0:NCOL], 0.5, float(NOWHERE), ALU.is_lt, ALU.mult))
            link(v.scalar_tensor_tensor(out=tbld[:, 0:NCOL], in0=pg[:, 0:NCOL], scalar=-1.0, in1=tbld[:, 0:NCOL],
                                        op0=ALU.add, op1=ALU.add))
            link(v.tensor_copy(tbldi[:, 0:NCOL], tbld[:, 0:NCOL]))
            v.tensor_scalar(tblti[:, 0:NCOL], tbldi[:, 0:NCOL], 3, None, ALU.logical_shift_right).then_inc(tb_ready, 1)

            ve.wait_ge(tb_ready, 1)
            pairs = ve.value_load(nbi[0:1, 0:1], min_val=MIN_BLOCKS // 2, max_val=NBMAX // 2)

            def hidden(b, n, first=False):
                ve.wait_ge(silu_ready, b + 1)
                if not first:
                    ve.wait_ge(y_filled, b - 1)
                v.tensor_tensor(hT[n], slabs(silu_g[n], 2), slabs(pA[:, n * 512 + F:n * 512 + 2 * F], 2),
                                ALU.mult).then_inc(h_ready, 1)

            def gate_column(b, n, first=False):
                if not first:
                    ve.wait_ge(y_ready, b - 1)
                v.tensor_copy(gcol[n], tblg[:, bass.ds(b, 1)]).then_inc(gc_ready, 1)

            for n in range(2):
                hidden(n, n, True)
                gate_column(n, n, True)
            with ve.Fori(1, pairs) as r:
                for n in range(2):
                    hidden(r * 2 + n, n)
                    gate_column(r * 2 + n, n)
            ve.wait_ge(s_ln2, 32)
            for i in range(NT):
                ve.wait_ge(s_yb[i % 3][1], 16 * (i // 3 + 1))
                v.tensor_tensor(acc[:, i, :], acc[:, i, :], land[i % 3][:, TOPK - 1, :], ALU.add).then_inc(yb_used, 1)
                ve.wait_ge(yb_used, i + 1)
                ve.wait_ge(sum_filled, i + 1)
                v.tensor_tensor(acc[:, i, :], acc[:, i, :], pairY[i % 2][:, :], ALU.add).then_inc(sum_taken, 1)
                ve.wait_ge(sum_taken, i + 1)
                statistics(acc[:, i, :], 0, D)
                variances(1)
                centred(acc[:, i, :], 0, hw[:, 0:D])
                rooted(1)
                normalised(acc[:, i, :], 0, hw[:, D:2 * D]).then_inc(out_ready, 1)

        @block.gpsimd
        def _(po):
            g = nc.gpsimd

            po.wait_ge(of_filled, NT)
            g.memset(xg[0], 0.0).then_inc(xg_clear, 1)
            po.wait_ge(x2_stored, 16 * NT)
            po.wait_ge(low_ready, 1)
            for x in range(NT * TOPK):
                if x >= OH_FLIGHT:
                    po.wait_ge(oh_used, x - OH_FLIGHT + 1)
                g.tensor_scalar(oh_place(x), iota, low[:, x:x + 1], None, ALU.is_equal).then_inc(ohp_ready, 1)
            po.wait_ge(sh_acc, NT)
            g.memset(xg[1], 0.0).then_inc(xg_clear, 1)
            po.wait_ge(xg_clear, 2)
            po.wait_ge(tb_ready, 1)
            pairs = po.value_load(nbi[0:1, 0:1], min_val=MIN_BLOCKS // 2, max_val=NBMAX // 2)
            last_block = po.value_load(nbi[0:1, 1:2], min_val=MIN_BLOCKS - 1, max_val=NBMAX - 1)

            def gather(b, n, chain, first=False):
                if not first:
                    po.wait_ge(xt_filled, b - 1)
                chain.link(g.tensor_copy(tokcol[n], tblti[:, bass.ds(b, 1)]))
                g.indirect_dma_start(xg[n], None, d["x2_dram"], bass.IndirectOffsetOnAxis(tokcol[n], 0),
                                     bounds_check=T - 1, oob_is_err=False).then_inc(xg_loaded[n], 16)

            def scatter(b, n, chain):
                po.wait_ge(y_ready, b + 1)
                chain.link(g.tensor_copy(dstcol[n], tbldi[:, bass.ds(b, 1)]))
                g.indirect_dma_start(d["y_dram"], bass.IndirectOffsetOnAxis(dstcol[n], 0), yrow[n], None,
                                     bounds_check=T * KSTRIDE - 1, oob_is_err=False).then_inc(y_stored[n], 16)

            chain = Chain(po, pool)
            gather(0, 0, chain, True)
            gather(1, 1, chain, True)
            gather(2, 0, chain)
            gather(3, 1, chain)
            scatter(0, 0, chain)
            chain.restart()
            with po.Fori(1, pairs) as r:
                gather(r * 2 + 2, 0, chain)
                scatter(r * 2 - 1, 1, chain)
                gather(r * 2 + 3, 1, chain)
                scatter(r * 2, 0, chain)
                chain.restart()
            scatter(last_block, 1, chain)
            for n in range(2):
                po.wait_ge(xg_loaded[n], pairs * 16 + 16)


_INS = ("x_prompt", "x_sample", "ln_in_g", "ln_in_b", "w_in", "a_ln_g", "a_ln_b", "a_ws", "a_sb",
        "hg_lb_logits", "hg_norm_g", "w_pa", "w_pb", "w_o", "ln1_g", "ln1_b", "w_router", "router_bias",
        "w_e_gate", "w_e_up", "w_e_down", "w_sh_gate", "w_sh_up", "w_sh_down", "ln2_g", "ln2_b")
_ROWS = {"ln_in_g", "ln_in_b", "a_ln_g", "a_ln_b", "hg_norm_g", "ln1_g", "ln1_b", "router_bias", "ln2_g", "ln2_b"}


def kernel(**inputs):
    import concourse.bacc as bacc
    from concourse.bass_utils import run_bass_kernel_spmd

    nc = bacc.Bacc("TRN2", target_bir_lowering=False, num_devices=1)
    arrays, d = {}, {}
    for name in _INS:
        a = np.ascontiguousarray(inputs[name])
        if name in _ROWS:
            a = a.reshape(1, -1)
        elif name != "hg_lb_logits":
            a = a.reshape(a.shape[1:])
        arrays[name] = a
    arrays["consts"] = constants()
    for name, a in arrays.items():
        d[name] = nc.dram_tensor(name, a.shape, mybir.dt.from_np(a.dtype), kind="ExternalInput").ap()
    d["y_prompt"] = nc.dram_tensor("y_prompt", (SEQ, D), F32, kind="ExternalOutput").ap()
    d["y_sample"] = nc.dram_tensor("y_sample", (DEC_SEQ, D), F32, kind="ExternalOutput").ap()
    d["x1_dram"] = nc.dram_tensor("x1_dram", (T, D), F32).ap()
    d["x2_dram"] = nc.dram_tensor("x2_dram", (T, D), F32).ap()
    d["y_dram"] = nc.dram_tensor("y_dram", (T * KSTRIDE, D), F32).ap()
    build(nc, d)
    r = run_bass_kernel_spmd(nc, [arrays], core_ids=[0]).results[0]
    return r["y_prompt"].reshape(1, SEQ, D), r["y_sample"].reshape(1, DEC_SEQ, D)
```
